# Optimizing a Trainium2 kernel written in Bass

```python
import math
import jax, jax.numpy as jnp
from jax import lax
import numpy as np
import math, functools

D_MODEL = 2048
BATCH = 1
SEQ = 256
DEPTH = 2

N_A = DEPTH // 2
N_B = DEPTH - N_A
A_QK_DIM = 128
A_V_DIM = 2 * A_QK_DIM
A_HEADS = D_MODEL // A_V_DIM
A_WIDTH = A_HEADS * A_V_DIM
B_HEAD_DIM = 128
B_HEADS = D_MODEL // B_HEAD_DIM
B_WIDTH = B_HEADS * B_HEAD_DIM
BLOCK = 128
NEG = -1e30
EPS = 1e-5
DN_ALPHA = (2.0 * DEPTH) ** 0.25
DN_BETA = (8.0 * DEPTH) ** -0.25


def layer_norm(x, g, b):
    xf = x.astype(jnp.float32)
    mu = jnp.mean(xf, axis=-1, keepdims=True)
    var = jnp.mean(jnp.square(xf - mu), axis=-1, keepdims=True)
    y = (xf - mu) * lax.rsqrt(var + EPS)
    return (y * g.astype(jnp.float32) + b.astype(jnp.float32)).astype(x.dtype)

def rms_norm(x, g):
    xf = x.astype(jnp.float32)
    y = xf * lax.rsqrt(jnp.mean(jnp.square(xf), axis=-1, keepdims=True) + EPS)
    return (y * g.astype(jnp.float32)).astype(x.dtype)

def to_blocks(a):
    b, s = a.shape[:2]
    a = a.reshape((b, s // BLOCK, BLOCK) + a.shape[2:])
    return jnp.moveaxis(a, 1, 0)

def from_blocks(a):
    a = jnp.moveaxis(a, 0, 1)
    return a.reshape((a.shape[0], a.shape[1] * a.shape[2]) + a.shape[3:])

def alibi_slopes(n_heads):
    return jnp.asarray([2.0 ** (-8.0 * (h + 1) / n_heads) for h in range(n_heads)], dtype=jnp.float32)

def diff_attention(h, w_in, w_out, lq1, lk1, lq2, lk2, subln_g, layer_idx):
    B, S, _ = h.shape
    proj = h @ w_in
    q, k, v, g = jnp.split(proj, 4, axis=-1)
    q = q.reshape(B, S, A_HEADS, 2, A_QK_DIM) * (A_QK_DIM ** -0.5)
    k = k.reshape(B, S, A_HEADS, 2, A_QK_DIM)
    v = v.reshape(B, S, A_HEADS, A_V_DIM)
    lam_init = 0.8 - 0.6 * math.exp(-0.3 * layer_idx)
    f32 = jnp.float32
    lam = (jnp.exp(jnp.sum(lq1.astype(f32) * lk1.astype(f32)))
           - jnp.exp(jnp.sum(lq2.astype(f32) * lk2.astype(f32))) + lam_init)
    slopes = alibi_slopes(A_HEADS)
    s_pos = jnp.arange(S)

    def block(args):
        qb, i = args
        t_pos = i * BLOCK + jnp.arange(BLOCK)
        dist = (t_pos[:, None] - s_pos[None, :]).astype(f32)
        bias = -slopes[:, None, None] * dist
        sc = jnp.einsum('bqhcd,bkhcd->bhcqk', qb, k).astype(f32) + bias[None, :, None]
        sc = jnp.where(dist >= 0, sc, NEG)
        p = jax.nn.softmax(sc, axis=-1)
        a = p[:, :, 0] - lam * p[:, :, 1]
        return jnp.einsum('bhqk,bkhe->bqhe', a.astype(v.dtype), v)

    o = from_blocks(lax.map(block, (to_blocks(q), jnp.arange(S // BLOCK))))
    o = rms_norm(o, subln_g) * (1.0 - lam_init)
    o = o.reshape(B, S, A_WIDTH) * jax.nn.silu(g)
    return o @ w_out

def shared_kv(x, c_act, w_mod_kv, b_mod_kv, w_kv, b_f):
    B, S, _ = x.shape
    mod = c_act @ w_mod_kv + b_mod_kv
    shift, scale = jnp.split(mod, 2, axis=-1)
    hk = x * (1.0 + scale[:, None]) + shift[:, None]
    kvf = hk @ w_kv
    k, v, zf = jnp.split(kvf, [B_WIDTH, 2 * B_WIDTH], axis=-1)
    k = k.reshape(B, S, B_HEADS, B_HEAD_DIM)
    v = v.reshape(B, S, B_HEADS, B_HEAD_DIM)
    log_f = jax.nn.log_sigmoid(zf.astype(jnp.float32) + b_f.astype(jnp.float32))
    F = jnp.cumsum(log_f, axis=1)
    return k, v, F

def forgetting_attention(h, w_q, w_out, k, v, F):
    B, S, _ = h.shape
    f32 = jnp.float32
    proj = h @ w_q
    q, g = jnp.split(proj, 2, axis=-1)
    q = q.reshape(B, S, B_HEADS, B_HEAD_DIM) * (B_HEAD_DIM ** -0.5)
    Fk = jnp.moveaxis(F, 1, 2)
    s_pos = jnp.arange(S)

    def block(args):
        qb, Fq, i = args
        t_pos = i * BLOCK + jnp.arange(BLOCK)
        causal = t_pos[:, None] >= s_pos[None, :]
        decay = jnp.moveaxis(Fq, 1, 2)[..., None] - Fk[:, :, None, :]
        sc = jnp.einsum('bqhd,bkhd->bhqk', qb, k).astype(f32) + decay
        sc = jnp.where(causal, sc, NEG)
        p = jax.nn.softmax(sc, axis=-1)
        return jnp.einsum('bhqk,bkhd->bqhd', p.astype(v.dtype), v)

    o = from_blocks(lax.map(block, (to_blocks(q), to_blocks(F), jnp.arange(S // BLOCK))))
    o = o.reshape(B, S, B_WIDTH) * jax.nn.silu(g)
    return o @ w_out

def first_inputs(seed: int = 0) -> dict:
    key = jax.random.key(seed)
    ks = jax.random.split(key, 20)
    nrm = jax.random.normal
    D = D_MODEL
    x = nrm(ks[0], (BATCH, SEQ, D), jnp.float32)
    c = nrm(ks[1], (BATCH, D), jnp.float32)
    w_mod = nrm(ks[2], (DEPTH, D, 3 * D), jnp.float32) * D ** -0.5
    b_mod = nrm(ks[3], (DEPTH, 3 * D), jnp.float32) * 0.02
    ln_g = 1.0 + 0.02 * nrm(ks[4], (DEPTH, D), jnp.float32)
    ln_b = 0.02 * nrm(ks[5], (DEPTH, D), jnp.float32)
    a_w_in = nrm(ks[6], (N_A, D, 4 * A_WIDTH), jnp.float32) * D ** -0.5
    a_w_out = nrm(ks[7], (N_A, A_WIDTH, D), jnp.float32) * (A_WIDTH ** -0.5 * DN_BETA)
    a_lam_q1 = 0.1 * nrm(ks[8], (N_A, A_QK_DIM), jnp.float32)
    a_lam_k1 = 0.1 * nrm(ks[9], (N_A, A_QK_DIM), jnp.float32)
    a_lam_q2 = 0.1 * nrm(ks[10], (N_A, A_QK_DIM), jnp.float32)
    a_lam_k2 = 0.1 * nrm(ks[11], (N_A, A_QK_DIM), jnp.float32)
    a_subln_g = 1.0 + 0.02 * nrm(ks[12], (N_A, A_V_DIM), jnp.float32)
    kv_w_mod = nrm(ks[13], (D, 2 * D), jnp.float32) * D ** -0.5
    kv_b_mod = nrm(ks[14], (2 * D,), jnp.float32) * 0.02
    kv_w = nrm(ks[15], (D, 2 * B_WIDTH + B_HEADS), jnp.float32) * D ** -0.5
    kv_b_f = jax.random.uniform(ks[16], (B_HEADS,), jnp.float32, minval=1.0, maxval=6.0)
    b_w_in = nrm(ks[17], (N_B, D, 2 * B_WIDTH), jnp.float32) * D ** -0.5
    b_w_out = nrm(ks[18], (N_B, B_WIDTH, D), jnp.float32) * (B_WIDTH ** -0.5 * DN_BETA)
    return {"x": x, "c": c, "w_mod": w_mod, "b_mod": b_mod, "ln_g": ln_g, "ln_b": ln_b,
            "a_w_in": a_w_in, "a_w_out": a_w_out, "a_lam_q1": a_lam_q1, "a_lam_k1": a_lam_k1,
            "a_lam_q2": a_lam_q2, "a_lam_k2": a_lam_k2, "a_subln_g": a_subln_g,
            "kv_w_mod": kv_w_mod, "kv_b_mod": kv_b_mod, "kv_w": kv_w, "kv_b_f": kv_b_f,
            "b_w_in": b_w_in, "b_w_out": b_w_out}

def first_block(x, c, w_mod, b_mod, ln_g, ln_b, a_w_in, a_w_out, a_lam_q1, a_lam_k1,
              a_lam_q2, a_lam_k2, a_subln_g, kv_w_mod, kv_b_mod, kv_w, kv_b_f,
              b_w_in, b_w_out):
    c_act = jax.nn.silu(c)
    kv = None
    for l in range(DEPTH):
        mod = c_act @ w_mod[l] + b_mod[l]
        shift, scale, gate = jnp.split(mod, 3, axis=-1)
        h = x * (1.0 + scale[:, None]) + shift[:, None]
        if l < N_A:
            y = diff_attention(h, a_w_in[l], a_w_out[l], a_lam_q1[l], a_lam_k1[l],
                               a_lam_q2[l], a_lam_k2[l], a_subln_g[l], l)
        else:
            if kv is None:
                kv = shared_kv(x, c_act, kv_w_mod, kv_b_mod, kv_w, kv_b_f)
            k_sh, v_sh, F_sh = kv
            y = forgetting_attention(h, b_w_in[l - N_A], b_w_out[l - N_A], k_sh, v_sh, F_sh)
        x = layer_norm(DN_ALPHA * x + gate[:, None] * y, ln_g[l], ln_b[l])
    return x


DEPTH_2 = 1

GRID_W = 64
CTX_LEN = 256
N_MIXERS = 2
S5_GROUP = 16
S5_GROUPS = D_MODEL // S5_GROUP
S5_STATE = 64
S5_DT_MIN = 0.001
S5_DT_MAX = 0.1
HG_HEADS = 16
HG_DK = D_MODEL // HG_HEADS
HG_DV = D_MODEL // HG_HEADS
HG_CHUNK = 32
MLP_HIDDEN = 4 * D_MODEL
NORM_EPS = 1e-6


def rmsnorm(x, g):
    xf = x.astype(jnp.float32)
    y = xf * lax.rsqrt(jnp.mean(xf * xf, axis=-1, keepdims=True) + NORM_EPS)
    return (y * g.astype(jnp.float32)).astype(x.dtype)

def adaln(cond, w, b):
    return jnp.split(jax.nn.silu(cond) @ w + b, 6, axis=-1)

def modulate(h, shift, scale):
    return h * (1 + scale) + shift

def raster_to_colmajor(h):
    b, n, d = h.shape
    rows = n // GRID_W
    return h.reshape(b, rows, GRID_W, d).transpose(0, 2, 1, 3).reshape(b, n, d)

def colmajor_to_raster(h):
    b, n, d = h.shape
    rows = n // GRID_W
    return h.reshape(b, GRID_W, rows, d).transpose(0, 2, 1, 3).reshape(b, n, d)

def sq_relu_mlp(h, w1, w2):
    return jnp.square(jax.nn.relu(h @ w1)) @ w2

def s5_discretise(a_re, a_im, log_dt, b_re, b_im):
    lam = lax.complex(a_re.astype(jnp.float32), a_im.astype(jnp.float32))
    dt = jnp.exp(log_dt.astype(jnp.float32))[:, None]
    lam_bar = jnp.exp(lam * dt)
    b = lax.complex(b_re.astype(jnp.float32), b_im.astype(jnp.float32))
    b_bar = ((lam_bar - 1) / lam)[..., None] * b
    return lam_bar, b_bar

def _lin_rec_combine(e1, e2):
    a1, b1 = e1
    a2, b2 = e2
    return a1 * a2, a2 * b1 + b2

def s5_scan(u, lam_bar, b_bar, s0, reverse):
    bu = jnp.einsum('btgh,gph->btgp', u, b_bar)
    first = -1 if reverse else 0
    bu = bu.at[:, first].add(lam_bar * s0)
    a = jnp.broadcast_to(lam_bar, bu.shape)
    _, states = lax.associative_scan(_lin_rec_combine, (a, bu), axis=1, reverse=reverse)
    return states

def s5_mixer(h_ctx, h_lat, a_re, a_im, log_dt, b_re, b_im, c_re, c_im, d_skip, w_glu, ctx_out):
    def to_groups(h):
        return h.astype(jnp.float32).reshape(h.shape[0], h.shape[1], S5_GROUPS, S5_GROUP)

    u_ctx, u_lat = to_groups(h_ctx), to_groups(h_lat)
    uc_ctx, uc_lat = u_ctx.astype(jnp.complex64), u_lat.astype(jnp.complex64)
    d = d_skip.astype(jnp.float32).reshape(S5_GROUPS, S5_GROUP)
    y_lat = u_lat * d
    y_ctx = u_ctx * d if ctx_out else None
    s0 = jnp.zeros((h_lat.shape[0], S5_GROUPS, S5_STATE), jnp.complex64)
    for direction in range(2):
        reverse = direction == 1
        lam_bar, b_bar = s5_discretise(a_re[direction], a_im[direction], log_dt[direction],
                                       b_re[direction], b_im[direction])
        c_mat = lax.complex(c_re[direction].astype(jnp.float32), c_im[direction].astype(jnp.float32))
        st_ctx = s5_scan(uc_ctx, lam_bar, b_bar, s0, reverse)
        s_ctx_final = st_ctx[:, 0] if reverse else st_ctx[:, -1]
        st_lat = s5_scan(uc_lat, lam_bar, b_bar, s_ctx_final, reverse)
        y_lat = y_lat + jnp.einsum('btgp,ghp->btgh', st_lat, c_mat).real
        if ctx_out:
            y_ctx = y_ctx + jnp.einsum('btgp,ghp->btgh', st_ctx, c_mat).real

    def glu_out(y, h):
        z = jax.nn.gelu(y.reshape(h.shape).astype(h.dtype))
        a, g = jnp.split(z @ w_glu, 2, axis=-1)
        return a * jax.nn.sigmoid(g)

    return (glu_out(y_ctx, h_ctx) if ctx_out else None), glu_out(y_lat, h_lat)

def hgrn_project(h, w_in, with_query):
    def heads(t):
        return t.astype(jnp.float32).reshape(t.shape[0], t.shape[1], HG_HEADS, -1)
    if with_query:
        q, i, zf, zb, g = jnp.split(h @ w_in, 5, axis=-1)
        return heads(jax.nn.silu(q)), heads(i), heads(zf), heads(zb), g
    i, zf, zb = jnp.split(h @ w_in[:, D_MODEL:4 * D_MODEL], 3, axis=-1)
    return None, heads(i), heads(zf), heads(zb), None

def forget_gate(logit, lb):
    lb = lb.astype(jnp.float32).reshape(HG_HEADS, HG_DK)
    log_f = jnp.logaddexp(jax.nn.log_sigmoid(logit), jnp.log(lb) + jax.nn.log_sigmoid(-logit))
    k = (1 - lb) * jax.nn.sigmoid(-logit)
    return log_f, k

def chunked_gated_recurrence(q, k, v, logf, s0):
    b_, t, h, kd = k.shape
    n = t // HG_CHUNK

    def chunks(z):
        return z.reshape(b_, n, HG_CHUNK, h, z.shape[-1])

    k, v, logf = chunks(k), chunks(v), chunks(logf)
    cum = jnp.cumsum(logf, axis=2)
    cum_last = cum[:, :, -1]
    k_end = k * jnp.exp(cum_last[:, :, None] - cum)
    u = jnp.einsum('bnchk,bnchv->bnhkv', k_end, v)

    def step(s, inp):
        decay, inc = inp
        return decay[..., None] * s + inc, s

    s_fin, s_in = lax.scan(step, s0, (jnp.moveaxis(jnp.exp(cum_last), 1, 0), jnp.moveaxis(u, 1, 0)))
    if q is None:
        return None, s_fin
    s_in = jnp.moveaxis(s_in, 0, 1)
    q = chunks(q)
    qb = q * jnp.exp(cum)
    kb = k * jnp.exp(-cum)
    scores = jnp.einsum('bnchk,bnshk->bnhcs', qb, kb)
    mask = jnp.tril(jnp.ones((HG_CHUNK, HG_CHUNK), dtype=bool))
    scores = jnp.where(mask, scores, 0.0)
    o = jnp.einsum('bnhcs,bnshv->bnchv', scores, v) + jnp.einsum('bnchk,bnhkv->bnchv', qb, s_in)
    return o.reshape(b_, t, h, v.shape[-1]), s_fin

def hgrn_readout(o, g, o_norm, w_out):
    b_, t, h, dv = o.shape
    o = o * lax.rsqrt(jnp.mean(o * o, axis=-1, keepdims=True) + NORM_EPS)
    o = o.reshape(b_, t, h * dv) * o_norm.astype(jnp.float32)
    return (o.astype(g.dtype) * jax.nn.silu(g)) @ w_out

def hgrn_mixer(h_ctx, h_lat, w_in, lb_fwd, lb_bwd, o_norm, w_out, ctx_out):
    q_l, v_l, zf_l, zb_l, g_l = hgrn_project(h_lat, w_in, True)
    q_c, v_c, zf_c, zb_c, g_c = hgrn_project(h_ctx, w_in, ctx_out)
    s0 = jnp.zeros((h_lat.shape[0], HG_HEADS, HG_DK, HG_DV), jnp.float32)
    flip = functools.partial(jnp.flip, axis=1)
    o_lat, o_ctx = [], []
    for z_c, z_l, lb, reverse in ((zf_c, zf_l, lb_fwd, False), (zb_c, zb_l, lb_bwd, True)):
        orient = flip if reverse else (lambda z: z)
        logf_c, k_c = forget_gate(z_c, lb)
        logf_l, k_l = forget_gate(z_l, lb)
        oc, s_ctx = chunked_gated_recurrence(orient(q_c) if ctx_out else None, orient(k_c), orient(v_c),
                                             orient(logf_c), s0)
        ol, _ = chunked_gated_recurrence(orient(q_l), orient(k_l), orient(v_l), orient(logf_l), s_ctx)
        o_lat.append(orient(ol))
        if ctx_out:
            o_ctx.append(orient(oc))
    y_lat = hgrn_readout(o_lat[0] + o_lat[1], g_l, o_norm, w_out)
    y_ctx = hgrn_readout(o_ctx[0] + o_ctx[1], g_c, o_norm, w_out) if ctx_out else None
    return y_ctx, y_lat

def second_inputs(seed: int = 0) -> dict:
    key = jax.random.key(seed)
    ks = iter(jax.random.split(key, 32))
    d = D_MODEL
    n_s5 = (DEPTH_2 + N_MIXERS - 1) // N_MIXERS
    n_hg = DEPTH_2 // N_MIXERS
    f32 = jnp.float32

    def nrm(shape, scale):
        return scale * jax.random.normal(next(ks), shape, f32)

    def gain(shape):
        return 1.0 + 0.05 * jax.random.normal(next(ks), shape, f32)

    return {
        "x": nrm((BATCH, SEQ, d), 1.0),
        "c": nrm((BATCH, d), 1.0),
        "ctx": nrm((BATCH, CTX_LEN, d), 1.0),
        "c_ctx": nrm((d,), 1.0),
        "w_mod": nrm((DEPTH_2, d, 6 * d), 0.5 * d ** -0.5),
        "b_mod": nrm((DEPTH_2, 6 * d), 0.02),
        "norm_mix_pre": gain((DEPTH_2, d)),
        "norm_mix_post": gain((DEPTH_2, d)),
        "norm_mlp_pre": gain((DEPTH_2, d)),
        "norm_mlp_post": gain((DEPTH_2, d)),
        "w_mlp_in": nrm((DEPTH_2, d, MLP_HIDDEN), d ** -0.5),
        "w_mlp_out": nrm((DEPTH_2, MLP_HIDDEN, d), MLP_HIDDEN ** -0.5),
        "s5_a_re": -0.5 + nrm((n_s5, 2, S5_GROUPS, S5_STATE), 0.01),
        "s5_a_im": math.pi * jnp.arange(S5_STATE, dtype=f32) + nrm((n_s5, 2, S5_GROUPS, S5_STATE), 0.01),
        "s5_log_dt": jax.random.uniform(next(ks), (n_s5, 2, S5_GROUPS), f32,
                                        math.log(S5_DT_MIN), math.log(S5_DT_MAX)),
        "s5_b_re": nrm((n_s5, 2, S5_GROUPS, S5_STATE, S5_GROUP), (2 * S5_GROUP) ** -0.5),
        "s5_b_im": nrm((n_s5, 2, S5_GROUPS, S5_STATE, S5_GROUP), (2 * S5_GROUP) ** -0.5),
        "s5_c_re": nrm((n_s5, 2, S5_GROUPS, S5_GROUP, S5_STATE), S5_STATE ** -0.5),
        "s5_c_im": nrm((n_s5, 2, S5_GROUPS, S5_GROUP, S5_STATE), S5_STATE ** -0.5),
        "s5_d": nrm((n_s5, d), 1.0),
        "s5_w_glu": nrm((n_s5, d, 2 * d), d ** -0.5),
        "hg_w_in": nrm((n_hg, d, 5 * d), d ** -0.5),
        "hg_lb_raw": nrm((2, n_hg, HG_HEADS * HG_DK), 0.1),
        "hg_o_norm": gain((n_hg, d)),
        "hg_w_out": nrm((n_hg, d, d), d ** -0.5),
    }

def second_block(x, c, ctx, c_ctx, w_mod, b_mod, norm_mix_pre, norm_mix_post, norm_mlp_pre, norm_mlp_post,
              w_mlp_in, w_mlp_out, s5_a_re, s5_a_im, s5_log_dt, s5_b_re, s5_b_im, s5_c_re, s5_c_im, s5_d,
              s5_w_glu, hg_w_in, hg_lb_raw, hg_o_norm, hg_w_out):
    lb_w = jax.nn.softmax(hg_lb_raw.astype(jnp.float32), axis=1)
    lb = jnp.cumsum(lb_w, axis=1) - lb_w[:, :1]
    x_lat, x_ctx = x, ctx
    for layer in range(DEPTH_2):
        ctx_live = layer < DEPTH_2 - 1
        j = layer // N_MIXERS
        sh1, sc1, gt1, sh2, sc2, gt2 = adaln(c, w_mod[layer], b_mod[layer])
        csh1, csc1, cgt1, csh2, csc2, cgt2 = adaln(c_ctx, w_mod[layer], b_mod[layer])
        h_lat = modulate(rmsnorm(x_lat, norm_mix_pre[layer]), sh1[:, None], sc1[:, None])
        h_ctx = modulate(rmsnorm(x_ctx, norm_mix_pre[layer]), csh1, csc1)
        if layer % N_MIXERS == 0:
            y_ctx, y_lat = s5_mixer(h_ctx, h_lat, s5_a_re[j], s5_a_im[j], s5_log_dt[j], s5_b_re[j], s5_b_im[j],
                                    s5_c_re[j], s5_c_im[j], s5_d[j], s5_w_glu[j], ctx_live)
        else:
            y_ctx, y_lat = hgrn_mixer(h_ctx, raster_to_colmajor(h_lat), hg_w_in[j], lb[0, j], lb[1, j],
                                      hg_o_norm[j], hg_w_out[j], ctx_live)
            y_lat = colmajor_to_raster(y_lat)
        x_lat = x_lat + gt1[:, None] * rmsnorm(y_lat, norm_mix_post[layer])
        h_lat = modulate(rmsnorm(x_lat, norm_mlp_pre[layer]), sh2[:, None], sc2[:, None])
        x_lat = x_lat + gt2[:, None] * rmsnorm(sq_relu_mlp(h_lat, w_mlp_in[layer], w_mlp_out[layer]),
                                               norm_mlp_post[layer])
        if ctx_live:
            x_ctx = x_ctx + cgt1 * rmsnorm(y_ctx, norm_mix_post[layer])
            h_ctx = modulate(rmsnorm(x_ctx, norm_mlp_pre[layer]), csh2, csc2)
            x_ctx = x_ctx + cgt2 * rmsnorm(sq_relu_mlp(h_ctx, w_mlp_in[layer], w_mlp_out[layer]),
                                           norm_mlp_post[layer])
    return x_lat


def setup_inputs(seed=0):
    out = dict(first_inputs(seed))
    for name, value in second_inputs(seed + 1).items():
        if name != "x":
            out[name + "_2"] = value
    return out


def reference(
    x, c, w_mod, b_mod, ln_g, ln_b, a_w_in, a_w_out, a_lam_q1, a_lam_k1, a_lam_q2, a_lam_k2,
    a_subln_g, kv_w_mod, kv_b_mod, kv_w, kv_b_f, b_w_in, b_w_out, c_2, ctx_2, c_ctx_2, w_mod_2,
    b_mod_2, norm_mix_pre_2, norm_mix_post_2, norm_mlp_pre_2, norm_mlp_post_2, w_mlp_in_2,
    w_mlp_out_2, s5_a_re_2, s5_a_im_2, s5_log_dt_2, s5_b_re_2, s5_b_im_2, s5_c_re_2, s5_c_im_2,
    s5_d_2, s5_w_glu_2, hg_w_in_2, hg_lb_raw_2, hg_o_norm_2, hg_w_out_2,
):
    x = first_block(
        x, c, w_mod, b_mod, ln_g, ln_b, a_w_in, a_w_out, a_lam_q1, a_lam_k1, a_lam_q2, a_lam_k2,
        a_subln_g, kv_w_mod, kv_b_mod, kv_w, kv_b_f, b_w_in, b_w_out,
    )
    return second_block(
        x, c_2, ctx_2, c_ctx_2, w_mod_2, b_mod_2, norm_mix_pre_2, norm_mix_post_2,
        norm_mlp_pre_2, norm_mlp_post_2, w_mlp_in_2, w_mlp_out_2, s5_a_re_2, s5_a_im_2,
        s5_log_dt_2, s5_b_re_2, s5_b_im_2, s5_c_re_2, s5_c_im_2, s5_d_2, s5_w_glu_2, hg_w_in_2,
        hg_lb_raw_2, hg_o_norm_2, hg_w_out_2,
    )


_drawn_inputs = setup_inputs


def setup_inputs(seed=0):
    import zlib

    import numpy as np

    out = dict(_drawn_inputs(seed))
    spreads = {}
    factors = {'b_mod': 5.731,
     'a_lam_q1': 7.892,
     'a_lam_k1': 8.0,
     'a_lam_q2': 8.0,
     'a_lam_k2': 6.597,
     'a_subln_g': 25.873,
     'kv_b_mod': 8.0,
     'ctx_2': 83.456,
     'c_ctx_2': 158.848,
     'norm_mix_pre_2': 3.799,
     'norm_mix_post_2': 4.011,
     'norm_mlp_pre_2': 3.584,
     'norm_mlp_post_2': 4.133,
     's5_a_re_2': 200.0,
     's5_a_im_2': 3.732,
     's5_log_dt_2': 4.764,
     's5_b_re_2': 4.348,
     's5_b_im_2': 4.294,
     's5_c_re_2': 4.315,
     's5_c_im_2': 4.269}
    for name, (base, spread) in spreads.items():
        noise = np.random.default_rng([zlib.crc32(name.encode()), seed]).standard_normal(out[name].shape)
        drawn = base * np.exp(spread * noise) if base else spread * noise
        out[name] = __import__('jax').numpy.asarray(drawn.astype(out[name].dtype))
    for name, factor in factors.items():
        out[name] = (out[name] * factor).astype(out[name].dtype)
    return out
```

```python
import math
from contextlib import ExitStack

import concourse.bass as bass
from concourse import mybir

F32 = mybir.dt.float32
ALU = mybir.AluOpType
ACT = mybir.ActivationFunctionType
AX = mybir.AxisListType.X
MUL, ADD, SUB, MAX, MIN = ALU.mult, ALU.add, ALU.subtract, ALU.max, ALU.min

D = 2048
KT = 16
ALPHA = 4.0 ** 0.25
LAM_INIT = 0.8 - 0.6 * math.exp(-0.3 * 0)
QK_SCALE = 128.0 ** -0.5
GELU_C = math.sqrt(2.0 / math.pi)
NSLOT = 3
SLOTF = 4096
DOUBLINGS = 10


class Queue:

    def __init__(self, sem):
        self.sem, self.n, self.items, self.seen = sem, 0, [], {}

    def wait(self, *tokens):
        for tok in tokens:
            if tok is None:
                continue
            if not isinstance(tok[-1], int):
                self.wait(*tok)
                continue
            sem, val = tok
            if self.seen.get(id(sem), 0) < val:
                self.seen[id(sem)] = val
                self.items.append(lambda e, s=sem, v=val: e.wait_ge(s, v))

    def do(self, fn, *tokens, inc=True):
        self.wait(*tokens)
        if inc:
            self.n += 1
            self.items.append(lambda e, f=fn: f(e).then_inc(self.sem, 1))
        else:
            self.items.append(fn)
        return (self.sem, self.n)

    @property
    def t(self):
        return (self.sem, self.n)

    def run(self, e):
        for f in self.items:
            f(e)


def pipeline(n, stages):
    for t in range(n + len(stages) - 1):
        for s in range(len(stages) - 1, -1, -1):
            if 0 <= t - s < n:
                stages[s](t - s)


def build(nc, A, out):
    with ExitStack() as ctx:
        sem = lambda name: ctx.enter_context(nc.semaphore(name))
        P, V, S, G = (Queue(sem(n)) for n in ("s_pe", "s_dve", "s_act", "s_pool"))
        SP = Queue(sem("s_sp"))

        dma_count = {}

        def dma(q, dst, src, s, *tokens):
            q.wait(*tokens)
            dma_count[s] = dma_count.get(s, 0) + 16
            q.items.append(lambda e: e.dma_start(dst, src).then_inc(sems[s], 16))
            return (sems[s], dma_count[s])

        sems = {n: sem("d_" + n) for n in (
            ["rows", "x", "ctx", "lam", "sub", "b", "c", "ar", "ai", "dt", "hc", "ms", "cl", "kk", "out", "bc0", "bc1", "zf"]
            + [f"ring{i}" for i in range(NSLOT)])}

        sb = lambda name, n: ctx.enter_context(nc.sbuf_tensor(name, [128, n], F32))
        ring = sb("ring", NSLOT * SLOTF)
        AR = sb("arena", 28672)
        LT = sb("LT", 2 * 128 * 17)
        L1, L2 = LT[:, 0:2304], LT[:, 2304:4352]
        MSB = sb("MSB", 2048)
        BBD = sb("BBD", 512)
        sm = sb("sm", 16 * 128)
        ident = sb("ident", 128)
        cols = sb("cols", 512)
        MODC = sb("MODC", 416)
        SF = sb("SF", 256 * 2)
        LR8 = sb("LR8", 256)
        LS8 = sb("LS8", 256)
        st = sb("st", 256)
        banks = [ctx.enter_context(nc.psum_tensor(f"bank{i}", [128, 512], F32)) for i in range(8)]

        m_state_d = nc.dram_tensor("m_state", [128, 128 * 256], F32).ap()
        cl_d = nc.dram_tensor("cl_out", [128, 128 * 256], F32).ap()
        toep_d = nc.dram_tensor("toep", [8, 16, 128, 128], F32).ap()

        def reg(off, n):
            return AR[:, off:off + n]

        ring_state = {"n": 0}
        slot_free = [None] * NSLOT

        def load(src, dst=None):
            i = ring_state["n"] % NSLOT
            ring_state["n"] += 1
            n = 1
            for d_ in src.shape[1:]:
                n *= d_
            t = ring[:, i * SLOTF:i * SLOTF + n]
            if len(src.shape) == 3:
                tv = t.rearrange("p (a b) -> p a b", a=src.shape[1])
            else:
                tv = t
            tok = dma(SP, tv, src, f"ring{i}", slot_free[i])
            return i, tv, tok

        def load_w(W, k0, n0, n=256):
            return load(W[k0:k0 + 2048, n0:n0 + n].rearrange("(k p) n -> p k n", p=128))

        plan = []
        loaded = []

        def ahead():
            while plan and len(loaded) < NSLOT and slot_ready[0] > 0:
                slot_ready[0] -= 1
                loaded.append(plan.pop(0)())

        slot_ready = [NSLOT]

        def take():
            ahead()
            return loaded.pop(0)

        def release(i, tok):
            slot_free[i] = tok
            slot_ready[0] += 1
            ahead()

        bank_free = [None] * 8
        turn = {}

        def bank(group):
            k = turn.get(group, 0)
            turn[group] = k + 1
            i = group[k % len(group)]
            return i, banks[i], bank_free[i]

        GA = (0, 1, 2)
        GB = (3, 4)
        GC = (5, 6)

        def mm(o, l, r, start, stop, *w, inc=False):
            return P.do(lambda e: e.matmul(o, l, r, start=start, stop=stop, skip_group_check=True), *w, inc=inc)

        def tr(o, i, *w, inc=False, k=128):
            idn = ident[0:k, 0:k]
            return P.do(lambda e: e.transpose(o, i, idn), *w, inc=inc)

        def tt(q, o, a, b, op, *w):
            return q.do(lambda e: e.tensor_tensor(o, a, b, op), *w)

        def ts(q, o, a, s1, s2, o1, o2, *w):
            if s2 is None:
                return q.do(lambda e: e.tensor_scalar(o, a, s1, None, o1), *w)
            return q.do(lambda e: e.tensor_scalar(o, a, s1, s2, o1, o2), *w)

        def stt(o, a, s, b, o1, o2, *w):
            return V.do(lambda e: e.scalar_tensor_tensor(out=o, in0=a, scalar=s, in1=b, op0=o1, op1=o2), *w)

        def act(o, i, f, *w, **kw):
            return S.do(lambda e: e.activation(o, i, f, **kw), *w)

        def recip(o, a, *w):
            return V.do(lambda e: e.reciprocal(o, a), *w)

        def copy(q, o, a, *w):
            if q is S:
                return S.do(lambda e: e.copy(o, a), *w)
            return q.do(lambda e: e.tensor_copy(o, a), *w)

        def rsqrt(o, v, tmp, *w):
            a = act(tmp, v, ACT.Ln, *w)
            b = act(o, tmp, ACT.Exp, a, scale=-0.5)
            tt(V, tmp, o, o, MUL, b)
            tt(V, tmp, tmp, v, MUL, V.t)
            ts(V, tmp, tmp, -0.5, 1.5, MUL, ADD, V.t)
            return tt(V, o, o, tmp, MUL, V.t)

        G.do(lambda e: e.memset(ident[:, :], 0.0))
        id_tok = G.do(lambda e: e.affine_select(out=ident[:, :], in_=ident[:, :], compare_op=ALU.not_equal, fill=1.0,
                                                base=0, pattern=[[-1, 128]], channel_multiplier=1), G.t)

        vecs = [("c", A["c"].rearrange("a (r n) -> (a r) n", n=128), 16),
                ("c2", A["c_2"].rearrange("a (r n) -> (a r) n", n=128), 16),
                ("cc", A["c_ctx_2"].rearrange("(r n) -> r n", n=128), 16),
                ("bm", A["b_mod"].rearrange("l (r n) -> (l r) n", n=128), 96),
                ("bkv", A["kv_b_mod"].rearrange("(r n) -> r n", n=128), 32),
                ("bm2", A["b_mod_2"].rearrange("l (r n) -> (l r) n", n=128), 96),
                ("npre", A["norm_mix_pre_2"].rearrange("l (r n) -> (l r) n", n=128), 16),
                ("npost", A["norm_mix_post_2"].rearrange("l (r n) -> (l r) n", n=128), 16),
                ("mpre", A["norm_mlp_pre_2"].rearrange("l (r n) -> (l r) n", n=128), 16),
                ("mpost", A["norm_mlp_post_2"].rearrange("l (r n) -> (l r) n", n=128), 16),
                ("sd", A["s5_d_2"].rearrange("l (r n) -> (l r) n", n=128), 16)]
        col = {}
        pos = 0
        rows_base = 24576
        for name, src, n in vecs:
            col[name] = pos
            r = 0
            while r < n:
                tile, p0 = (pos + r) // 128, (pos + r) % 128
                m = min(n - r, 128 - p0)
                rows_tok = dma(SP, reg(rows_base + tile * 128, 128)[p0:p0 + m, :], src[r:r + m, :], "rows")
                r += m
            pos += n
        ncol = pos
        for tile in range((ncol + 127) // 128):
            m = min(128, ncol - tile * 128)
            i, b, fr = bank(GA)
            t = tr(b[:, 0:m], reg(rows_base + tile * 128, 128)[0:m, :], rows_tok, id_tok, fr, inc=True, k=m)
            bank_free[i] = copy(V, cols[:, tile * 128:tile * 128 + m], b[:, 0:m], t)
        rows_read = P.t

        def C(name, a=0, n=16):
            return cols[:, col[name] + a:col[name] + a + n]

        cact = sm[:, 15 * 128:15 * 128 + 48]
        tmp = sm[:, 15 * 128 + 48:15 * 128 + 96]
        ts(V, tmp, C("c", 0, 48), -80.0, None, MAX, None, V.t)
        t = act(tmp, tmp, ACT.Exp, V.t, scale=-1.0)
        ts(V, tmp, tmp, 1.0, None, ADD, None, t)
        recip(tmp, tmp, V.t)
        cact_tok = tt(V, cact, tmp, C("c", 0, 48), MUL, V.t)
        cpair = cact[:, 16:48].rearrange("p (v k) -> p k v", v=2)

        def panels(W, k0, n0, n1):
            for n in range(n0, n1, 256):
                plan.append(lambda W=W, k0=k0, n=n: load_w(W, k0, n))

        panels(A["w_mod_2"][0], 0, 0, 4096)
        panels(A["w_mod_2"][0], 0, 4096, 12288)
        panels(A["w_mod"][0], 0, 0, 6144)
        panels(A["kv_w_mod"], 0, 0, 4096)
        panels(A["w_mod"][1], 0, 0, 6144)
        panels(A["a_w_in"][0], 0, 0, 8192)
        panels(A["a_w_out"][0], 0, 0, 2048)
        panels(A["b_w_in"][0], 0, 0, 4096)
        panels(A["kv_w"], 0, 0, 4096)
        panels(A["b_w_out"][0], 0, 0, 2048)
        s5_plan = []
        late = []

        MB0 = banks[7]
        m_off = {"m2": 0, "m2x": 96, "m0": 128, "kv": 176, "m1": 208}
        mod_tok = {}

        def mod_panels(name, n, which, biases, extra=None):
            base = m_off[name]
            for pnl in range(n // 2):
                i, w, tok = take()
                for j in range(2):
                    nt = 2 * pnl + j
                    for k in range(KT):
                        if which == "pair" and nt < 32:
                            o = MB0[:, 256 + 2 * nt:256 + 2 * nt + 2]
                            r = cpair[:, k, :]
                        else:
                            o = MB0[:, base + nt:base + nt + 1]
                            r = cact[:, (0 if which == "c" else 16) + k:(0 if which == "c" else 16) + k + 1]
                        t = mm(o, w[:, k, j * 128:(j + 1) * 128], r, k == 0, k == KT - 1, tok, cact_tok,
                               inc=(j == 1 and k == KT - 1))
                release(i, t)
                yield
            if which == "pair":
                pr = MB0[:, 256:320].rearrange("p (n v) -> p v n", v=2)
                tt(V, MODC[:, m_off["m2"]:m_off["m2"] + 32], pr[:, 0, :], C(biases, 0, 32), ADD, t)
                tt(V, MODC[:, m_off["m2x"]:m_off["m2x"] + 32], pr[:, 1, :], C(biases, 0, 32), ADD, t)
                mod_tok["first"] = V.t
                P.wait(V.t)
            else:
                off, boff = extra
                tt(V, MODC[:, base + off:base + n], MB0[:, base + off:base + n], C(biases, boff + off, n - off), ADD, t)
                mod_tok[name] = V.t
                P.wait(V.t)

        def M(name, a, n=16):
            return MODC[:, m_off[name] + a:m_off[name] + a + n]

        def run_all(gen, k=None):
            c = 0
            for _ in gen:
                c += 1
                if k is not None and c >= k:
                    return False
            return True

        def first_third():
            yield from mod_panels("m2", 32, "pair", "bm2")

        def rest_mods():
            base = m_off["m2"]
            for pnl in range(32):
                i, w, tok = take()
                for j in range(2):
                    nt = 32 + 2 * pnl + j
                    for k in range(KT):
                        t = mm(MB0[:, base + nt:base + nt + 1], w[:, k, j * 128:(j + 1) * 128],
                               cact[:, 16 + k:17 + k], k == 0, k == KT - 1, tok, inc=(j == 1 and k == KT - 1))
                release(i, t)
                yield
            tt(V, MODC[:, base + 32:base + 96], MB0[:, base + 32:base + 96], C("bm2", 32, 64), ADD, t)
            mod_tok["m2"] = V.t
            P.wait(V.t)
            yield from mod_panels("m0", 48, "c", "bm", (0, 0))
            yield from mod_panels("kv", 32, "c", "bkv", (0, 0))
            yield from mod_panels("m1", 48, "c", "bm", (0, 48))

        ahead()
        run_all(first_third())
        mods = rest_mods()
        mods_left = [32 + 24 + 16 + 24 + 1]

        def mod_step(n=1):
            for _ in range(n):
                if mods_left[0]:
                    mods_left[0] -= 1
                    next(mods, None)

        def bcast(dst, colap, *w):
            toks = []
            for q in range(4):
                i, b, fr = bank(GC)
                for j in range(4):
                    k = 4 * q + j
                    t = mm(b[:, 128 * j:128 * j + 128], colap[:, k:k + 1].to_broadcast([128, 128]), ident[:, :],
                           True, True, fr, *w, inc=(j == 3))
                bank_free[i] = copy(S, dst[:, 512 * q:512 * q + 512], b[:, :], t, *w)
            return bank_free[i]

        smt = [sm[:, i * 128:(i + 1) * 128] for i in range(15)]
        are, aim, dtb, zr, zi, wr, wi, ta, tb, tc = smt[:10]
        a_re_tok = dma(SP, are, A["s5_a_re_2"][0].rearrange("d (k g) p -> (d k) (g p)", g=2), "ar")
        a_im_tok = dma(SP, aim, A["s5_a_im_2"][0].rearrange("d (k g) p -> (d k) (g p)", g=2), "ai")
        dt_tok = dma(SP, tc[:, 0:2], A["s5_log_dt_2"][0].rearrange("d (k g) -> (d k) g", g=2), "dt")
        t = act(tc[:, 2:4], tc[:, 0:2], ACT.Exp, dt_tok)
        sc0 = 2.0 ** -DOUBLINGS
        for g in range(2):
            h = slice(g * 64, g * 64 + 64)
            ts(V, zr[:, h], are[:, h], tc[:, 2 + g:3 + g], sc0, MUL, MUL, t, a_re_tok, a_im_tok)
            ts(V, zi[:, h], aim[:, h], tc[:, 2 + g:3 + g], sc0, MUL, MUL)
        ts(V, wr, zr, 1.0 / 6, 1.0, MUL, ADD, V.t)
        ts(V, wi, zi, 1.0 / 6, None, MUL, None)
        for n in (5, 4, 3, 2):
            tt(V, ta, zr, wr, MUL, V.t)
            tt(V, tb, zi, wi, MUL)
            tt(V, ta, ta, tb, SUB, V.t)
            tt(V, tb, zr, wi, MUL, V.t)
            tt(V, wi, zi, wr, MUL, V.t)
            tt(V, tb, tb, wi, ADD, V.t)
            ts(V, wr, ta, 1.0 / n, 1.0, MUL, ADD, V.t)
            ts(V, wi, tb, 1.0 / n, None, MUL, None)
        tt(V, ta, zr, wr, MUL, V.t)
        tt(V, tb, zi, wi, MUL)
        tt(V, ta, ta, tb, SUB, V.t)
        tt(V, tb, zr, wi, MUL, V.t)
        tt(V, wi, zi, wr, MUL, V.t)
        tt(V, wi, tb, wi, ADD, V.t)
        copy(V, wr, ta, V.t)
        for _ in range(DOUBLINGS):
            stt(ta, wr, 2.0, wr, ADD, MUL, V.t)
            tt(V, tb, wi, wi, MUL)
            stt(wi, wr, 1.0, wi, ADD, MUL, V.t)
            tt(V, wr, ta, tb, SUB, V.t)
            ts(V, wi, wi, 2.0, None, MUL, None, V.t)
        cr, ci, den, lbr, lbi, pr_, pi_ = smt[8], smt[9], smt[10], smt[11], smt[12], smt[13], smt[14]
        tt(V, den, are, are, MUL, V.t)
        tt(V, zr, aim, aim, MUL)
        tt(V, den, den, zr, ADD, V.t)
        recip(den, den, V.t)
        tt(V, ta, wr, are, MUL, V.t)
        tt(V, zr, wi, aim, MUL)
        tt(V, ta, ta, zr, ADD, V.t)
        tt(V, cr, ta, den, MUL, V.t)
        tt(V, ta, wi, are, MUL, V.t)
        tt(V, zr, wr, aim, MUL)
        tt(V, ta, ta, zr, SUB, V.t)
        tt(V, ci, ta, den, MUL, V.t)
        ts(V, lbr, wr, 1.0, None, ADD, None, V.t)
        copy(V, lbi, wi)
        tcr, tci, t1r, t1i = smt[0], smt[1], smt[2], smt[3]
        i, b, fr = bank(GA)
        for j, s_ in enumerate((cr, ci, lbr, lbi)):
            t = tr(b[:, 128 * j:128 * j + 128], s_, V.t, fr, id_tok, inc=(j == 3))
        bank_free[i] = copy(V, sm[:, 0:512], b[:, :], t)

        L1v = L1[:, :].rearrange("p (r d t) -> p r d t", r=2, t=9)
        L2v = L2[:, :].rearrange("p (r d t) -> p r d t", r=2, t=8)
        curr, curi, nxr, nxi = smt[4], smt[5], smt[6], smt[7]
        pa, pb_ = smt[10], smt[11]
        V.do(lambda e: e.memset(curr, 1.0), V.t)
        V.do(lambda e: e.memset(curi, 0.0), V.t)
        for tau in range(9):
            for r_, cur in enumerate((curr, curi)):
                copy(V, L1v[:, r_, 0:64, tau], cur[:, 0:64], V.t)
                copy(V, L1v[:, r_, 64:128, 8 - tau], cur[:, 64:128])
                if tau < 8:
                    copy(V, L2v[:, r_, 0:64, 7 - tau], cur[:, 0:64])
                    copy(V, L2v[:, r_, 64:128, tau], cur[:, 64:128])
            if tau == 8:
                copy(V, LR8[:, 0:128], curr)
                copy(V, LR8[:, 128:256], curr)
                ts(V, LS8[:, 0:128], curi, -1.0, None, MUL, None)
                copy(V, LS8[:, 128:256], curi)
                break
            tt(V, pa, curr, t1r, MUL, V.t)
            tt(V, pb_, curi, t1i, MUL)
            tt(V, nxr, pa, pb_, SUB, V.t)
            tt(V, pa, curr, t1i, MUL, V.t)
            tt(V, pb_, curi, t1r, MUL)
            tt(V, nxi, pa, pb_, ADD, V.t)
            curr, nxr = nxr, curr
            curi, nxi = nxi, curi
        L_tok = V.t

        R1, R2, R3, R4, R5 = 0, 4096, 8192, 12288, 16384

        def rms_stat(xv, junk, slot, eps, *w):
            for t2 in range(2):
                a = act(junk, xv[:, t2, :], ACT.Square, *w, S.t, accum_out=st[:, slot + 2 + t2:slot + 3 + t2])
            ts(V, st[:, slot + 2:slot + 4], st[:, slot + 2:slot + 4], 1.0 / D, eps, MUL, ADD, S.t)
            return rsqrt(st[:, slot:slot + 2], st[:, slot + 2:slot + 4], st[:, slot + 4:slot + 6], V.t)

        def make_u(xv, hv, rslot, abc, bbc, hc, hc2, U, step, *w):
            hc_free = prev_perm = None
            for qd in range(4):
                cs = slice(512 * qd, 512 * qd + 512)
                for t2 in range(2):
                    stt(hv[:, t2, cs], xv[:, t2, cs], st[:, rslot + t2:rslot + t2 + 1], abc[:, cs], MUL, MUL, *w, V.t)
                    tt(V, hv[:, t2, cs], hv[:, t2, cs], bbc[:, cs], ADD, V.t)
                for t2 in range(2):
                    tok = dma(G, hc[16 * t2:16 * t2 + 16, :, :],
                              hv[:, t2, cs], "hc", V.t, prev_perm)
                sv = hc[0:32, :, :].rearrange("p q (g h) -> p g q h", h=16)
                for q_, g0, g1 in ((V, 0, 14), (S, 14, 26), (G, 26, 32)):
                    copy(q_, hc2[0:32, g0:g1, :, :], sv[:, g0:g1], tok, hc_free, *w)
                perm = (V.t, S.t, G.t)
                for g8 in range(0, 32, 16):
                    i, b, fr = bank(GA)
                    for j in range(16):
                        g = g8 + j
                        t = tr(b[:, 32 * j:32 * j + 32], hc2[0:32, g, :, :].rearrange("p q h -> p (q h)"), perm, fr,
                               inc=(j == 15), k=32)
                    g0 = 32 * qd + g8
                    bank_free[i] = copy(S, U[:, g0:g0 + 16, :], b[:, :].rearrange("p (g c) -> p g c", g=16), t, *w)
                hc_free, prev_perm = t, perm
                step()
            return bank_free[i]

        ctxv = reg(R1, 4096).rearrange("p (t n) -> p t n", t=2)
        hc = reg(R2, 4096).rearrange("p (q n) -> p q n", q=8)
        abc, bbc = reg(R3, 2048), reg(R3 + 2048, 2048)
        U = reg(R4, 4096).rearrange("p (g c) -> p g c", c=32)
        ctx_tok = dma(SP, ctxv, A["ctx_2"][0].rearrange("(t p) n -> p t n", p=128), "ctx")
        acol = st[:, 64:80]
        stt(acol, M("m2x", 16), 1.0, C("npre"), ADD, MUL, mod_tok["first"])
        acol2 = st[:, 80:96]
        stt(acol2, M("m2", 16), 1.0, C("npre"), ADD, MUL, mod_tok["first"])
        ctok = V.t
        a1 = bcast(abc, acol, ctok)
        a2 = bcast(bbc, M("m2x", 0), ctok)
        rt = rms_stat(ctxv, reg(R5, 2048), 0, 1e-6, ctx_tok)
        hc2 = reg(R5 + 2048, 4096).rearrange("p (g q h) -> p g q h", g=32, q=8)
        u_tok = make_u(ctxv, ctxv, 0, abc, bbc, hc, hc2, U, lambda: mod_step(2), ctx_tok, a1, a2, rt)

        braw = reg(R5, 4096).rearrange("p (r g q h) -> p r g q h", r=2, g=2, h=16)
        b_tok = dma(SP, reg(R5, 2048), A["s5_b_re_2"][0].rearrange("d (k g) p h -> (d k) (g p h)", g=2), "b", S.t, P.t, V.t, G.t)
        b_tok = dma(SP, reg(R5 + 2048, 2048), A["s5_b_im_2"][0].rearrange("d (k g) p h -> (d k) (g p h)", g=2), "b")
        bT = reg(R3, 4096).rearrange("p (r d h) -> p r d h", r=2, h=16)
        Bb = reg(R2, 4096).rearrange("p (r d h) -> p r d h", r=2, h=16)

        def to_state(raw_fn, dst, tok, *w):
            for r_ in range(2):
                for h4 in range(4):
                    i, b, fr = bank(GA)
                    for j in range(4):
                        for g2 in range(2):
                            t = mm(b[64 * g2:64 * g2 + 64, 128 * j:128 * j + 128], raw_fn(r_, g2, 4 * h4 + j),
                                   ident[:, :], True, True, tok, fr, inc=(j == 3 and g2 == 1))
                    bank_free[i] = copy(S, dst[:, r_, :, 4 * h4:4 * h4 + 4].rearrange("p d h -> p h d"),
                                        b[:, :].rearrange("p (h d) -> p h d", h=4), t, *w)
            return bank_free[i]

        t = to_state(lambda r_, g2, h: braw[:, r_, g2, :, h], bT, b_tok, V.t, P.t)
        tmpb = reg(R5, 2048).rearrange("p (d h) -> p d h", h=16)

        def bcw(x):
            return x.unsqueeze(2).to_broadcast([128, 128, 16])

        tt(V, tmpb, bT[:, 1], bcw(tci), MUL, t, u_tok)
        tt(V, Bb[:, 0], bT[:, 0], bcw(tcr), MUL)
        tt(V, Bb[:, 0], Bb[:, 0], tmpb, SUB, V.t)
        tt(V, tmpb, bT[:, 0], bcw(tci), MUL, V.t)
        tt(V, Bb[:, 1], bT[:, 1], bcw(tcr), MUL)
        tt(V, Bb[:, 1], Bb[:, 1], tmpb, ADD, V.t)
        Bb_tok = V.t

        def cmul(xr, xi, Lv, T, d0, outr, outi, t1, t2, neg, w_r, w_i):
            o4 = lambda y: y.rearrange("p (d t h) -> p d t h", d=8, t=T)
            for k in range(0, 8, 8):
                X = lambda x: x[:, d0:d0 + 8, :].unsqueeze(2).to_broadcast([128, 8, T, 16])
                Lb = lambda r_: Lv[:, r_, d0:d0 + 8, :].unsqueeze(3).to_broadcast([128, 8, T, 16])
                tt(V, o4(outr), X(xr), Lb(0), MUL, *w_r)
                tt(V, o4(t1), X(xi), Lb(1), MUL, V.t)
                tt(V, outr, outr, t1, SUB, V.t)
                r_tok = V.t
                tt(V, o4(outi), X(xr), Lb(1), MUL, *w_i)
                tt(V, o4(t2), X(xi), Lb(0), MUL, V.t)
                if neg:
                    stt(outi, outi, -1.0, t2, MUL, SUB, V.t)
                else:
                    tt(V, outi, outi, t2, ADD, V.t)
                return r_tok, V.t

        Vc = reg(R5, 8192).rearrange("p (k r d) -> p k r d", k=32, r=2)
        ms_dma = None
        vmat = MSB[:, :].rearrange("p (d r m) -> p d r m", d=8, r=2)
        blr, bli = reg(R3, 1024), reg(R3 + 1024, 1024)
        bt1, bt2 = reg(R3 + 2048, 1024), reg(R3 + 3072, 1024)
        bl_free = Bb_tok

        def v_matmuls(mv, Uv, d0, n, dst, base_tok, *w):
            i, b, fr = bank(GB)
            bv = b[:, :].rearrange("p (d r c) -> p d r c", r=2, c=32)
            for dd in range(n):
                dg = d0 + dd
                gp = dg % 64
                for r_ in range(2):
                    for g2 in range(2):
                        t = mm(bv[64 * g2:64 * g2 + 64, dd, r_, :], mv[:, dd, r_, 64 * g2:64 * g2 + 64],
                               Uv[:, 2 * gp + g2, :], True, True, fr, base_tok, *w,
                               inc=(dd == n - 1 and r_ == 1 and g2 == 1))
            if d0 < 64:
                dv = dst[:, :, :, d0:d0 + n]
                bank_free[i] = None
                for r_ in range(2):
                    tok = copy(S, dv[:, :, r_, :].rearrange("p k d -> p d k"), bv[:, 0:n, r_, :], t)
            else:
                for r_ in range(2):
                    tok = copy(S, dst[:, ::-1, r_, d0:d0 + n].rearrange("p k d -> p d k"), bv[:, 0:n, r_, :], t)
            bank_free[i] = tok
            return t, tok

        for ch in range(16):
            d0 = 8 * ch
            r_tok, i_tok = cmul(Bb[:, 0], Bb[:, 1], L2v, 8, d0, blr, bli, bt1, bt2, False,
                                (bl_free, L_tok, Bb_tok), (bl_free,))
            for r_, src in enumerate((blr, bli)):
                for half in range(2):
                    i, b, fr = bank(GA)
                    for j in range(4):
                        dd = 4 * half + j
                        t = tr(b[:, 128 * j:128 * j + 128], src[:, 128 * dd:128 * dd + 128],
                               i_tok, fr, inc=(j == 3))
                    bank_free[i] = copy(S, vmat[:, 4 * half:4 * half + 4, r_, :],
                                        b[:, :].rearrange("p (d m) -> p d m", d=4), t, ms_dma, P.t)
            bl_free = P.t
            ms_ready = bank_free[i]
            v_pe, v_tok = v_matmuls(vmat, U, d0, 8, Vc, ms_ready, u_tok, Bb_tok)
            ms_dma = dma(G, m_state_d[:, d0 * 256:d0 * 256 + 2048], MSB[:, :], "ms", ms_ready)
            mod_step(2)
        ms_all = ms_dma

        stA, stB = SF[:, 0:256], SF[:, 256:512]
        t_1, t_2 = sm[:, 512:768], sm[:, 768:1024]
        l_swap = lambda x: x.rearrange("p (r d) -> p r d", r=2)

        def chunk_step(cur, nxt, vk, *w):
            tt(V, t_1, cur, LR8[:, :], MUL, V.t, *w)
            tt(V, l_swap(t_2), l_swap(cur)[:, ::-1, :], l_swap(LS8[:, :]), MUL)
            tt(V, t_1, t_1, vk, ADD, V.t)
            return tt(V, nxt, t_1, t_2, ADD, V.t)

        V.do(lambda e: e.memset(stA, 0.0), V.t)
        cur, nxt = stA, stB
        for k in range(32):
            vk = Vc[:, k].rearrange("p r d -> p (r d)")
            chunk_step(cur, nxt, vk, v_tok)
            cur, nxt = nxt, cur
        ctx_state = V.t

        c_src = lambda n: A[n][0].rearrange("d (k g) h p -> (d k) (g h p)", g=2)
        c_tok = dma(SP, reg(R5, 2048), c_src("s5_c_re_2"), "c", ctx_state)
        c_tok = dma(SP, reg(R5 + 2048, 2048), c_src("s5_c_im_2"), "c")
        craw = reg(R5, 4096).rearrange("p (r g h q) -> p r g h q", r=2, g=2, h=16)
        cT = reg(R4, 4096).rearrange("p (r d h) -> p r d h", r=2, h=16)
        cT_tok = to_state(lambda r_, g2, h: craw[:, r_, g2, h, :], cT, c_tok, v_pe)
        KK = reg(R1, 3840).rearrange("p (a j h) -> p a j h", a=16, j=15)
        mask16 = smt[0]
        V.do(lambda e: e.tensor_reduce(mask16[:, 0:16], ident[:, :].rearrange("p (b h) -> p h b", b=8), AX, ADD),
             Bb_tok, V.t, id_tok)
        tt(V, KK[:, :, 7, :], C("sd").unsqueeze(2).to_broadcast([128, 16, 16]),
           mask16[:, 0:16].unsqueeze(1).to_broadcast([128, 16, 16]), MUL, V.t, u_tok)
        clr, cli = reg(R3, 1152), reg(R3 + 1152, 1152)
        ct1, ct2 = reg(R5 + 4096, 1152), reg(R5 + 5248, 1152)
        bd = BBD[:, :].rearrange("p (d r m) -> p d r m", d=8, r=2)
        bd_zero = G.do(lambda e: e.memset(BBD[:, :], 0.0))
        cl_dma = None
        kk_pe = None
        for ch in range(16):
            d0 = 8 * ch
            for g2 in range(2):
                for r_ in range(2):
                    tok = copy(G, bd[64 * g2:64 * g2 + 64, :, r_, 16 * g2:16 * g2 + 16],
                               Bb[64 * g2:64 * g2 + 64, r_, d0:d0 + 8, :], bd_zero, Bb_tok, kk_pe)
            bd_tok = tok
            r_tok, i_tok = cmul(cT[:, 0], cT[:, 1], L1v, 9, d0, clr, cli, ct1, ct2, True,
                                (cT_tok, cl_dma, kk_pe, bl_free), (cl_dma, kk_pe))
            clrv = clr.rearrange("p (d x) -> p d x", d=8)
            cliv = cli.rearrange("p (d x) -> p d x", d=8)
            fwd = ch < 8
            ko = 0 if fwd else 16
            oo = 16 if fwd else 0
            i, b, fr = bank(GB)
            bv = b[:, 0:256].rearrange("p (a x) -> p a x", a=2)
            for a in range(2):
                for m in range(4):
                    dd = 4 * a + m
                    o = bv[32 * m:32 * m + 32, a, :]
                    mm(o, bd[:, dd, 0, :], clrv[:, dd, ko:ko + 128], True, False, bd_tok, i_tok, fr)
                    kk_pe = mm(o, bd[:, dd, 1, :], cliv[:, dd, ko:ko + 128], False, True, inc=(dd == 7))
            a0 = (d0 % 64) // 4
            kb = bv.rearrange("p a (t h) -> p a t h", t=8)
            if fwd:
                copy(V, KK[:, a0:a0 + 2, 8:15, :], kb[:, :, 1:8, :], kk_pe)
                kz = kb[:, :, 0, :]
            else:
                copy(V, KK[:, a0:a0 + 2, 0:7, :], kb[:, :, 0:7, :], kk_pe)
                kz = kb[:, :, 7, :]
            bank_free[i] = tt(V, KK[:, a0:a0 + 2, 7, :], KK[:, a0:a0 + 2, 7, :], kz, ADD, V.t)
            dst = cl_d[:, d0 * 256:d0 * 256 + 2048].rearrange("p (d r x) -> p d r x", d=8, r=2)
            dma(G, dst[:, :, 0, :], clrv[:, :, oo:oo + 128], "cl", i_tok)
            cl_dma = dma(G, dst[:, :, 1, :], cliv[:, :, oo:oo + 128], "cl", i_tok)
            mod_step(2)
        for q in range(8):
            kk_dma = dma(G, toep_d[q].rearrange("a p x -> p a x"),
                         KK[:, :, 7 - q:15 - q, :].rearrange("p a j h -> p a (j h)"), "kk", V.t)
        mod_step(1000)
        cl_all, kk_all = cl_dma, kk_dma

        x_free = (kk_all, V.t)
        xv = reg(0, 4096).rearrange("p (t n) -> p t n", t=2)
        hT = reg(4096, 4096).rearrange("p (k n) -> p k n", k=16)
        qT = reg(8192, 4096).rearrange("p (k n) -> p k n", k=16)
        kT = reg(12288, 4096).rearrange("p (k n) -> p k n", k=16)
        vN = reg(16384, 4096).rearrange("p (t n) -> p t n", t=2)
        gN = reg(20480, 4096).rearrange("p (t n) -> p t n", t=2)
        bcA, bcB = reg(24576, 2048), reg(26624, 2048)
        distm = L1[:, 0:512].rearrange("p (t s) -> p t s", t=2)
        negm = L1[:, 512:1024].rearrange("p (t s) -> p t s", t=2)
        tri = L1[:, 1024:1536].rearrange("p (t s) -> p t s", t=2)
        phase0 = (V.t, P.t, S.t, G.t, cl_all, ms_all)
        x_tok = dma(SP, xv, A["x"][0].rearrange("(t p) n -> p t n", p=128), "x", *x_free)

        for t2 in range(2):
            G.do(lambda e, t2=t2: e.iota(distm[:, t2, :], pattern=[[-1, 256]], base=128 * t2, channel_multiplier=1,
                                         allow_small_or_imprecise_dtypes=True), *phase0)
            G.do(lambda e, t2=t2: e.affine_select(out=distm[:, t2, :], in_=distm[:, t2, :], compare_op=ALU.is_ge,
                                                  fill=1e33, base=128 * t2, pattern=[[-1, 256]],
                                                  channel_multiplier=1), G.t)
            G.do(lambda e, t2=t2: e.memset(negm[:, t2, :], 0.0))
            G.do(lambda e, t2=t2: e.affine_select(out=negm[:, t2, :], in_=negm[:, t2, :], compare_op=ALU.is_ge,
                                                  fill=-1e30, base=128 * t2, pattern=[[-1, 256]],
                                                  channel_multiplier=1), G.t)
            G.do(lambda e, t2=t2: e.memset(tri[:, t2, :], 1.0))
            G.do(lambda e, t2=t2: e.affine_select(out=tri[:, t2, :], in_=tri[:, t2, :], compare_op=ALU.is_ge,
                                                  fill=0.0, base=-128 * t2, pattern=[[1, 256]],
                                                  channel_multiplier=-1), G.t)
        mask_tok = G.t

        lam_t = sm[:, 0:512]
        for i_, n in enumerate(("a_lam_q1", "a_lam_k1", "a_lam_q2", "a_lam_k2")):
            lam_tok = dma(SP, sm[:, 128 * i_:128 * i_ + 128], A[n].to_broadcast([128, 128]), "lam", *phase0)
        sub_bc = sm[:, 512:768]
        sub_tok = dma(SP, sub_bc, A["a_subln_g"].to_broadcast([128, 256]), "sub", *phase0)
        tt(V, sm[:, 0:128], sm[:, 0:128], sm[:, 128:256], MUL, lam_tok)
        tt(V, sm[:, 256:384], sm[:, 256:384], sm[:, 384:512], MUL, lam_tok)
        ls = st[:, 100:104]
        V.do(lambda e: e.reduce_sum(ls[:, 0:1], sm[:, 0:128], AX), V.t)
        V.do(lambda e: e.reduce_sum(ls[:, 1:2], sm[:, 256:384], AX), V.t)
        t = act(ls[:, 2:4], ls[:, 0:2], ACT.Exp, V.t)
        nlam = st[:, 104:105]
        tt(V, nlam, ls[:, 3:4], ls[:, 2:3], SUB, t)
        ts(V, nlam, nlam, -LAM_INIT, None, ADD, None, V.t)
        ts(V, sub_bc, sub_bc, 1.0 - LAM_INIT, None, MUL, None, sub_tok)
        lam_ready = V.t

        def x_transposed(src, dst, acol_, bcol_, *w):
            for k2 in range(8):
                i, b, fr = bank(GA)
                for j in range(2):
                    for t2 in range(2):
                        k = 2 * k2 + j
                        t = tr(b[:, 256 * j + 128 * t2:256 * j + 128 * t2 + 128], src[:, t2, 128 * k:128 * k + 128],
                               fr, *w, inc=(j == 1 and t2 == 1))
                for j in range(2):
                    k = 2 * k2 + j
                    if k2 % 2 == 0:
                        tok = ts(V, dst[:, k, :], b[:, 256 * j:256 * j + 256], acol_[:, k:k + 1], bcol_[:, k:k + 1],
                                 MUL, ADD, t, *w)
                    else:
                        tok2 = act(dst[:, k, :], b[:, 256 * j:256 * j + 256], ACT.Identity, t, *w,
                                   scale=acol_[:, k:k + 1], bias=bcol_[:, k:k + 1])
                bank_free[i] = V.t if k2 % 2 == 0 else S.t
            return tok, tok2

        def plus1(dst, a, *w):
            return ts(V, dst, a, 1.0, None, ADD, None, *w)

        def dense_T(hin, npan, dst_fn, *w):
            for pnl in range(npan):
                i, wt, tok = take()
                bi, b, fr = bank(GA)
                P.wait(fr, *w)
                for j in range(2):
                    for k in range(KT):
                        t = mm(b[:, 256 * j:256 * j + 256], wt[:, k, 128 * j:128 * j + 128], hin[:, k, :],
                               k == 0, k == KT - 1, tok, inc=(j == 1 and k == KT - 1))
                release(i, t)
                bank_free[bi] = dst_fn(pnl, b[:, :].rearrange("p (j n) -> p j n", j=2), t)

        def dense_N(hin, npan, dst_fn, *w, kslots=1):
            for pnl in range(npan):
                bb = [bank(GB), bank(GC)] if kslots > 1 else [bank(GB), bank(GB)]
                for ks in range(kslots):
                    i, wt, tok = take()
                    for t2 in range(2):
                        bi, b, fr = bb[t2]
                        for k in range(KT):
                            t = mm(b[:, 0:256], hin[:, ks * KT + k, 128 * t2:128 * t2 + 128], wt[:, k, :],
                                   ks == 0 and k == 0, ks == kslots - 1 and k == KT - 1, tok, fr, *w,
                                   inc=(k == KT - 1))
                        if ks == kslots - 1:
                            bank_free[bi] = dst_fn(pnl, t2, b[:, 0:256], t)
                    release(i, t)

        def silu_panel(dst, ps, tk, ex, extra=None):
            t = act(ex, ps, ACT.Sigmoid, tk, V.t)
            if extra is not None:
                tt(V, ex, ex, extra, MUL, t)
                t = V.t
            return tt(V, dst, ps, ex, MUL, t)

        sc1 = st[:, 110:126]
        plus1(sc1, M("m0", 16), mod_tok["m0"])
        toks = x_transposed(xv, hT, sc1, M("m0", 0), x_tok, V.t, *phase0)

        def put_q(pnl, b, t):
            return S.do(lambda e: e.mul(qT[:, 2 * pnl:2 * pnl + 2, :], b, QK_SCALE), t)

        def put_k(pnl, b, t):
            return copy(V, kT[:, 2 * pnl:2 * pnl + 2, :], b, t)

        dense_T(hT, 8, put_q, *toks)
        q_tok = S.t
        dense_T(hT, 8, put_k, *toks)
        k_tok = V.t

        def put_v(pnl, t2, b, t):
            return copy(S, vN[:, t2, 256 * pnl:256 * pnl + 256], b, t)

        dense_N(hT, 8, put_v, *toks)
        v_tok = S.t
        exb = MSB[:, 0:256]

        def put_g(pnl, t2, b, t):
            return silu_panel(gN[:, t2, 256 * pnl:256 * pnl + 256], b, t, exb, sub_bc)

        V.wait(lam_ready)
        dense_N(hT, 8, put_g, *toks)
        g_tok = V.t
        h_dead = P.t

        oN = reg(4096, 4096).rearrange("p (t n) -> p t n", t=2)
        NBUF = 3
        wk = L2[:, 0:1536].rearrange("p (i x) -> p i x", i=NBUF)
        aT_ = MSB[:, 256:1792].rearrange("p (i x) -> p i x", i=6)
        stat = st[:, 128:176]
        ssq = st[:, 176:192]
        info = {}

        def items_a(i):
            return i // 2, i % 2

        def a_scores(i):
            h, t2 = items_a(i)
            w_ = 128 * (t2 + 1)
            bi, b, fr = bank(GA)
            for c in range(2):
                t = mm(b[:, 256 * c:256 * c + w_], qT[:, 2 * h + c, 128 * t2:128 * t2 + 128],
                       kT[:, 2 * h + c, 0:w_], True, True, fr, q_tok, k_tok, inc=(c == 1))
            info[i] = {"b": bi, "s": t}

        def a_soft(i):
            h, t2 = items_a(i)
            w_ = 128 * (t2 + 1)
            slope = 2.0 ** (-8.0 * (h + 1) / 8)
            n = info[i]
            b = banks[n["b"]]
            p = wk[:, i % NBUF, :].rearrange("p (c s) -> p c s", c=2)[:, :, 0:w_]
            sb_ = stat[:, 6 * (i % NBUF):6 * (i % NBUF) + 6]
            prev = info.get(i - NBUF, {})
            bv = b[:, :].rearrange("p (c s) -> p c s", c=2)[:, :, 0:w_]
            t = stt(p, distm[:, t2, 0:w_].unsqueeze(1).to_broadcast([128, 2, w_]), -slope, bv, MUL, ADD,
                    n["s"], mask_tok, prev.get("tr"), V.t)
            bank_free[n["b"]] = t
            V.do(lambda e: e.tensor_reduce(sb_[:, 0:2], p, AX, MAX, negate=True), V.t)
            mx = V.t
            for c in range(2):
                t = act(p[:, c, :], p[:, c, :], ACT.Exp, mx, bias=sb_[:, c:c + 1], accum_out=sb_[:, 2 + c:3 + c])
            n["e"] = S.t

        def a_mix(i):
            h, t2 = items_a(i)
            w_ = 128 * (t2 + 1)
            n = info[i]
            p = wk[:, i % NBUF, :].rearrange("p (c s) -> p c s", c=2)[:, :, 0:w_]
            sb_ = stat[:, 6 * (i % NBUF):6 * (i % NBUF) + 6]
            recip(sb_[:, 4:6], sb_[:, 2:4], n["e"])
            tt(V, sb_[:, 5:6], sb_[:, 5:6], nlam, MUL, V.t)
            ts(V, p[:, 0, :], p[:, 0, :], sb_[:, 4:5], None, MUL, None, V.t)
            n["a"] = stt(p[:, 0, :], p[:, 1, :], sb_[:, 5:6], p[:, 0, :], MUL, ADD, V.t)

        def a_turn(i):
            h, t2 = items_a(i)
            n = info[i]
            p = wk[:, i % NBUF, 0:256]
            bi, b, fr = bank(GB)
            for s in range(t2 + 1):
                t = tr(b[:, 128 * s:128 * s + 128], p[:, 128 * s:128 * s + 128], n["a"], fr, inc=(s == t2))
            n["tr"] = t
            w_ = 128 * (t2 + 1)
            bank_free[bi] = copy(V, aT_[:, i % NBUF * 2:i % NBUF * 2 + 2, :].rearrange("p a b -> p (a b)")[:, 0:w_],
                                 b[:, 0:w_], t, info.get(i - NBUF, {}).get("pv"))
            n["aT"] = bank_free[bi]

        def a_out(i):
            h, t2 = items_a(i)
            n = info[i]
            bi, b, fr = bank(GC)
            av = aT_[:, i % NBUF * 2:i % NBUF * 2 + 2, :].rearrange("p a b -> p (a b)")
            for s in range(t2 + 1):
                t = mm(b[:, 0:256], av[:, 128 * s:128 * s + 128], vN[:, s, 256 * h:256 * h + 256],
                       s == 0, s == t2, n["aT"], fr, v_tok, inc=(s == t2))
            n["pv"] = t
            o = oN[:, t2, 256 * h:256 * h + 256]
            c1 = copy(S, o, b[:, 0:256], t, h_dead)
            act(MSB[:, 1792:2048], b[:, 0:256], ACT.Square, S.t, accum_out=ssq[:, 2 * h + t2:2 * h + t2 + 1])
            bank_free[bi] = S.t

        P.wait(V.t)
        pipeline(16, [a_scores, a_soft, a_mix, a_turn, a_out])
        ts(V, ssq, ssq, 1.0 / 256, 1e-5, MUL, ADD, S.t)
        rs = st[:, 192:208]
        rsqrt(rs, ssq, st[:, 208:224], V.t)
        for h in range(8):
            for t2 in range(2):
                o = oN[:, t2, 256 * h:256 * h + 256]
                stt(o, o, rs[:, 2 * h + t2:2 * h + t2 + 1], gN[:, t2, 256 * h:256 * h + 256], MUL, MUL, V.t, g_tok)

        def to_T(src, dst, *w):
            for k2 in range(8):
                i, b, fr = bank(GA)
                for j in range(2):
                    for t2 in range(2):
                        k = 2 * k2 + j
                        t = tr(b[:, 256 * j + 128 * t2:256 * j + 128 * t2 + 128], src[:, t2, 128 * k:128 * k + 128],
                               fr, *w, inc=(j == 1 and t2 == 1))
                q_ = V if k2 % 2 else S
                bank_free[i] = copy(q_, dst[:, 2 * k2:2 * k2 + 2, :], b[:, :].rearrange("p (j n) -> p j n", j=2),
                                    t, *w)
            return V.t, S.t

        oT = qT
        toks = to_T(oN, oT, V.t, P.t)

        def residual(toks, gate, gdone):
            def put(pnl, t2, b, t):
                cs = slice(256 * pnl, 256 * pnl + 256)
                tmp_ = MSB[:, 256 * t2:256 * t2 + 256]
                r = tt(V, tmp_, b, bcA[:, cs], MUL, t, gdone, V.t)
                stt(xv[:, t2, cs], xv[:, t2, cs], ALPHA, tmp_, MUL, ADD, V.t)
                return r
            dense_N(oT, 8, put, *toks)
            return V.t

        def layer_norm(l, *w):
            lg = dma(G, bcA, A["ln_g"][l:l + 1, :].to_broadcast([128, 2048]), "bc0", *w)
            lb = dma(G, bcB, A["ln_b"][l:l + 1, :].to_broadcast([128, 2048]), "bc1", *w)
            bs = MSB[:, 512:560].rearrange("p (t c s) -> p t c s", t=2, c=4)
            mv = st[:, 0:4].rearrange("p (t s) -> p t s", t=2)
            for t2 in range(2):
                for c in range(4):
                    V.do(lambda e, t2=t2, c=c: e.bn_stats(bs[:, t2, c, :], xv[:, t2, 512 * c:512 * c + 512]), V.t)
                V.do(lambda e, t2=t2: e.bn_aggr(mv[:, t2, :], bs[:, t2, :, :].rearrange("p c s -> p (c s)")), V.t)
            ts(V, st[:, 4:6], mv[:, :, 1], 1e-5, None, ADD, None, V.t)
            rsqrt(st[:, 6:8], st[:, 4:6], st[:, 8:10], V.t)
            for t2 in range(2):
                for hf in range(2):
                    cs = slice(1024 * hf, 1024 * hf + 1024)
                    ts(V, xv[:, t2, cs], xv[:, t2, cs], mv[:, t2, 0:1], st[:, 6 + t2:7 + t2], SUB, MUL, V.t)
                    tt(V, xv[:, t2, cs], xv[:, t2, cs], bcA[:, cs], MUL, V.t, lg)
                    tt(V, xv[:, t2, cs], xv[:, t2, cs], bcB[:, cs], ADD, V.t, lb)
            return V.t

        gb = bcast(bcA, M("m0", 32), mod_tok["m0"], *phase0)
        residual(toks, bcA, gb)
        xt = layer_norm(0, V.t)

        hkT = vN_ = None
        h1 = hT
        sc2 = st[:, 110:126]
        plus1(sc2, M("m1", 16), xt, P.t)
        toks = x_transposed(xv, h1, sc2, M("m1", 0), V.t, P.t)
        dense_T(h1, 8, put_q, *toks)
        q_tok = S.t

        def put_g2(pnl, t2, b, t):
            return silu_panel(gN[:, t2, 256 * pnl:256 * pnl + 256], b, t, exb)

        dense_N(h1, 8, put_g2, *toks)
        g_tok = V.t
        plus1(sc2, M("kv", 16), V.t, P.t, S.t)
        toks = x_transposed(xv, h1, sc2, M("kv", 0), V.t, P.t)
        dense_T(h1, 8, put_k, *toks)
        k_tok = V.t
        dense_N(h1, 8, put_v, *toks)
        v_tok = S.t
        zw = sm[:, 768:1024].rearrange("p (k n) -> p k n", k=16)
        bf = sm[:, 1024:1040]
        zf_tok = dma(SP, zw, A["kv_w"][:, 4096:4112].rearrange("(k p) n -> p k n", p=128), "zf", *phase0)
        zf_tok = dma(SP, bf, A["kv_b_f"].rearrange("(a n) -> a n", a=1).to_broadcast([128, 16]), "zf")
        lf = sm[:, 1056:1088].rearrange("p (t h) -> p t h", t=2)
        tz = sm[:, 1088:1120].rearrange("p (t h) -> p t h", t=2)
        bi, b, fr = bank(GA)
        for t2 in range(2):
            for k in range(KT):
                t = mm(b[:, 16 * t2:16 * t2 + 16], h1[:, k, 128 * t2:128 * t2 + 128], zw[:, k, :], k == 0, k == KT - 1,
                       fr, zf_tok, *toks, inc=(t2 == 1 and k == KT - 1))
        bz = b[:, 0:32].rearrange("p (t h) -> p t h", t=2)
        zz = sm[:, 1120:1152].rearrange("p (t h) -> p t h", t=2)
        bank_free[bi] = tt(V, zz, bz, bf.unsqueeze(1).to_broadcast([128, 2, 16]), ADD, t, zf_tok)
        ts(V, tz, zz, -1.0, None, MUL, None, V.t)
        tt(V, tz, tz, zz, MIN, V.t)
        t = act(tz, tz, ACT.Exp, V.t)
        t = act(tz, tz, ACT.Ln, t, bias=1.0)
        ts(V, lf, zz, 0.0, None, MIN, None, V.t)
        tt(V, lf, lf, tz, SUB, V.t, t)
        FT = sm[:, 1152:1408]
        nFT = sm[:, 1408:1664]
        bi, b, fr = bank(GA)
        for s in range(2):
            t = mm(b[0:16, 0:256], lf[:, s, :], tri[:, s, :], s == 0, s == 1, V.t, fr, mask_tok, inc=(s == 1))
        copy(V, FT[0:16, :], b[0:16, 0:256], t)
        bank_free[bi] = ts(V, nFT[0:16, :], b[0:16, 0:256], -1.0, None, MUL, None, t)
        f_tok = V.t
        h_dead = P.t
        info.clear()
        wk2 = L2[:, 0:1024].rearrange("p (i x) -> p i x", i=4)
        stat2 = st[:, 128:144]

        def f_scores(i):
            h, t2 = i // 2, i % 2
            w_ = 128 * (t2 + 1)
            bi, b, fr = bank(GA)
            sel = ident[0:16, h:h + 1]
            mm(b[:, 0:w_], qT[:, h, 128 * t2:128 * t2 + 128], kT[:, h, 0:w_], True, False, fr, q_tok, k_tok, f_tok)
            mm(b[:, 0:w_], FT[0:16, 128 * t2:128 * t2 + 128], sel.to_broadcast([16, w_]), False, False)
            t = mm(b[:, 0:w_], sel.to_broadcast([16, 128]), nFT[0:16, 0:w_], False, True, inc=True)
            info[i] = {"b": bi, "s": t}

        def f_soft(i):
            h, t2 = i // 2, i % 2
            w_ = 128 * (t2 + 1)
            n = info[i]
            p = wk2[:, i % 4, 0:w_]
            s_ = stat2[:, 4 * (i % 4):4 * (i % 4) + 4]
            bank_free[n["b"]] = tt(V, p, banks[n["b"]][:, 0:w_], negm[:, t2, 0:w_], ADD, n["s"], mask_tok,
                                   info.get(i - 4, {}).get("tr"), V.t)
            V.do(lambda e: e.tensor_reduce(s_[:, 0:1], p, AX, MAX, negate=True), V.t, info.get(i - 4, {}).get("o"))
            act(p, p, ACT.Exp, V.t, bias=s_[:, 0:1], accum_out=s_[:, 1:2])
            n["e"] = S.t

        def f_turn(i):
            h, t2 = i // 2, i % 2
            w_ = 128 * (t2 + 1)
            n = info[i]
            p = wk2[:, i % 4, 0:w_]
            bi, b, fr = bank(GB)
            for s in range(t2 + 1):
                t = tr(b[:, 128 * s:128 * s + 128], p[:, 128 * s:128 * s + 128], n["e"], fr, inc=(s == t2))
            n["tr"] = t
            bank_free[bi] = copy(S, aT_[:, i % 3 * 2:i % 3 * 2 + 2, :].rearrange("p a b -> p (a b)")[:, 0:w_],
                                 b[:, 0:w_], t, info.get(i - 3, {}).get("pv"))
            n["aT"] = bank_free[bi]

        def f_out(i):
            h, t2 = i // 2, i % 2
            n = info[i]
            bi, b, fr = bank(GC)
            av = aT_[:, i % 3 * 2:i % 3 * 2 + 2, :].rearrange("p a b -> p (a b)")
            for s in range(t2 + 1):
                t = mm(b[:, 0:128], av[:, 128 * s:128 * s + 128], vN[:, s, 128 * h:128 * h + 128],
                       s == 0, s == t2, n["aT"], fr, v_tok, inc=(s == t2))
            n["pv"] = t
            s_ = stat2[:, 4 * (i % 4):4 * (i % 4) + 4]
            recip(s_[:, 2:3], s_[:, 1:2], n["e"])
            cs = slice(128 * h, 128 * h + 128)
            bank_free[bi] = stt(oN[:, t2, cs], b[:, 0:128], s_[:, 2:3], gN[:, t2, cs], MUL, MUL, V.t, t, h_dead, g_tok)
            n["o"] = V.t

        pipeline(32, [f_scores, f_soft, f_turn, f_out])
        toks = to_T(oN, oT, V.t, P.t)
        gb = bcast(bcA, M("m1", 32), mod_tok["m1"], V.t)
        residual(toks, bcA, gb)
        xt = layer_norm(1, V.t)

        everything = (V.t, P.t, S.t, G.t)

        def load_cl(n):
            i = ring_state["n"] % NSLOT
            ring_state["n"] += 1
            t_ = ring[:, i * SLOTF:(i + 1) * SLOTF]
            dma(SP, t_[:, 0:2048], cl_d[:, n * 2048:(n + 1) * 2048], f"ring{i}", slot_free[i])
            tok = dma(SP, t_[:, 2048:4096], cl_d[:, 16384 + n * 2048:16384 + (n + 1) * 2048], f"ring{i}")
            return i, t_.rearrange("p (b d r x) -> p b d r x", b=2, d=8, r=2), tok

        def load_toep(n):
            i = ring_state["n"] % NSLOT
            ring_state["n"] += 1
            t_ = ring[:, i * SLOTF:i * SLOTF + 2048].rearrange("p (g x) -> p g x", x=128)
            for qq in range(8):
                src = toep_d[qq].rearrange("a (b h) x -> h (a b) x", h=16)[:, 16 * n:16 * n + 16, :]
                tok = dma(SP, t_[16 * qq:16 * qq + 16, :, :], src, f"ring{i}", slot_free[i])
            return i, t_, tok

        wg = A["s5_w_glu_2"][0]

        def load_glu(n0):
            i = ring_state["n"] % NSLOT
            ring_state["n"] += 1
            t_ = ring[:, i * SLOTF:(i + 1) * SLOTF].rearrange("p (k n) -> p k n", k=16)
            src = wg[:, n0:n0 + 256].rearrange("(k g t h) n -> g t h k n", g=8, t=2, h=16)
            for gg in range(8):
                for g2 in range(2):
                    d_ = t_[16 * gg:16 * gg + 16, :, :].rearrange("p (k t) n -> p t k n", t=2)[:, g2]
                    tok = dma(SP, d_, src[gg, g2], f"ring{i}", slot_free[i])
            return i, t_, tok

        SP.wait(ms_all, cl_all, kk_all)
        for n in range(8):
            plan.append(lambda n=n: load(m_state_d[:, n * 4096:(n + 1) * 4096]))
        for n in range(8):
            plan.append(lambda n=n: load_cl(n))
            plan.append(lambda n=n: load_toep(n))
        for n in range(0, 4096, 256):
            plan.append(lambda n=n: load_glu(n))
        panels(A["w_mlp_in_2"][0], 0, 0, 8192)
        for n in range(0, 2048, 256):
            for ks in range(4):
                plan.append(lambda n=n, ks=ks: load_w(A["w_mlp_out_2"][0], 2048 * ks, n))
        ahead()

        hcL = reg(4096, 4096).rearrange("p (q n) -> p q n", q=8)
        abc, bbc = reg(8192, 2048), reg(10240, 2048)
        UL = LT[:, 0:4096].rearrange("p (g c) -> p g c", c=32)
        VL = reg(20480, 8192).rearrange("p (k r d) -> p k r d", k=32, r=2)
        hL = reg(12288, 4096).rearrange("p (t n) -> p t n", t=2)
        a1 = bcast(abc, acol2, *everything)
        a2 = bcast(bbc, M("m2", 0), *everything)
        rt = rms_stat(xv, reg(16384, 2048), 0, 1e-6, *everything)
        hc2L = reg(16384, 4096).rearrange("p (g q h) -> p g q h", g=32, q=8)
        u_tok = make_u(xv, hL, 0, abc, bbc, hcL, hc2L, UL, lambda: None, a1, a2, rt, *everything)
        u_read = (V.t, P.t, u_tok)
        for sl in range(8):
            i, wt, tok = take()
            mv = wt.rearrange("p (d r m) -> p d r m", d=16, r=2)
            for hf in range(2):
                t, vt = v_matmuls(mv[:, 8 * hf:8 * hf + 8], UL, 16 * sl + 8 * hf, 8, VL, tok, u_tok)
            release(i, t)
        Sb = reg(4096, 16384).rearrange("p (r d g c) -> p r d g c", r=2, d=128, g=2)
        G.do(lambda e: e.memset(Sb[0:64, :, :, 1, :], 0.0), u_read)
        z0 = G.do(lambda e: e.memset(Sb[64:128, :, :, 0, :], 0.0))
        cur, nxt = stA, stB
        saved = None
        for k in range(32):
            for g2 in range(2):
                pp = slice(64 * g2, 64 * g2 + 64)
                c3 = l_swap(cur[pp, :])
                copy(S, Sb[pp, :, 0:64, g2, k], c3[:, :, 0:64], V.t, u_read)
                copy(S, Sb[pp, :, 64:128, g2, 31 - k], c3[:, :, 64:128])
            if k < 31:
                chunk_step(cur, nxt, VL[:, k].rearrange("p r d -> p (r d)"), vt, saved)
            saved = S.t
            cur, nxt = nxt, cur
        s_tok, scan_done = S.t, V.t
        Y = reg(20480, 8192).rearrange("p (k q g h) -> p k q g h", k=8, q=8, g=8)
        for q in range(8):
            i1, cl, tok1 = take()
            i2, wt, tok2 = take()
            for g4 in range(2):
                bi, b, fr = bank(GA)
                for j in range(4):
                    gg = 4 * g4 + j
                    gp = 8 * q + gg
                    o = b[0:64, 128 * j:128 * j + 128]
                    for d_ in range(2):
                        for r_ in range(2):
                            mm(o, Sb[:, r_, 64 * d_ + gp, :, :].rearrange("p g c -> p (g c)"), cl[:, d_, gg, r_, :],
                               d_ == 0 and r_ == 0, False, tok1, fr, s_tok, z0)
                    for g2 in range(2):
                        t = mm(b[32 * g2:32 * g2 + 32, 128 * j:128 * j + 128], UL[:, 2 * gp + g2, :],
                               wt[:, 2 * gg + g2, :], False, True, tok2, inc=(j == 3 and g2 == 1))
                bank_free[bi] = copy(V if g4 % 2 else S,
                                     Y[0:64, q, :, 4 * g4:4 * g4 + 4, :].rearrange("p q g h -> p g q h"),
                                     b[0:64, :].rearrange("p (g q h) -> p g q h", g=4, q=8), t, scan_done)
            release(i1, t)
            release(i2, t)
        y_tok = (V.t, S.t, P.t)
        zT = reg(4096, 4096).rearrange("p (k n) -> p k n", k=16)
        for k8 in range(8):
            bi, b, fr = bank(GA)
            for q in range(8):
                t = tr(b[:, 64 * q:64 * q + 64], Y[0:64, k8, q, :, :].rearrange("p g h -> p (g h)"), fr, y_tok, inc=(q == 7), k=64)
            bv = b[:, :].rearrange("p (q g c) -> p q g c", q=8, g=2)
            ends = []
            for g2 in range(2):
                ends.append(copy(S if k8 % 2 else V, zT[:, 2 * k8 + g2, :].rearrange("p (c q) -> p q c", q=8), bv[:, :, g2, :],
                                 t, y_tok))
            bank_free[bi] = tuple(ends)
        z_tok = (V.t, S.t, P.t)
        for q in range(4):
            z = reg(4096 + 1024 * q, 1024)
            e_ = reg(8192 + 1024 * q, 1024)
            tt(V, e_, z, z, MUL, z_tok)
            ts(V, e_, e_, 0.044715, 1.0, MUL, ADD, V.t)
            tt(V, e_, e_, z, MUL, V.t)
            t = act(e_, e_, ACT.Sigmoid, V.t, scale=2.0 * GELU_C)
            tt(V, z, z, e_, MUL, t)
        gelu_tok = V.t
        aN = reg(12288, 4096).rearrange("p (t n) -> p t n", t=2)

        def put_a(pnl, t2, b, t):
            return copy(S, aN[:, t2, 256 * pnl:256 * pnl + 256], b, t, z_tok)

        dense_N(zT, 8, put_a, gelu_tok)
        a_tok = S.t

        def put_mix(pnl, t2, b, t):
            t = act(exb, b, ACT.Sigmoid, t, V.t)
            o = aN[:, t2, 256 * pnl:256 * pnl + 256]
            tt(V, o, o, exb, MUL, t, a_tok)
            return t

        dense_N(zT, 8, put_mix, gelu_tok)
        pcol = st[:, 64:80]
        tt(V, pcol, M("m2", 32), C("npost"), MUL, V.t)
        gb = bcast(bcA, pcol, V.t, z_tok)
        rt = rms_stat(aN, reg(16384, 2048), 0, 1e-6, V.t)
        tmpN = reg(4096, 4096).rearrange("p (t n) -> p t n", t=2)
        glu_read = P.t
        for t2 in range(2):
            for hf in range(2):
                cs = slice(1024 * hf, 1024 * hf + 1024)
                stt(tmpN[:, t2, cs], aN[:, t2, cs], st[:, t2:t2 + 1], bcA[:, cs], MUL, MUL, rt, gb, glu_read)
                tt(V, xv[:, t2, cs], xv[:, t2, cs], tmpN[:, t2, cs], ADD, V.t)
        rt = rms_stat(xv, reg(16384, 2048), 0, 1e-6, V.t)
        for t2 in range(2):
            ts(V, tmpN[:, t2, :], xv[:, t2, :], st[:, t2:t2 + 1], None, MUL, None, rt)
        stt(pcol, M("m2", 64), 1.0, C("mpre"), ADD, MUL, P.t, V.t)
        h2T = reg(20480, 4096).rearrange("p (k n) -> p k n", k=16)
        toks = x_transposed(tmpN, h2T, pcol, M("m2", 48), V.t)
        hid = reg(4096, 16384).rearrange("p (k n) -> p k n", k=64)
        dead = (P.t, V.t, S.t)

        def put_h(pnl, b, t):
            o = hid[:, 2 * pnl:2 * pnl + 2, :]
            r = act(o, b, ACT.Relu, t, dead)
            tt(G, o, o, o, MUL, r)
            return r

        dense_T(h2T, 32, put_h, *toks)
        pcol2 = st[:, 80:96]
        tt(V, pcol2, M("m2", 80), C("mpost"), MUL)
        gb = bcast(bcA, pcol2, V.t, rt)
        yN = reg(20480, 4096).rearrange("p (t n) -> p t n", t=2)
        h2_read = P.t

        def put_y(pnl, t2, b, t):
            return copy(V if t2 else S, yN[:, t2, 256 * pnl:256 * pnl + 256], b, t, h2_read)

        dense_N(hid, 8, put_y, G.t, kslots=4)
        rt = rms_stat(yN, reg(26624, 2048), 0, 1e-6, V.t, S.t)
        out_v = out[0].rearrange("(t p) n -> p t n", p=128)
        for t2 in range(2):
            stt(yN[:, t2, :], yN[:, t2, :], st[:, t2:t2 + 1], bcA, MUL, MUL, rt, gb)
            o_t = tt(V, xv[:, t2, :], xv[:, t2, :], yN[:, t2, :], ADD, V.t)
            o_tok = dma(SP, out_v[:, t2, :], xv[:, t2, :], "out", o_t)
        SP.wait(o_tok, V.t, S.t, P.t, G.t)

        assert not plan and not loaded
        block = ctx.enter_context(nc.Block())

        @block.sync
        def _(e):
            SP.run(e)

        @block.gpsimd
        def _(e):
            G.run(e)

        @block.scalar
        def _(e):
            S.run(e)

        @block.vector
        def _(e):
            V.run(e)

        @block.tensor
        def _(e):
            P.run(e)


_INS = ["x", "c", "w_mod", "b_mod", "ln_g", "ln_b", "a_w_in", "a_w_out", "a_lam_q1", "a_lam_k1", "a_lam_q2",
        "a_lam_k2", "a_subln_g", "kv_w_mod", "kv_b_mod", "kv_w", "kv_b_f", "b_w_in", "b_w_out", "c_2", "ctx_2",
        "c_ctx_2", "w_mod_2", "b_mod_2", "norm_mix_pre_2", "norm_mix_post_2", "norm_mlp_pre_2", "norm_mlp_post_2",
        "w_mlp_in_2", "w_mlp_out_2", "s5_a_re_2", "s5_a_im_2", "s5_log_dt_2", "s5_b_re_2", "s5_b_im_2",
        "s5_c_re_2", "s5_c_im_2", "s5_d_2", "s5_w_glu_2"]


def kernel(**inputs):
    import numpy as _np
    import concourse.bacc as _bacc
    from concourse.bass_utils import run_bass_kernel_spmd as _run

    nc = _bacc.Bacc("TRN2", target_bir_lowering=False, num_devices=1)
    arrays, args = {}, {}
    for name in _INS:
        a = _np.ascontiguousarray(inputs[name])
        arrays[f"in_{name}"] = a
        args[name] = nc.dram_tensor(f"in_{name}", a.shape, mybir.dt.from_np(a.dtype), kind="ExternalInput").ap()
    out = nc.dram_tensor("out_0", (1, 256, 2048), F32, kind="ExternalOutput").ap()
    build(nc, args, out)
    r = _run(nc, [arrays], core_ids=[0])
    return r.results[0]["out_0"]
```

```python
import math
from contextlib import ExitStack

import concourse.bass as bass
from concourse import mybir

F32 = mybir.dt.float32
ALU = mybir.AluOpType
ACT = mybir.ActivationFunctionType
AX = mybir.AxisListType.X
MUL, ADD, SUB, MAX, MIN = ALU.mult, ALU.add, ALU.subtract, ALU.max, ALU.min

D = 2048
KT = 16
ALPHA = 4.0 ** 0.25
LAM_INIT = 0.8 - 0.6 * math.exp(-0.3 * 0)
QK_SCALE = 128.0 ** -0.5
GELU_C = math.sqrt(2.0 / math.pi)
NSLOT = 3
SLOTF = 4096
DOUBLINGS = 10


class Queue:

    def __init__(self, sem):
        self.sem, self.n, self.items, self.seen = sem, 0, [], {}

    def wait(self, *tokens):
        for tok in tokens:
            if tok is None:
                continue
            if not isinstance(tok[-1], int):
                self.wait(*tok)
                continue
            sem, val = tok
            if self.seen.get(id(sem), 0) < val:
                self.seen[id(sem)] = val
                self.items.append(lambda e, s=sem, v=val: e.wait_ge(s, v))

    def do(self, fn, *tokens, inc=True):
        self.wait(*tokens)
        if inc:
            self.n += 1
            self.items.append(lambda e, f=fn: f(e).then_inc(self.sem, 1))
        else:
            self.items.append(fn)
        return (self.sem, self.n)

    @property
    def t(self):
        return (self.sem, self.n)

    def run(self, e):
        for f in self.items:
            f(e)


def pipeline(n, stages):
    for t in range(n + len(stages) - 1):
        for s in range(len(stages) - 1, -1, -1):
            if 0 <= t - s < n:
                stages[s](t - s)


def build(nc, A, out):
    with ExitStack() as ctx:
        sem = lambda name: ctx.enter_context(nc.semaphore(name))
        P, V, S, G = (Queue(sem(n)) for n in ("s_pe", "s_dve", "s_act", "s_pool"))
        SP = Queue(sem("s_sp"))

        dma_count = {}

        def dma(q, dst, src, s, *tokens):
            q.wait(*tokens)
            dma_count[s] = dma_count.get(s, 0) + 16
            q.items.append(lambda e: e.dma_start(dst, src).then_inc(sems[s], 16))
            return (sems[s], dma_count[s])

        sems = {n: sem("d_" + n) for n in (
            ["rows", "x", "ctx", "lam", "sub", "b", "c", "ar", "ai", "dt", "hc", "ms", "cl", "kk", "out", "bc0", "bc1", "zf", "qkv", "sd"]
            + [f"st{i}" for i in range(4)] + ["at0", "at1", "at3", "p0", "p1", "p2"]
            + [f"ring{i}" for i in range(NSLOT)])}

        sb = lambda name, n: ctx.enter_context(nc.sbuf_tensor(name, [128, n], F32))
        ring = sb("ring", NSLOT * SLOTF)
        AR = sb("arena", 28672)
        LT = sb("LT", 2 * 128 * 17)
        L1, L2 = LT[:, 0:2304], LT[:, 2304:4352]
        MSB = sb("MSB", 2048)
        BBD = sb("BBD", 512)
        sm = sb("sm", 16 * 128)
        ident = sb("ident", 128)
        cols = sb("cols", 512)
        MODC = sb("MODC", 416)
        SF = sb("SF", 256 * 2)
        LR8 = sb("LR8", 256)
        LS8 = sb("LS8", 256)
        st = sb("st", 256)
        ACC = sb("ACC", 512)
        SUBG = sb("SUBG", 256)
        banks = [ctx.enter_context(nc.psum_tensor(f"bank{i}", [128, 512], F32)) for i in range(8)]

        m_state_d = nc.dram_tensor("m_state", [128, 128 * 256], F32).ap()
        cl_d = nc.dram_tensor("cl_out", [128, 128 * 256], F32).ap()
        proj_d = [nc.dram_tensor(f"proj{i}", [128, 4096], F32).ap() for i in range(4)]
        toep_d = nc.dram_tensor("toep", [8, 16, 128, 128], F32).ap()

        def reg(off, n):
            return AR[:, off:off + n]

        ring_state = {"n": 0}
        slot_free = [None] * NSLOT

        def load(src, dst=None):
            i = ring_state["n"] % NSLOT
            ring_state["n"] += 1
            n = 1
            for d_ in src.shape[1:]:
                n *= d_
            t = ring[:, i * SLOTF:i * SLOTF + n]
            if len(src.shape) == 3:
                tv = t.rearrange("p (a b) -> p a b", a=src.shape[1])
            else:
                tv = t
            tok = dma(SP, tv, src, f"ring{i}", slot_free[i])
            return i, tv, tok

        def load_w(W, k0, n0, n=256):
            return load(W[k0:k0 + 2048, n0:n0 + n].rearrange("(k p) n -> p k n", p=128))

        def take(fn):
            return fn()

        def release(i, tok):
            slot_free[i] = tok

        bank_free = [None] * 8
        turn = {}

        def bank(group):
            k = turn.get(group, 0)
            turn[group] = k + 1
            i = group[k % len(group)]
            return i, banks[i], bank_free[i]

        GA = (0, 1, 2)
        GB = (3, 4)
        GC = (5, 6)

        def mm(o, l, r, start, stop, *w, inc=False):
            return P.do(lambda e: e.matmul(o, l, r, start=start, stop=stop, skip_group_check=True), *w, inc=inc)

        def tr(o, i, *w, inc=False, k=128):
            idn = ident[0:k, 0:k]
            return P.do(lambda e: e.transpose(o, i, idn), *w, inc=inc)

        def tt(q, o, a, b, op, *w):
            return q.do(lambda e: e.tensor_tensor(o, a, b, op), *w)

        def ts(q, o, a, s1, s2, o1, o2, *w):
            if s2 is None:
                return q.do(lambda e: e.tensor_scalar(o, a, s1, None, o1), *w)
            return q.do(lambda e: e.tensor_scalar(o, a, s1, s2, o1, o2), *w)

        def stt(o, a, s, b, o1, o2, *w):
            return V.do(lambda e: e.scalar_tensor_tensor(out=o, in0=a, scalar=s, in1=b, op0=o1, op1=o2), *w)

        def act(o, i, f, *w, **kw):
            return S.do(lambda e: e.activation(o, i, f, **kw), *w)

        def recip(o, a, *w):
            return V.do(lambda e: e.reciprocal(o, a), *w)

        def copy(q, o, a, *w):
            if q is S:
                return S.do(lambda e: e.copy(o, a), *w)
            return q.do(lambda e: e.tensor_copy(o, a), *w)

        def rsqrt(o, v, tmp, *w):
            a = act(tmp, v, ACT.Ln, *w)
            b = act(o, tmp, ACT.Exp, a, scale=-0.5)
            tt(V, tmp, o, o, MUL, b)
            tt(V, tmp, tmp, v, MUL, V.t)
            ts(V, tmp, tmp, -0.5, 1.5, MUL, ADD, V.t)
            return tt(V, o, o, tmp, MUL, V.t)

        G.do(lambda e: e.memset(ident[:, :], 0.0))
        id_tok = G.do(lambda e: e.affine_select(out=ident[:, :], in_=ident[:, :], compare_op=ALU.not_equal, fill=1.0,
                                                base=0, pattern=[[-1, 128]], channel_multiplier=1), G.t)

        vecs = [("c", A["c"].rearrange("a (r n) -> (a r) n", n=128), 16),
                ("c2", A["c_2"].rearrange("a (r n) -> (a r) n", n=128), 16),
                ("cc", A["c_ctx_2"].rearrange("(r n) -> r n", n=128), 16),
                ("bm", A["b_mod"].rearrange("l (r n) -> (l r) n", n=128), 96),
                ("bkv", A["kv_b_mod"].rearrange("(r n) -> r n", n=128), 32),
                ("bm2", A["b_mod_2"].rearrange("l (r n) -> (l r) n", n=128), 96),
                ("npre", A["norm_mix_pre_2"].rearrange("l (r n) -> (l r) n", n=128), 16),
                ("npost", A["norm_mix_post_2"].rearrange("l (r n) -> (l r) n", n=128), 16),
                ("mpre", A["norm_mlp_pre_2"].rearrange("l (r n) -> (l r) n", n=128), 16),
                ("mpost", A["norm_mlp_post_2"].rearrange("l (r n) -> (l r) n", n=128), 16)]
        col = {}
        pos = 0
        rows_base = 0
        for name, src, n in vecs:
            col[name] = pos
            r = 0
            while r < n:
                tile, p0 = (pos + r) // 128, (pos + r) % 128
                m = min(n - r, 128 - p0)
                rows_tok = dma(SP, reg(rows_base + tile * 128, 128)[p0:p0 + m, :], src[r:r + m, :], "rows")
                r += m
            pos += n
        col["sd"] = pos
        sd_src = A["s5_d_2"][0].rearrange("(g a m h) -> g a m h", g=2, a=16, m=4)
        tile, p0 = pos // 128, pos % 128
        assert p0 + 16 <= 128
        for g2 in range(2):
            sd_dst = reg(rows_base + tile * 128, 128)[p0:p0 + 16, :].rearrange("p (m g h) -> p m g h", m=4, g=2)
            rows_tok = dma(SP, sd_dst[:, :, g2, :], sd_src[g2], "rows")
        pos += 16
        ncol = pos
        for tile in range((ncol + 127) // 128):
            m = min(128, ncol - tile * 128)
            i, b, fr = bank(GA)
            t = tr(b[:, 0:m], reg(rows_base + tile * 128, 128)[0:m, :], rows_tok, id_tok, fr, inc=True, k=m)
            bank_free[i] = copy(V, cols[:, tile * 128:tile * 128 + m], b[:, 0:m], t)
        rows_read = P.t

        def C(name, a=0, n=16):
            return cols[:, col[name] + a:col[name] + a + n]

        cact = sm[:, 15 * 128:15 * 128 + 48]
        tmp = sm[:, 15 * 128 + 48:15 * 128 + 96]
        ts(V, tmp, C("c", 0, 48), -80.0, None, MAX, None, V.t)
        t = act(tmp, tmp, ACT.Exp, V.t, scale=-1.0)
        ts(V, tmp, tmp, 1.0, None, ADD, None, t)
        recip(tmp, tmp, V.t)
        cact_tok = tt(V, cact, tmp, C("c", 0, 48), MUL, V.t)
        cpair = cact[:, 16:48].rearrange("p (v k) -> p k v", v=2)

        MB0 = banks[7]
        m_off = {"m2": 0, "m2x": 96, "m0": 128, "kv": 176, "m1": 208}
        mod_tok = {}
        ones = sm[:, 14 * 128:14 * 128 + 1]
        ones_tok = V.do(lambda e: e.memset(ones, 1.0))
        acc_free = [None, None]
        wm, wm2 = A["w_mod"], A["w_mod_2"][0]
        groups = [("m0s", wm[0], "m0", 0, 32, "bm", 0), ("m2a", wm2, "m2", 0, 32, "bm2", 0),
                  ("m0g", wm[0], "m0", 32, 48, "bm", 0), ("m1", wm[1], "m1", 0, 48, "bm", 48),
                  ("kv", A["kv_w_mod"], "kv", 0, 32, "bkv", 0), ("m2b", wm2, "m2", 32, 80, "bm2", 0),
                  ("m2c", wm2, "m2", 80, 96, "bm2", 0)]
        jobs = [(g, nt) for g in groups for nt in range(g[3], g[4], 2)]

        def mod(n=1, dve=False):
            for _ in range(n):
                mod_sums()
                if not jobs:
                    return
                (name, W, dst, nt0, nt1, bias, boff), nt = jobs.pop(0)
                base = m_off[dst]
                c0 = 0 if dst in ("m0", "m1") or dst == "kv" else 16
                i, w, tok = take(lambda: load_w(W, 0, 128 * nt))
                if name != "m2a" and dve:
                    h = mod.turn % 2
                    mod.turn += 1
                    a = ACC[:, 256 * h:256 * h + 256]
                    ts(V, a, w[:, 0, :], cact[:, c0:c0 + 1], None, MUL, None, tok, acc_free[h], cact_tok)
                    for k in range(1, KT):
                        stt(a, w[:, k, :], cact[:, c0 + k:c0 + k + 1], a, MUL, ADD, V.t)
                    release(i, V.t)
                    mod.pending.append((h, a, base + nt, V.t))
                else:
                    for j in range(2):
                        for k in range(KT):
                            if name == "m2a":
                                o, r = MB0[:, 256 + 2 * (nt + j):258 + 2 * (nt + j)], cpair[:, k, :]
                            else:
                                o, r = MB0[:, base + nt + j:base + nt + j + 1], cact[:, c0 + k:c0 + k + 1]
                            t = mm(o, w[:, k, j * 128:(j + 1) * 128], r, k == 0, k == KT - 1, tok, cact_tok,
                                   inc=(j == 1 and k == KT - 1))
                    release(i, t)
                if nt + 2 == nt1:
                    mod_sums()
                    if name == "m2a":
                        pr = MB0[:, 256:320].rearrange("p (n v) -> p v n", v=2)
                        tt(V, MODC[:, 0:32], pr[:, 0, :], C(bias, 0, 32), ADD, P.t)
                        tt(V, MODC[:, 96:128], pr[:, 1, :], C(bias, 0, 32), ADD)
                    else:
                        tt(V, MODC[:, base + nt0:base + nt1], MB0[:, base + nt0:base + nt1],
                           C(bias, boff + nt0, nt1 - nt0), ADD, P.t)
                    mod_tok[name] = V.t
                    P.wait(V.t)

        mod.turn = 0
        mod.pending = []

        def mod_sums():
            for h, a, o, at in mod.pending:
                for j in range(2):
                    acc_free[h] = mm(MB0[:, o + j:o + j + 1], a[:, 128 * j:128 * j + 128], ones, True, True, at,
                                     ones_tok, inc=True)
            mod.pending = []


        def mod_until(name, **kw):
            while name not in mod_tok:
                mod(1, **kw)

        def M(name, a, n=16):
            return MODC[:, m_off[name] + a:m_off[name] + a + n]

        def bcast(dst, colap, *w):
            toks = []
            for q in range(4):
                i, b, fr = bank(GC)
                for j in range(4):
                    k = 4 * q + j
                    t = mm(b[:, 128 * j:128 * j + 128], colap[:, k:k + 1].to_broadcast([128, 128]), ident[:, :],
                           True, True, fr, *w, inc=(j == 3))
                bank_free[i] = copy(S, dst[:, 512 * q:512 * q + 512], b[:, :], t, *w)
            return bank_free[i]

        def x_transposed(src, dst, acol_, bcol_, *w):
            for k2 in range(8):
                i, b, fr = bank(GA)
                for j in range(2):
                    for t2 in range(2):
                        k = 2 * k2 + j
                        t = tr(b[:, 256 * j + 128 * t2:256 * j + 128 * t2 + 128], src[:, t2, 128 * k:128 * k + 128],
                               fr, *w, inc=(j == 1 and t2 == 1))
                for j in range(2):
                    k = 2 * k2 + j
                    if k2 % 2 == 0:
                        tok = ts(V, dst[:, k, :], b[:, 256 * j:256 * j + 256], acol_[:, k:k + 1], bcol_[:, k:k + 1],
                                 MUL, ADD, t, *w)
                    else:
                        tok2 = act(dst[:, k, :], b[:, 256 * j:256 * j + 256], ACT.Identity, t, *w,
                                   scale=acol_[:, k:k + 1], bias=bcol_[:, k:k + 1])
                bank_free[i] = V.t if k2 % 2 == 0 else S.t
            return tok, tok2

        R1, R2, R3, R4, R5 = 0, 4096, 8192, 12288, 16384

        def rms_stat(xv, junk, slot, eps, *w):
            for t2 in range(2):
                a = act(junk, xv[:, t2, :], ACT.Square, *w, S.t, accum_out=st[:, slot + 2 + t2:slot + 3 + t2])
            ts(V, st[:, slot + 2:slot + 4], st[:, slot + 2:slot + 4], 1.0 / D, eps, MUL, ADD, S.t)
            return rsqrt(st[:, slot:slot + 2], st[:, slot + 2:slot + 4], st[:, slot + 4:slot + 6], V.t)

        def make_u(xv, hv, rslot, abc, bbc, hc, hc2, U, step, *w):
            pe, pm = [None, None], [None, None]
            for pc in range(8):
                cs = slice(256 * pc, 256 * pc + 256)
                hb = hc[:, 2048 * (pc % 2):2048 * (pc % 2) + 2048].rearrange("p (q n) -> p q n", q=8)
                h2 = hc2[:, 2048 * (pc % 2):2048 * (pc % 2) + 2048].rearrange("p (g q h) -> p g q h", g=16, q=8)
                for t2 in range(2):
                    stt(hv[:, t2, cs], xv[:, t2, cs], st[:, rslot + t2:rslot + t2 + 1], abc[:, cs], MUL, MUL, *w)
                for t2 in range(2):
                    tt(V, hv[:, t2, cs], hv[:, t2, cs], bbc[:, cs], ADD, V.t)
                for t2 in range(2):
                    tok = dma(G, hb[16 * t2:16 * t2 + 16, :, :], hv[:, t2, cs], f"at{pc % 2}", V.t, pm[pc % 2])
                if pc % 2:
                    step()
                sv = hb[0:32, :, :].rearrange("p q (g h) -> p g q h", h=16)
                c1 = copy(V, h2[0:32, 0:8, :, :], sv[:, 0:8], tok, pe[pc % 2], *w)
                c2 = copy(S, h2[0:32, 8:16, :, :], sv[:, 8:16], tok, pe[pc % 2], *w)
                pm[pc % 2] = (c1, c2)
                i, b, fr = bank(GB)
                for j in range(16):
                    t = tr(b[:, 32 * j:32 * j + 32], h2[0:32, j, :, :].rearrange("p q h -> p (q h)"), c1, c2, fr,
                           inc=(j == 15), k=32)
                pe[pc % 2] = t
                bank_free[i] = copy(S, U[:, 16 * pc:16 * pc + 16, :], b[:, :].rearrange("p (g c) -> p g c", g=16), t, *w)
            return bank_free[i]

        def by_pair(dst, src, s_, q_, *w):
            n = dst.shape[1] // 2
            for d_ in range(2):
                for g2 in range(2):
                    tok = dma(q_, dst[64 * d_:64 * d_ + 64, n * g2:n * g2 + n], src[d_, 64 * g2:64 * g2 + 64], s_, *w)
            return tok

        hT = reg(24576, 4096).rearrange("p (k n) -> p k n", k=16)
        x0 = reg(R4, 4096).rearrange("p (t n) -> p t n", t=2)
        x_tok = dma(S, x0, A["x"][0].rearrange("(t p) n -> p t n", p=128), "x")
        braw = reg(R5, 4096).rearrange("p (r g q h) -> p r g q h", r=2, g=2, h=16)
        craw = reg(R5 + 4096, 4096).rearrange("p (r g h q) -> p r g h q", r=2, g=2, h=16)
        for r_, nm in enumerate(("re", "im")):
            b_tok = by_pair(reg(R5 + 2048 * r_, 2048), A[f"s5_b_{nm}_2"][0].rearrange("d g p h -> d g (p h)"), "b", G)
            c_tok = by_pair(reg(R5 + 4096 + 2048 * r_, 2048), A[f"s5_c_{nm}_2"][0].rearrange("d g h p -> d g (h p)"),
                            "c", G)
        mod_until("m0s", dve=True)
        sc1 = st[:, 110:126]
        ts(V, sc1, M("m0", 16), 1.0, None, ADD, None, mod_tok["m0s"])
        hT_toks = x_transposed(x0, hT, sc1, M("m0", 0), x_tok, V.t)

        smt = [sm[:, i * 128:(i + 1) * 128] for i in range(15)]
        are, aim, dtb, zr, zi, wr, wi, ta, tb, tc = smt[:10]
        a_re_tok = by_pair(are, A["s5_a_re_2"][0], "ar", G)
        a_im_tok = by_pair(aim, A["s5_a_im_2"][0], "ai", G)
        dt_tok = by_pair(tc[:, 0:2], A["s5_log_dt_2"][0].unsqueeze(2), "dt", G)
        t = act(tc[:, 2:4], tc[:, 0:2], ACT.Exp, dt_tok)
        sc0 = 2.0 ** -DOUBLINGS
        for g in range(2):
            h = slice(g * 64, g * 64 + 64)
            ts(V, zr[:, h], are[:, h], tc[:, 2 + g:3 + g], sc0, MUL, MUL, t, a_re_tok, a_im_tok)
            ts(V, zi[:, h], aim[:, h], tc[:, 2 + g:3 + g], sc0, MUL, MUL)
        ts(V, wr, zr, 1.0 / 6, 1.0, MUL, ADD, V.t)
        ts(V, wi, zi, 1.0 / 6, None, MUL, None)
        for n in (5, 4, 3, 2):
            tt(V, ta, zr, wr, MUL, V.t)
            tt(V, tb, zi, wi, MUL)
            tt(V, ta, ta, tb, SUB, V.t)
            tt(V, tb, zr, wi, MUL, V.t)
            tt(V, wi, zi, wr, MUL, V.t)
            tt(V, tb, tb, wi, ADD, V.t)
            ts(V, wr, ta, 1.0 / n, 1.0, MUL, ADD, V.t)
            ts(V, wi, tb, 1.0 / n, None, MUL, None)
        tt(V, ta, zr, wr, MUL, V.t)
        tt(V, tb, zi, wi, MUL)
        tt(V, ta, ta, tb, SUB, V.t)
        tt(V, tb, zr, wi, MUL, V.t)
        tt(V, wi, zi, wr, MUL, V.t)
        tt(V, wi, tb, wi, ADD, V.t)
        copy(V, wr, ta, V.t)
        for _ in range(DOUBLINGS):
            stt(ta, wr, 2.0, wr, ADD, MUL, V.t)
            tt(V, tb, wi, wi, MUL)
            stt(wi, wr, 1.0, wi, ADD, MUL, V.t)
            tt(V, wr, ta, tb, SUB, V.t)
            ts(V, wi, wi, 2.0, None, MUL, None, V.t)
        cr, ci, den, lbr, lbi, pr_, pi_ = smt[8], smt[9], smt[10], smt[11], smt[12], smt[13], smt[14]
        tt(V, den, are, are, MUL, V.t)
        tt(V, zr, aim, aim, MUL)
        tt(V, den, den, zr, ADD, V.t)
        recip(den, den, V.t)
        tt(V, ta, wr, are, MUL, V.t)
        tt(V, zr, wi, aim, MUL)
        tt(V, ta, ta, zr, ADD, V.t)
        tt(V, cr, ta, den, MUL, V.t)
        tt(V, ta, wi, are, MUL, V.t)
        tt(V, zr, wr, aim, MUL)
        tt(V, ta, ta, zr, SUB, V.t)
        tt(V, ci, ta, den, MUL, V.t)
        ts(V, lbr, wr, 1.0, None, ADD, None, V.t)
        copy(V, lbi, wi)
        tcr, tci, t1r, t1i = smt[0], smt[1], smt[2], smt[3]
        i, b, fr = bank(GA)
        for j, s_ in enumerate((cr, ci, lbr, lbi)):
            t = tr(b[:, 128 * j:128 * j + 128], s_, V.t, fr, id_tok, inc=(j == 3))
        bank_free[i] = copy(V, sm[:, 0:512], b[:, :], t)

        L1v = L1[:, :].rearrange("p (r d t) -> p r d t", r=2, t=9)
        L2v = L2[:, :].rearrange("p (r d t) -> p r d t", r=2, t=8)
        curr, curi, nxr, nxi = smt[4], smt[5], smt[6], smt[7]
        pa, pb_ = smt[10], smt[11]
        V.do(lambda e: e.memset(curr, 1.0), V.t)
        V.do(lambda e: e.memset(curi, 0.0), V.t)
        for tau in range(9):
            for r_, cur in enumerate((curr, curi)):
                copy(V, L1v[:, r_, 0:64, tau], cur[:, 0:64], V.t)
                copy(V, L1v[:, r_, 64:128, 8 - tau], cur[:, 64:128])
                if tau < 8:
                    copy(V, L2v[:, r_, 0:64, 7 - tau], cur[:, 0:64])
                    copy(V, L2v[:, r_, 64:128, tau], cur[:, 64:128])
            if tau == 8:
                copy(V, LR8[:, 0:128], curr)
                copy(V, LR8[:, 128:256], curr)
                ts(V, LS8[:, 0:128], curi, -1.0, None, MUL, None)
                copy(V, LS8[:, 128:256], curi)
                break
            tt(V, pa, curr, t1r, MUL, V.t)
            tt(V, pb_, curi, t1i, MUL)
            tt(V, nxr, pa, pb_, SUB, V.t)
            tt(V, pa, curr, t1i, MUL, V.t)
            tt(V, pb_, curi, t1r, MUL)
            tt(V, nxi, pa, pb_, ADD, V.t)
            curr, nxr = nxr, curr
            curi, nxi = nxi, curi
        L_tok = V.t

        def to_state(raw_fn, dst, tok, *w):
            for r_ in range(2):
                for h4 in range(4):
                    i, b, fr = bank(GA)
                    for j in range(4):
                        for g2 in range(2):
                            t = mm(b[64 * g2:64 * g2 + 64, 128 * j:128 * j + 128], raw_fn(r_, g2, 4 * h4 + j),
                                   ident[:, :], True, True, tok, fr, inc=(j == 3 and g2 == 1))
                    bank_free[i] = copy(S, dst[:, r_, :, 4 * h4:4 * h4 + 4].rearrange("p d h -> p h d"),
                                        b[:, :].rearrange("p (h d) -> p h d", h=4), t, *w)
            return bank_free[i]


        bT = reg(R3, 4096).rearrange("p (r d h) -> p r d h", r=2, h=16)
        Bb = reg(R2, 4096).rearrange("p (r d h) -> p r d h", r=2, h=16)
        cT = reg(R4, 4096).rearrange("p (r d h) -> p r d h", r=2, h=16)
        bT_tok = to_state(lambda r_, g2, h: braw[:, r_, g2, :, h], bT, b_tok)
        cT_tok = to_state(lambda r_, g2, h: craw[:, r_, g2, h, :], cT, c_tok, hT_toks)
        tmpb = reg(R5, 2048).rearrange("p (d h) -> p d h", h=16)

        def bcw(x):
            return x.unsqueeze(2).to_broadcast([128, 128, 16])

        tt(V, tmpb, bT[:, 1], bcw(tci), MUL, bT_tok, P.t)
        tt(V, Bb[:, 0], bT[:, 0], bcw(tcr), MUL)
        tt(V, Bb[:, 0], Bb[:, 0], tmpb, SUB, V.t)
        tt(V, tmpb, bT[:, 0], bcw(tci), MUL, V.t)
        tt(V, Bb[:, 1], bT[:, 1], bcw(tcr), MUL)
        tt(V, Bb[:, 1], Bb[:, 1], tmpb, ADD, V.t)
        Bb_tok = V.t
        def cmul(xr, xi, Lv, T, d0, outr, outi, t1, t2, neg, w_r, w_i):
            o4 = lambda y: y.rearrange("p (d t h) -> p d t h", d=8, t=T)
            for k in range(0, 8, 8):
                X = lambda x: x[:, d0:d0 + 8, :].unsqueeze(2).to_broadcast([128, 8, T, 16])
                Lb = lambda r_: Lv[:, r_, d0:d0 + 8, :].unsqueeze(3).to_broadcast([128, 8, T, 16])
                tt(V, o4(outr), X(xr), Lb(0), MUL, *w_r)
                tt(V, o4(t1), X(xi), Lb(1), MUL, V.t)
                tt(V, outr, outr, t1, SUB, V.t)
                r_tok = V.t
                tt(V, o4(outi), X(xr), Lb(1), MUL, *w_i)
                tt(V, o4(t2), X(xi), Lb(0), MUL, V.t)
                if neg:
                    stt(outi, outi, -1.0, t2, MUL, SUB, V.t)
                else:
                    tt(V, outi, outi, t2, ADD, V.t)
                return r_tok, V.t

        def v_matmuls(mv, Uv, d0, n, dst, base_tok, *w):
            i, b, fr = bank(GB)
            bv = b[:, :].rearrange("p (d r c) -> p d r c", r=2, c=32)
            for dd in range(n):
                dg = d0 + dd
                gp = dg % 64
                for r_ in range(2):
                    for g2 in range(2):
                        t = mm(bv[64 * g2:64 * g2 + 64, dd, r_, :], mv[:, dd, r_, 64 * g2:64 * g2 + 64],
                               Uv[:, gp + 64 * g2, :], True, True, fr, base_tok, *w,
                               inc=(dd == n - 1 and r_ == 1 and g2 == 1))
            if d0 < 64:
                dv = dst[:, :, :, d0:d0 + n]
                bank_free[i] = None
                for r_ in range(2):
                    tok = copy(S, dv[:, :, r_, :].rearrange("p k d -> p d k"), bv[:, 0:n, r_, :], t)
            else:
                for r_ in range(2):
                    tok = copy(S, dst[:, ::-1, r_, d0:d0 + n].rearrange("p k d -> p d k"), bv[:, 0:n, r_, :], t)
            bank_free[i] = tok
            return t, tok


        KK = reg(R1, 3840).rearrange("p (a j h) -> p a j h", a=16, j=15)
        mask16 = smt[0]
        V.do(lambda e: e.tensor_reduce(mask16[:, 0:16], ident[:, :].rearrange("p (b h) -> p h b", b=8), AX, ADD),
             V.t, id_tok)
        tt(V, KK[:, :, 7, :], C("sd").unsqueeze(2).to_broadcast([128, 16, 16]),
           mask16[:, 0:16].unsqueeze(1).to_broadcast([128, 16, 16]), MUL, V.t, rows_read)
        clr, cli = reg(R3, 1152), reg(R3 + 1152, 1152)
        ct1, ct2 = reg(R3 + 2304, 1152), reg(R5, 1152)
        bd = BBD[:, :].rearrange("p (d r m) -> p d r m", d=8, r=2)
        bd_zero = G.do(lambda e: e.memset(BBD[:, :], 0.0))

        stage = {"bufs": [MSB[:, 512 * i:512 * i + 512] for i in range(3)], "n": 0, "free": [None] * 4,
                 "after": None}
        proj_tok = [None] * 4
        win = A["a_w_in"][0]
        sub_tok = dma(G, SUBG[:, :], A["a_subln_g"].to_broadcast([128, 256]), "sub")
        ts(V, SUBG[:, :], SUBG[:, :], 1.0 - LAM_INIT, None, MUL, None, sub_tok)
        subg_tok = V.t
        gx = ACC

        def project(pnl):
            which, loc = pnl // 8, pnl % 8
            sbi = stage["n"] % len(stage["bufs"])
            stage["n"] += 1
            buf = stage["bufs"][sbi]
            i, wt, tok = take(lambda: load_w(win, 0, 256 * pnl))
            if which < 2:
                bi, b, fr = bank(GA)
                for j in range(2):
                    for k in range(KT):
                        t = mm(b[:, 256 * j:256 * j + 256], wt[:, k, 128 * j:128 * j + 128], hT[:, k, :],
                               k == 0, k == KT - 1, tok, fr, hT_toks, inc=(j == 1 and k == KT - 1))
                release(i, t)
                if which == 0:
                    tok = S.do(lambda e: e.mul(buf, b[:, :], QK_SCALE), t, stage["free"][sbi], stage["after"])
                else:
                    tok = copy(S, buf, b[:, :], t, stage["free"][sbi], stage["after"])
                bank_free[bi] = tok
                dst = proj_d[which][:, 512 * loc:512 * loc + 512]
                stage["free"][sbi] = proj_tok[which] = dma(G, dst, buf, f"st{sbi}", tok)
            else:
                bi, b, fr = bank(GA)
                for t2 in range(2):
                    for k in range(KT):
                        t = mm(b[:, 256 * t2:256 * t2 + 256], hT[:, k, 128 * t2:128 * t2 + 128], wt[:, k, :],
                               k == 0, k == KT - 1, tok, fr, hT_toks, inc=(t2 == 1 and k == KT - 1))
                release(i, t)
                if which == 2:
                    tok = copy(S, buf, b[:, :], t, stage["free"][sbi], stage["after"])
                else:
                    gb_ = GXB
                    t = act(gb_, b[:, :], ACT.Sigmoid, t, V.t)
                    g2v = gb_.rearrange("p (t n) -> p t n", t=2)
                    tt(V, g2v, g2v, SUBG[:, :].unsqueeze(1).to_broadcast([128, 2, 256]), MUL, t, subg_tok)
                    tok = tt(V, buf, b[:, :], gb_, MUL, V.t, stage["free"][sbi], stage["after"])
                bank_free[bi] = tok
                dst = proj_d[which].rearrange("p (t n) -> p t n", t=2)[:, :, 256 * loc:256 * loc + 256]
                stage["free"][sbi] = proj_tok[which] = dma(G, dst, buf.rearrange("p (t n) -> p t n", t=2),
                                                           f"st{sbi}", tok)

        cl_dma = None
        kk_pe = None
        pend = {}

        def cl_make(ch):
            d0 = 8 * ch
            for g2 in range(2):
                for r_ in range(2):
                    tok = copy(G, bd[64 * g2:64 * g2 + 64, :, r_, 16 * g2:16 * g2 + 16],
                               Bb[64 * g2:64 * g2 + 64, r_, d0:d0 + 8, :], bd_zero, Bb_tok, pend.get("kk_pe"))
            r_tok, i_tok = cmul(cT[:, 0], cT[:, 1], L1v, 9, d0, clr, cli, ct1, ct2, True,
                                (cT_tok, pend.get("cl_dma"), pend.get("kk_pe"), Bb_tok),
                                (pend.get("cl_dma"), pend.get("kk_pe")))
            oo = 16 if ch < 8 else 0
            clrv = clr.rearrange("p (d x) -> p d x", d=8)
            cliv = cli.rearrange("p (d x) -> p d x", d=8)
            dst = cl_d[:, d0 * 256:d0 * 256 + 2048].rearrange("p (d r x) -> p d r x", d=8, r=2)
            dma(G, dst[:, :, 0, :], clrv[:, :, oo:oo + 128], "cl", i_tok)
            pend["cl_dma"] = dma(G, dst[:, :, 1, :], cliv[:, :, oo:oo + 128], "cl", i_tok)
            return tok, i_tok

        def cl_kernels(ch, bd_tok, i_tok):
            d0 = 8 * ch
            clrv = clr.rearrange("p (d x) -> p d x", d=8)
            cliv = cli.rearrange("p (d x) -> p d x", d=8)
            fwd = ch < 8
            ko = 0 if fwd else 16
            i, b, fr = bank(GB)
            bv = b[:, 0:256].rearrange("p (a x) -> p a x", a=2)
            for a in range(2):
                for m in range(4):
                    dd = 4 * a + m
                    o = bv[32 * m:32 * m + 32, a, :]
                    mm(o, bd[:, dd, 0, :], clrv[:, dd, ko:ko + 128], True, False, bd_tok, i_tok, fr)
                    kk_pe = mm(o, bd[:, dd, 1, :], cliv[:, dd, ko:ko + 128], False, True, inc=(dd == 7))
            pend["kk_pe"] = kk_pe
            a0 = (d0 % 64) // 4
            kb = bv.rearrange("p a (t h) -> p a t h", t=8)
            if fwd:
                copy(V, KK[:, a0:a0 + 2, 8:15, :], kb[:, :, 1:8, :], kk_pe)
                kz = kb[:, :, 0, :]
            else:
                copy(V, KK[:, a0:a0 + 2, 0:7, :], kb[:, :, 0:7, :], kk_pe)
                kz = kb[:, :, 7, :]
            bank_free[i] = tt(V, KK[:, a0:a0 + 2, 7, :], KK[:, a0:a0 + 2, 7, :], kz, ADD, V.t)

        GXB = MSB[:, 1536:2048]
        for ch in range(16):
            args_ = cl_make(ch)
            project(ch)
            if "m2a" not in mod_tok:
                mod(2)
            elif ch % 2:
                mod(1)
            cl_kernels(ch, *args_)
        for q in range(8):
            kk_dma = dma(G, toep_d[q].rearrange("a p x -> p a x"),
                         KK[:, :, 7 - q:15 - q, :].rearrange("p a j h -> p a (j h)"), "kk", V.t)
        cl_all, kk_all = pend["cl_dma"], kk_dma
        mod_until("m2a")

        distm = L1[:, 0:512].rearrange("p (t s) -> p t s", t=2)
        negm = L1[:, 512:1024].rearrange("p (t s) -> p t s", t=2)
        tri = L1[:, 1024:1536].rearrange("p (t s) -> p t s", t=2)
        tables_read = V.t

        for t2 in range(2):
            G.do(lambda e, t2=t2: e.iota(distm[:, t2, :], pattern=[[-1, 256]], base=128 * t2, channel_multiplier=1,
                                         allow_small_or_imprecise_dtypes=True), tables_read)
            G.do(lambda e, t2=t2: e.affine_select(out=distm[:, t2, :], in_=distm[:, t2, :], compare_op=ALU.is_ge,
                                                  fill=1e33, base=128 * t2, pattern=[[-1, 256]],
                                                  channel_multiplier=1), G.t)
            G.do(lambda e, t2=t2: e.memset(negm[:, t2, :], 0.0))
            G.do(lambda e, t2=t2: e.affine_select(out=negm[:, t2, :], in_=negm[:, t2, :], compare_op=ALU.is_ge,
                                                  fill=-1e30, base=128 * t2, pattern=[[-1, 256]],
                                                  channel_multiplier=1), G.t)
            G.do(lambda e, t2=t2: e.memset(tri[:, t2, :], 1.0))
            G.do(lambda e, t2=t2: e.affine_select(out=tri[:, t2, :], in_=tri[:, t2, :], compare_op=ALU.is_ge,
                                                  fill=0.0, base=-128 * t2, pattern=[[1, 256]],
                                                  channel_multiplier=-1), G.t)
        mask_tok = G.t

        lam_t = sm[:, 0:512]
        for i_, n in enumerate(("a_lam_q1", "a_lam_k1", "a_lam_q2", "a_lam_k2")):
            lam_tok = dma(G, sm[:, 128 * i_:128 * i_ + 128], A[n].to_broadcast([128, 128]), "lam", tables_read)
        tt(V, sm[:, 0:128], sm[:, 0:128], sm[:, 128:256], MUL, lam_tok)
        tt(V, sm[:, 256:384], sm[:, 256:384], sm[:, 384:512], MUL, lam_tok)
        ls = st[:, 100:104]
        V.do(lambda e: e.reduce_sum(ls[:, 0:1], sm[:, 0:128], AX), V.t)
        V.do(lambda e: e.reduce_sum(ls[:, 1:2], sm[:, 256:384], AX), V.t)
        t = act(ls[:, 2:4], ls[:, 0:2], ACT.Exp, V.t)
        nlam = st[:, 104:105]
        tt(V, nlam, ls[:, 3:4], ls[:, 2:3], SUB, t)
        ts(V, nlam, nlam, -LAM_INIT, None, ADD, None, V.t)
        lam_ready = V.t


        ctxv = reg(R1, 4096).rearrange("p (t n) -> p t n", t=2)
        abc, bbc = reg(R5, 2048), reg(R5 + 2048, 2048)
        hc, hc2 = reg(R5 + 4096, 4096), reg(R3, 4096)
        U = reg(R4, 4096).rearrange("p (g c) -> p g c", c=32)
        ctx_tok = dma(G, ctxv, A["ctx_2"][0].rearrange("(t p) n -> p t n", p=128), "ctx", kk_all, V.t)
        acol = st[:, 64:80]
        stt(acol, M("m2x", 16), 1.0, C("npre"), ADD, MUL, mod_tok["m2a"])
        acol2 = st[:, 80:96]
        stt(acol2, M("m2", 16), 1.0, C("npre"), ADD, MUL)
        ctok = V.t
        a1 = bcast(abc, acol, ctok)
        a2 = bcast(bbc, M("m2x", 0), ctok)
        rt = rms_stat(ctxv, hc[:, 0:2048], 0, 1e-6, ctx_tok)
        u_steps = iter(range(16, 20))
        u_tok = make_u(ctxv, ctxv, 0, abc, bbc, hc, hc2, U, lambda: project(next(u_steps)),
                       ctx_tok, a1, a2, rt, cl_all, P.t)

        Vc = reg(R5, 8192).rearrange("p (k r d) -> p k r d", k=32, r=2)
        vmat = MSB[:, :].rearrange("p (d r m) -> p d r m", d=8, r=2)
        blr, bli = reg(R3, 1024), reg(R3 + 1024, 1024)
        bt1, bt2 = reg(R3 + 2048, 1024), reg(R3 + 3072, 1024)
        old_stage = tuple(stage["free"])
        stage.update(bufs=[reg(R1 + 512 * i, 512) for i in range(4)], n=0, free=[None] * 4,
                     after=(old_stage, V.t, u_tok, (sems["at0"], dma_count["at0"]), (sems["at1"], dma_count["at1"])))
        GXB = reg(R1 + 2048, 512)
        S.wait(stage["after"])
        pend["bl_free"] = (P.t, V.t, S.t, G.t)
        pend["ms"] = old_stage

        def bl_make(ch):
            return cmul(Bb[:, 0], Bb[:, 1], L2v, 8, 8 * ch, blr, bli, bt1, bt2, False,
                        (pend["bl_free"],), (pend["bl_free"],))[1]

        def bl_turn(ch, i_tok):
            d0 = 8 * ch
            for r_, src in enumerate((blr, bli)):
                for half in range(2):
                    i, b, fr = bank(GC)
                    for j in range(4):
                        dd = 4 * half + j
                        t = tr(b[:, 128 * j:128 * j + 128], src[:, 128 * dd:128 * dd + 128],
                               i_tok, fr, inc=(j == 3))
                    bank_free[i] = copy(S, vmat[:, 4 * half:4 * half + 4, r_, :],
                                        b[:, :].rearrange("p (d m) -> p d m", d=4), t, pend["ms"], pend.get("v_pe"))
            pend["bl_free"] = P.t
            pend["ms_ready"] = S.t
            pend["ms"] = dma(G, m_state_d[:, d0 * 256:d0 * 256 + 2048], MSB[:, :], "ms", S.t)

        def bl_v(ch):
            pend["v_pe"], pend["v_tok"] = v_matmuls(vmat, U, 8 * ch, 8, Vc, pend["ms_ready"], u_tok)

        npnl = 20
        for ch in range(16):
            it = bl_make(ch)
            if ch < 12:
                project(npnl)
                npnl += 1
            bl_turn(ch, it)
            mod(1, dve=True)
            if ch % 2 or ch >= 12:
                mod(1)
            bl_v(ch)
        ms_all = pend["ms"]
        v_ctx = (pend["v_tok"], V.t)

        stA, stB = SF[:, 0:256], SF[:, 256:512]
        t_1, t_2 = sm[:, 512:768], sm[:, 768:1024]
        l_swap = lambda x: x.rearrange("p (r d) -> p r d", r=2)

        def chunk_step(cur, nxt, vk, *w, q=V):
            tt(q, t_1, cur, LR8[:, :], MUL, q.t, *w)
            tt(q, l_swap(t_2), l_swap(cur)[:, ::-1, :], l_swap(LS8[:, :]), MUL)
            tt(q, t_1, t_1, vk, ADD, q.t)
            return tt(q, nxt, t_1, t_2, ADD, q.t)

        def scan_ctx():
            cur, nxt = stA, stB
            G.do(lambda e: e.memset(stA, 0.0), v_ctx)
            for k in range(32):
                chunk_step(cur, nxt, Vc[:, k].rearrange("p r d -> p (r d)"), v_ctx, q=G)
                cur, nxt = nxt, cur

        xv = reg(0, 4096).rearrange("p (t n) -> p t n", t=2)
        exb = MSB[:, 0:256]
        vN = reg(4096, 4096).rearrange("p (t n) -> p t n", t=2)
        qT = reg(8192, 4096).rearrange("p (k n) -> p k n", k=16)
        kT = reg(12288, 4096).rearrange("p (k n) -> p k n", k=16)
        gN = reg(20480, 4096).rearrange("p (t n) -> p t n", t=2)
        oN = reg(24576, 4096).rearrange("p (t n) -> p t n", t=2)
        bcA, bcB = reg(12288, 2048), reg(14336, 2048)
        phase0 = (V.t, P.t, S.t, cl_all, ms_all)
        q_tok = dma(SP, reg(8192, 4096), proj_d[0], "p0", phase0, proj_tok[0])
        k_tok = dma(SP, reg(12288, 4096), proj_d[1], "p1", proj_tok[1])
        v_tok = dma(SP, reg(4096, 4096), proj_d[2], "p2", proj_tok[2])
        stage_read = tuple(x_ for x_ in stage["free"])
        x_tok = dma(SP, xv, A["x"][0].rearrange("(t p) n -> p t n", p=128), "x", stage_read, proj_tok[3])
        V.wait(phase0)
        S.wait(phase0)
        scan_ctx()
        g_tok = dma(G, reg(20480, 4096), proj_d[3], "at3", G.t, proj_tok[3])

        def plus1(dst, a, *w):
            return ts(V, dst, a, 1.0, None, ADD, None, *w)

        def dense_T(hin, W, n0, npan, dst_fn, *w, side=None):
            for pnl in range(npan):
                i, wt, tok = take(lambda: load_w(W, 0, n0 + 256 * pnl))
                bi, b, fr = bank(GA)
                P.wait(fr, *w)
                for j in range(2):
                    for k in range(KT):
                        t = mm(b[:, 256 * j:256 * j + 256], wt[:, k, 128 * j:128 * j + 128], hin[:, k, :],
                               k == 0, k == KT - 1, tok, inc=(j == 1 and k == KT - 1))
                release(i, t)
                bank_free[bi] = dst_fn(pnl, b[:, :].rearrange("p (j n) -> p j n", j=2), t)
                if side:
                    side()

        def dense_N(hin, W, n0, npan, dst_fn, *w, kslots=1, side=None):
            for pnl in range(npan):
                bb = [bank(GB), bank(GC)] if kslots > 1 else [bank(GB), bank(GB)]
                for ks in range(kslots):
                    i, wt, tok = take(lambda: load_w(W, 2048 * ks, n0 + 256 * pnl))
                    for t2 in range(2):
                        bi, b, fr = bb[t2]
                        for k in range(KT):
                            t = mm(b[:, 0:256], hin[:, ks * KT + k, 128 * t2:128 * t2 + 128], wt[:, k, :],
                                   ks == 0 and k == 0, ks == kslots - 1 and k == KT - 1, tok, fr, *w,
                                   inc=(k == KT - 1))
                        if ks == kslots - 1:
                            bank_free[bi] = dst_fn(pnl, t2, b[:, 0:256], t)
                    release(i, t)
                if side:
                    side()

        def silu_panel(dst, ps, tk, ex, extra=None):
            t = act(ex, ps, ACT.Sigmoid, tk, V.t)
            if extra is not None:
                tt(V, ex, ex, extra, MUL, t)
                t = V.t
            return tt(V, dst, ps, ex, MUL, t)

        def put_q(pnl, b, t):
            return S.do(lambda e: e.mul(qT[:, 2 * pnl:2 * pnl + 2, :], b, QK_SCALE), t)

        def put_k(pnl, b, t):
            return copy(V, kT[:, 2 * pnl:2 * pnl + 2, :], b, t)

        def put_v(pnl, t2, b, t):
            return copy(S, vN[:, t2, 256 * pnl:256 * pnl + 256], b, t)

        exb = MSB[:, 0:256]

        h_dead = P.t

        NBUF = 3
        wk = L2[:, 0:1536].rearrange("p (i x) -> p i x", i=NBUF)
        aT_ = MSB[:, 256:1792].rearrange("p (i x) -> p i x", i=6)
        stat = st[:, 128:176]
        ssq = st[:, 176:192]
        info = {}

        def items_a(i):
            return i // 2, i % 2

        def a_scores(i):
            h, t2 = items_a(i)
            w_ = 128 * (t2 + 1)
            bi, b, fr = bank(GA)
            for c in range(2):
                t = mm(b[:, 256 * c:256 * c + w_], qT[:, 2 * h + c, 128 * t2:128 * t2 + 128],
                       kT[:, 2 * h + c, 0:w_], True, True, fr, q_tok, k_tok, inc=(c == 1))
            info[i] = {"b": bi, "s": t}

        def a_soft(i):
            h, t2 = items_a(i)
            w_ = 128 * (t2 + 1)
            slope = 2.0 ** (-8.0 * (h + 1) / 8)
            n = info[i]
            b = banks[n["b"]]
            p = wk[:, i % NBUF, :].rearrange("p (c s) -> p c s", c=2)[:, :, 0:w_]
            sb_ = stat[:, 6 * (i % NBUF):6 * (i % NBUF) + 6]
            prev = info.get(i - NBUF, {})
            bv = b[:, :].rearrange("p (c s) -> p c s", c=2)[:, :, 0:w_]
            t = stt(p, distm[:, t2, 0:w_].unsqueeze(1).to_broadcast([128, 2, w_]), -slope, bv, MUL, ADD,
                    n["s"], mask_tok, prev.get("tr"), V.t)
            bank_free[n["b"]] = t
            V.do(lambda e: e.tensor_reduce(sb_[:, 0:2], p, AX, MAX, negate=True), V.t)
            mx = V.t
            for c in range(2):
                t = act(p[:, c, :], p[:, c, :], ACT.Exp, mx, bias=sb_[:, c:c + 1], accum_out=sb_[:, 2 + c:3 + c])
            n["e"] = S.t

        def a_mix(i):
            h, t2 = items_a(i)
            w_ = 128 * (t2 + 1)
            n = info[i]
            p = wk[:, i % NBUF, :].rearrange("p (c s) -> p c s", c=2)[:, :, 0:w_]
            sb_ = stat[:, 6 * (i % NBUF):6 * (i % NBUF) + 6]
            recip(sb_[:, 4:6], sb_[:, 2:4], n["e"])
            tt(V, sb_[:, 5:6], sb_[:, 5:6], nlam, MUL, V.t)
            ts(V, p[:, 0, :], p[:, 0, :], sb_[:, 4:5], None, MUL, None, V.t)
            n["a"] = stt(p[:, 0, :], p[:, 1, :], sb_[:, 5:6], p[:, 0, :], MUL, ADD, V.t)

        def a_turn(i):
            h, t2 = items_a(i)
            n = info[i]
            p = wk[:, i % NBUF, 0:256]
            bi, b, fr = bank(GB)
            for s in range(t2 + 1):
                t = tr(b[:, 128 * s:128 * s + 128], p[:, 128 * s:128 * s + 128], n["a"], fr, inc=(s == t2))
            n["tr"] = t
            w_ = 128 * (t2 + 1)
            bank_free[bi] = copy(V, aT_[:, i % NBUF * 2:i % NBUF * 2 + 2, :].rearrange("p a b -> p (a b)")[:, 0:w_],
                                 b[:, 0:w_], t, info.get(i - NBUF, {}).get("pv"))
            n["aT"] = bank_free[bi]

        def a_out(i):
            h, t2 = items_a(i)
            n = info[i]
            bi, b, fr = bank(GC)
            av = aT_[:, i % NBUF * 2:i % NBUF * 2 + 2, :].rearrange("p a b -> p (a b)")
            for s in range(t2 + 1):
                t = mm(b[:, 0:256], av[:, 128 * s:128 * s + 128], vN[:, s, 256 * h:256 * h + 256],
                       s == 0, s == t2, n["aT"], fr, v_tok, inc=(s == t2))
            n["pv"] = t
            o = oN[:, t2, 256 * h:256 * h + 256]
            c1 = copy(S, o, b[:, 0:256], t, h_dead)
            act(MSB[:, 1792:2048], b[:, 0:256], ACT.Square, S.t, accum_out=ssq[:, 2 * h + t2:2 * h + t2 + 1])
            bank_free[bi] = S.t

        pipeline(16, [lambda i: (a_scores(i), mod(1)), a_soft, a_mix, a_turn, a_out])
        ts(V, ssq, ssq, 1.0 / 256, 1e-5, MUL, ADD, S.t)
        rs = st[:, 192:208]
        rsqrt(rs, ssq, st[:, 208:224], V.t)
        for h in range(8):
            for t2 in range(2):
                o = oN[:, t2, 256 * h:256 * h + 256]
                stt(o, o, rs[:, 2 * h + t2:2 * h + t2 + 1], gN[:, t2, 256 * h:256 * h + 256], MUL, MUL, V.t, g_tok)

        def to_T(src, dst, *w):
            for k2 in range(8):
                i, b, fr = bank(GA)
                for j in range(2):
                    for t2 in range(2):
                        k = 2 * k2 + j
                        t = tr(b[:, 256 * j + 128 * t2:256 * j + 128 * t2 + 128], src[:, t2, 128 * k:128 * k + 128],
                               fr, *w, inc=(j == 1 and t2 == 1))
                q_ = V if k2 % 2 else S
                bank_free[i] = copy(q_, dst[:, 2 * k2:2 * k2 + 2, :], b[:, :].rearrange("p (j n) -> p j n", j=2),
                                    t, *w)
            return V.t, S.t

        oT = qT
        toks = to_T(oN, oT, V.t, P.t)

        dmod = lambda: mod(1, dve=True)

        def residual(toks, W, gdone, side=None):
            def put(pnl, t2, b, t):
                cs = slice(256 * pnl, 256 * pnl + 256)
                tmp_ = MSB[:, 256 * t2:256 * t2 + 256]
                r = tt(V, tmp_, b, bcA[:, cs], MUL, t, gdone, V.t)
                stt(xv[:, t2, cs], xv[:, t2, cs], ALPHA, tmp_, MUL, ADD, V.t)
                return r
            dense_N(oT, W, 0, 8, put, *toks, side=side)
            return V.t

        def layer_norm(l, *w):
            lg = dma(G, bcA, A["ln_g"][l:l + 1, :].to_broadcast([128, 2048]), "bc0", *w)
            lb = dma(G, bcB, A["ln_b"][l:l + 1, :].to_broadcast([128, 2048]), "bc1", *w)
            bs = MSB[:, 512:560].rearrange("p (t c s) -> p t c s", t=2, c=4)
            mv = st[:, 0:4].rearrange("p (t s) -> p t s", t=2)
            for t2 in range(2):
                for c in range(4):
                    V.do(lambda e, t2=t2, c=c: e.bn_stats(bs[:, t2, c, :], xv[:, t2, 512 * c:512 * c + 512]), V.t)
                V.do(lambda e, t2=t2: e.bn_aggr(mv[:, t2, :], bs[:, t2, :, :].rearrange("p c s -> p (c s)")), V.t)
            ts(V, st[:, 4:6], mv[:, :, 1], 1e-5, None, ADD, None, V.t)
            rsqrt(st[:, 6:8], st[:, 4:6], st[:, 8:10], V.t)
            for t2 in range(2):
                for hf in range(2):
                    cs = slice(1024 * hf, 1024 * hf + 1024)
                    ts(V, xv[:, t2, cs], xv[:, t2, cs], mv[:, t2, 0:1], st[:, 6 + t2:7 + t2], SUB, MUL, V.t)
                    tt(V, xv[:, t2, cs], xv[:, t2, cs], bcA[:, cs], MUL, V.t, lg)
                    tt(V, xv[:, t2, cs], xv[:, t2, cs], bcB[:, cs], ADD, V.t, lb)
            return V.t

        mod_until("m0g")
        gb = bcast(bcA, M("m0", 32), mod_tok["m0g"], P.t)
        residual((toks, x_tok), A["a_w_out"][0], gb, side=dmod)
        xt = layer_norm(0, V.t)

        h1 = hT
        mod_until("kv")
        sc2 = st[:, 110:126]
        plus1(sc2, M("m1", 16), xt, P.t, S.t)
        toks = x_transposed(xv, h1, sc2, M("m1", 0), V.t, P.t)
        dense_T(h1, A["b_w_in"][0], 0, 8, put_q, *toks, side=dmod)
        q_tok = S.t

        def put_g2(pnl, t2, b, t):
            return silu_panel(gN[:, t2, 256 * pnl:256 * pnl + 256], b, t, exb)

        dense_N(h1, A["b_w_in"][0], 2048, 8, put_g2, *toks, side=dmod)
        g_tok = V.t
        plus1(sc2, M("kv", 16), V.t, P.t, S.t)
        toks = x_transposed(xv, h1, sc2, M("kv", 0), V.t, P.t)
        dense_T(h1, A["kv_w"], 0, 8, put_k, *toks, side=dmod)
        k_tok = V.t
        dense_N(h1, A["kv_w"], 2048, 8, put_v, *toks, side=dmod)
        v_tok = S.t
        zw = sm[:, 768:1024].rearrange("p (k n) -> p k n", k=16)
        bf = sm[:, 1024:1040]
        zf_tok = dma(G, zw, A["kv_w"][:, 4096:4112].rearrange("(k p) n -> p k n", p=128), "zf", G.t)
        zf_tok = dma(G, bf, A["kv_b_f"].rearrange("(a n) -> a n", a=1).to_broadcast([128, 16]), "zf")
        lf = sm[:, 1056:1088].rearrange("p (t h) -> p t h", t=2)
        tz = sm[:, 1088:1120].rearrange("p (t h) -> p t h", t=2)
        bi, b, fr = bank(GA)
        for t2 in range(2):
            for k in range(KT):
                t = mm(b[:, 16 * t2:16 * t2 + 16], h1[:, k, 128 * t2:128 * t2 + 128], zw[:, k, :], k == 0, k == KT - 1,
                       fr, zf_tok, *toks, inc=(t2 == 1 and k == KT - 1))
        bz = b[:, 0:32].rearrange("p (t h) -> p t h", t=2)
        zz = sm[:, 1120:1152].rearrange("p (t h) -> p t h", t=2)
        bank_free[bi] = tt(V, zz, bz, bf.unsqueeze(1).to_broadcast([128, 2, 16]), ADD, t, zf_tok)
        ts(V, tz, zz, -1.0, None, MUL, None, V.t)
        tt(V, tz, tz, zz, MIN, V.t)
        t = act(tz, tz, ACT.Exp, V.t)
        t = act(tz, tz, ACT.Ln, t, bias=1.0)
        ts(V, lf, zz, 0.0, None, MIN, None, V.t)
        tt(V, lf, lf, tz, SUB, V.t, t)
        FT = sm[:, 1152:1408]
        nFT = sm[:, 1408:1664]
        bi, b, fr = bank(GA)
        for s in range(2):
            t = mm(b[0:16, 0:256], lf[:, s, :], tri[:, s, :], s == 0, s == 1, V.t, fr, mask_tok, inc=(s == 1))
        copy(V, FT[0:16, :], b[0:16, 0:256], t)
        bank_free[bi] = ts(V, nFT[0:16, :], b[0:16, 0:256], -1.0, None, MUL, None, t)
        f_tok = V.t
        h_dead = P.t
        info.clear()
        wk2 = L2[:, 0:1024].rearrange("p (i x) -> p i x", i=4)
        stat2 = st[:, 128:144]

        def f_scores(i):
            h, t2 = i // 2, i % 2
            w_ = 128 * (t2 + 1)
            bi, b, fr = bank(GA)
            sel = ident[0:16, h:h + 1]
            mm(b[:, 0:w_], qT[:, h, 128 * t2:128 * t2 + 128], kT[:, h, 0:w_], True, False, fr, q_tok, k_tok, f_tok)
            mm(b[:, 0:w_], FT[0:16, 128 * t2:128 * t2 + 128], sel.to_broadcast([16, w_]), False, False)
            t = mm(b[:, 0:w_], sel.to_broadcast([16, 128]), nFT[0:16, 0:w_], False, True, inc=True)
            info[i] = {"b": bi, "s": t}

        def f_soft(i):
            h, t2 = i // 2, i % 2
            w_ = 128 * (t2 + 1)
            n = info[i]
            p = wk2[:, i % 4, 0:w_]
            s_ = stat2[:, 4 * (i % 4):4 * (i % 4) + 4]
            bank_free[n["b"]] = tt(V, p, banks[n["b"]][:, 0:w_], negm[:, t2, 0:w_], ADD, n["s"], mask_tok,
                                   info.get(i - 4, {}).get("tr"), V.t)
            V.do(lambda e: e.tensor_reduce(s_[:, 0:1], p, AX, MAX, negate=True), V.t, info.get(i - 4, {}).get("o"))
            act(p, p, ACT.Exp, V.t, bias=s_[:, 0:1], accum_out=s_[:, 1:2])
            n["e"] = S.t

        def f_turn(i):
            h, t2 = i // 2, i % 2
            w_ = 128 * (t2 + 1)
            n = info[i]
            p = wk2[:, i % 4, 0:w_]
            bi, b, fr = bank(GB)
            for s in range(t2 + 1):
                t = tr(b[:, 128 * s:128 * s + 128], p[:, 128 * s:128 * s + 128], n["e"], fr, inc=(s == t2))
            n["tr"] = t
            bank_free[bi] = copy(S, aT_[:, i % 3 * 2:i % 3 * 2 + 2, :].rearrange("p a b -> p (a b)")[:, 0:w_],
                                 b[:, 0:w_], t, info.get(i - 3, {}).get("pv"))
            n["aT"] = bank_free[bi]

        def f_out(i):
            h, t2 = i // 2, i % 2
            n = info[i]
            bi, b, fr = bank(GC)
            av = aT_[:, i % 3 * 2:i % 3 * 2 + 2, :].rearrange("p a b -> p (a b)")
            for s in range(t2 + 1):
                t = mm(b[:, 0:128], av[:, 128 * s:128 * s + 128], vN[:, s, 128 * h:128 * h + 128],
                       s == 0, s == t2, n["aT"], fr, v_tok, inc=(s == t2))
            n["pv"] = t
            s_ = stat2[:, 4 * (i % 4):4 * (i % 4) + 4]
            recip(s_[:, 2:3], s_[:, 1:2], n["e"])
            cs = slice(128 * h, 128 * h + 128)
            bank_free[bi] = stt(oN[:, t2, cs], b[:, 0:128], s_[:, 2:3], gN[:, t2, cs], MUL, MUL, V.t, t, h_dead, g_tok)
            n["o"] = V.t

        pipeline(32, [f_scores, f_soft, f_turn, f_out])
        toks = to_T(oN, oT, V.t, P.t)
        gb = bcast(bcA, M("m1", 32), mod_tok["m1"], V.t, P.t)
        abc, bbc = reg(24576, 2048), reg(26624, 2048)
        a1 = bcast(abc, acol2, P.t)
        a2 = bcast(bbc, M("m2", 0))
        residual(toks, A["b_w_out"][0], gb)
        xt = layer_norm(1, V.t)

        everything = (V.t, P.t, S.t, G.t)

        def load_cl(n):
            i = ring_state["n"] % NSLOT
            ring_state["n"] += 1
            t_ = ring[:, i * SLOTF:(i + 1) * SLOTF]
            dma(SP, t_[:, 0:2048], cl_d[:, n * 2048:(n + 1) * 2048], f"ring{i}", slot_free[i])
            tok = dma(SP, t_[:, 2048:4096], cl_d[:, 16384 + n * 2048:16384 + (n + 1) * 2048], f"ring{i}")
            return i, t_.rearrange("p (b d r x) -> p b d r x", b=2, d=8, r=2), tok

        def load_toep(n):
            i = ring_state["n"] % NSLOT
            ring_state["n"] += 1
            t_ = ring[:, i * SLOTF:i * SLOTF + 2048].rearrange("p (g x) -> p g x", x=128)
            for qq in range(8):
                src = toep_d[qq].rearrange("a (b h) x -> h (a b) x", h=16)[:, 16 * n:16 * n + 16, :]
                tok = dma(SP, t_[16 * qq:16 * qq + 16, :, :], src, f"ring{i}", slot_free[i])
            return i, t_, tok

        SP.wait(ms_all, cl_all, kk_all)
        hcL, hc2L = reg(4096, 4096), reg(8192, 4096)
        hL = reg(16384, 4096).rearrange("p (t n) -> p t n", t=2)
        UL = LT[:, 0:4096].rearrange("p (g c) -> p g c", c=32)
        VL = reg(20480, 8192).rearrange("p (k r d) -> p k r d", k=32, r=2)
        rt = rms_stat(xv, reg(12288, 2048), 0, 1e-6, *everything)
        u_tok = make_u(xv, hL, 0, abc, bbc, hcL, hc2L, UL, lambda: None, a1, a2, rt, *everything)
        u_read = (V.t, P.t, u_tok)
        S.wait(u_read)
        for sl in range(8):
            i, wt, tok = take(lambda: load(m_state_d[:, sl * 4096:(sl + 1) * 4096]))
            mv = wt.rearrange("p (d r m) -> p d r m", d=16, r=2)
            for hf in range(2):
                t, vt = v_matmuls(mv[:, 8 * hf:8 * hf + 8], UL, 16 * sl + 8 * hf, 8, VL, tok, u_tok)
            release(i, t)
        Sb = reg(4096, 16384).rearrange("p (r d g c) -> p r d g c", r=2, d=128, g=2)
        G.do(lambda e: e.memset(Sb[0:64, :, :, 1, :], 0.0), u_read)
        z0 = G.do(lambda e: e.memset(Sb[64:128, :, :, 0, :], 0.0))
        cur, nxt = stA, stB
        saved = None
        for k in range(32):
            for g2 in range(2):
                pp = slice(64 * g2, 64 * g2 + 64)
                c3 = l_swap(cur[pp, :])
                copy(S, Sb[pp, :, 0:64, g2, k], c3[:, :, 0:64], V.t, u_read)
                copy(S, Sb[pp, :, 64:128, g2, 31 - k], c3[:, :, 64:128])
            if k < 31:
                chunk_step(cur, nxt, VL[:, k].rearrange("p r d -> p (r d)"), vt, saved)
            saved = S.t
            cur, nxt = nxt, cur
        s_tok, scan_done = S.t, V.t
        Y = reg(20480, 8192).rearrange("p (k q g h) -> p k q g h", k=8, q=8, g=8)
        for q in range(8):
            i1, cl, tok1 = take(lambda: load_cl(q))
            i2, wt, tok2 = take(lambda: load_toep(q))
            for g4 in range(2):
                bi, b, fr = bank(GA)
                for j in range(4):
                    gg = 4 * g4 + j
                    gp = 8 * q + gg
                    o = b[0:64, 128 * j:128 * j + 128]
                    for d_ in range(2):
                        for r_ in range(2):
                            mm(o, Sb[:, r_, 64 * d_ + gp, :, :].rearrange("p g c -> p (g c)"), cl[:, d_, gg, r_, :],
                               d_ == 0 and r_ == 0, False, tok1, fr, s_tok, z0)
                    for g2 in range(2):
                        t = mm(b[32 * g2:32 * g2 + 32, 128 * j:128 * j + 128], UL[:, gp + 64 * g2, :],
                               wt[:, 2 * gg + g2, :], False, True, tok2, inc=(j == 3 and g2 == 1))
                bank_free[bi] = copy(V if g4 % 2 else S,
                                     Y[0:64, q, :, 4 * g4:4 * g4 + 4, :].rearrange("p q g h -> p g q h"),
                                     b[0:64, :].rearrange("p (g q h) -> p g q h", g=4, q=8), t, scan_done)
            release(i1, t)
            release(i2, t)
        y_tok = (V.t, S.t, P.t)
        zT = reg(4096, 4096).rearrange("p (k n) -> p k n", k=16)
        for k8 in range(8):
            bi, b, fr = bank(GA)
            for q in range(8):
                t = tr(b[:, 64 * q:64 * q + 64], Y[0:64, k8, q, :, :].rearrange("p g h -> p (g h)"), fr, y_tok, inc=(q == 7), k=64)
            bv = b[:, :].rearrange("p (q g c) -> p q g c", q=8, g=2)
            ends = []
            for g2 in range(2):
                ends.append(copy(S if k8 % 2 else V, zT[:, 8 * g2 + k8, :].rearrange("p (c q) -> p q c", q=8), bv[:, :, g2, :],
                                 t, y_tok))
            bank_free[bi] = tuple(ends)
        z_tok = (V.t, S.t, P.t)
        for q in range(4):
            z = reg(4096 + 1024 * q, 1024)
            e_ = reg(8192 + 1024 * q, 1024)
            tt(V, e_, z, z, MUL, z_tok)
            ts(V, e_, e_, 0.044715, 1.0, MUL, ADD, V.t)
            tt(V, e_, e_, z, MUL, V.t)
            t = act(e_, e_, ACT.Sigmoid, V.t, scale=2.0 * GELU_C)
            tt(V, z, z, e_, MUL, t)
        gelu_tok = V.t
        aN = reg(12288, 4096).rearrange("p (t n) -> p t n", t=2)

        def put_a(pnl, t2, b, t):
            return copy(S, aN[:, t2, 256 * pnl:256 * pnl + 256], b, t, z_tok)

        dense_N(zT, A["s5_w_glu_2"][0], 0, 8, put_a, gelu_tok)
        a_tok = S.t

        def put_mix(pnl, t2, b, t):
            t = act(exb, b, ACT.Sigmoid, t, V.t)
            o = aN[:, t2, 256 * pnl:256 * pnl + 256]
            tt(V, o, o, exb, MUL, t, a_tok)
            return t

        dense_N(zT, A["s5_w_glu_2"][0], 2048, 8, put_mix, gelu_tok)
        pcol = st[:, 64:80]
        tt(V, pcol, M("m2", 32), C("npost"), MUL, V.t)
        bcA = reg(24576, 2048)
        gb = bcast(bcA, pcol, V.t, z_tok)
        rt = rms_stat(aN, reg(16384, 2048), 0, 1e-6, V.t)
        tmpN = reg(4096, 4096).rearrange("p (t n) -> p t n", t=2)
        glu_read = P.t
        for t2 in range(2):
            for hf in range(2):
                cs = slice(1024 * hf, 1024 * hf + 1024)
                stt(tmpN[:, t2, cs], aN[:, t2, cs], st[:, t2:t2 + 1], bcA[:, cs], MUL, MUL, rt, gb, glu_read)
                tt(V, xv[:, t2, cs], xv[:, t2, cs], tmpN[:, t2, cs], ADD, V.t)
        rt = rms_stat(xv, reg(16384, 2048), 0, 1e-6, V.t)
        for t2 in range(2):
            ts(V, tmpN[:, t2, :], xv[:, t2, :], st[:, t2:t2 + 1], None, MUL, None, rt)
        stt(pcol, M("m2", 64), 1.0, C("mpre"), ADD, MUL, P.t, V.t)
        h2T = reg(20480, 4096).rearrange("p (k n) -> p k n", k=16)
        toks = x_transposed(tmpN, h2T, pcol, M("m2", 48), V.t)
        hid = reg(4096, 16384).rearrange("p (k n) -> p k n", k=64)
        dead = (P.t, V.t, S.t)

        def put_h(pnl, b, t):
            o = hid[:, 2 * pnl:2 * pnl + 2, :]
            r = act(o, b, ACT.Relu, t, dead)
            tt(G, o, o, o, MUL, r)
            return r

        dense_T(h2T, A["w_mlp_in_2"][0], 0, 32, put_h, *toks)
        pcol2 = st[:, 80:96]
        tt(V, pcol2, M("m2", 80), C("mpost"), MUL)
        gb = bcast(bcA, pcol2, V.t, rt)
        yN = reg(20480, 4096).rearrange("p (t n) -> p t n", t=2)
        h2_read = P.t

        def put_y(pnl, t2, b, t):
            return copy(V if t2 else S, yN[:, t2, 256 * pnl:256 * pnl + 256], b, t, h2_read)

        dense_N(hid, A["w_mlp_out_2"][0], 0, 8, put_y, G.t, kslots=4)
        rt = rms_stat(yN, reg(26624, 2048), 0, 1e-6, V.t, S.t)
        out_v = out[0].rearrange("(t p) n -> p t n", p=128)
        for t2 in range(2):
            stt(yN[:, t2, :], yN[:, t2, :], st[:, t2:t2 + 1], bcA, MUL, MUL, rt, gb)
            o_t = tt(V, xv[:, t2, :], xv[:, t2, :], yN[:, t2, :], ADD, V.t)
            o_tok = dma(SP, out_v[:, t2, :], xv[:, t2, :], "out", o_t)
        SP.wait(o_tok, V.t, S.t, P.t, G.t)

        assert not jobs and not mod.pending
        block = ctx.enter_context(nc.Block())

        @block.sync
        def _(e):
            SP.run(e)

        @block.gpsimd
        def _(e):
            G.run(e)

        @block.scalar
        def _(e):
            S.run(e)

        @block.vector
        def _(e):
            V.run(e)

        @block.tensor
        def _(e):
            P.run(e)


_INS = ["x", "c", "w_mod", "b_mod", "ln_g", "ln_b", "a_w_in", "a_w_out", "a_lam_q1", "a_lam_k1", "a_lam_q2",
        "a_lam_k2", "a_subln_g", "kv_w_mod", "kv_b_mod", "kv_w", "kv_b_f", "b_w_in", "b_w_out", "c_2", "ctx_2",
        "c_ctx_2", "w_mod_2", "b_mod_2", "norm_mix_pre_2", "norm_mix_post_2", "norm_mlp_pre_2", "norm_mlp_post_2",
        "w_mlp_in_2", "w_mlp_out_2", "s5_a_re_2", "s5_a_im_2", "s5_log_dt_2", "s5_b_re_2", "s5_b_im_2",
        "s5_c_re_2", "s5_c_im_2", "s5_d_2", "s5_w_glu_2"]


def kernel(**inputs):
    import numpy as _np
    import concourse.bacc as _bacc
    from concourse.bass_utils import run_bass_kernel_spmd as _run

    nc = _bacc.Bacc("TRN2", target_bir_lowering=False, num_devices=1)
    arrays, args = {}, {}
    for name in _INS:
        a = _np.ascontiguousarray(inputs[name])
        arrays[f"in_{name}"] = a
        args[name] = nc.dram_tensor(f"in_{name}", a.shape, mybir.dt.from_np(a.dtype), kind="ExternalInput").ap()
    out = nc.dram_tensor("out_0", (1, 256, 2048), F32, kind="ExternalOutput").ap()
    build(nc, args, out)
    r = _run(nc, [arrays], core_ids=[0])
    return r.results[0]["out_0"]
```

```python
import math
from contextlib import ExitStack

import concourse.bass as bass
from concourse import mybir

F32 = mybir.dt.float32
F32R = mybir.dt.float32r
ALU = mybir.AluOpType
ACT = mybir.ActivationFunctionType
AX = mybir.AxisListType.X
MUL, ADD, SUB, MAX, MIN = ALU.mult, ALU.add, ALU.subtract, ALU.max, ALU.min

D = 2048
KT = 16
ALPHA = 4.0 ** 0.25
LAM_INIT = 0.8 - 0.6 * math.exp(-0.3 * 0)
QK_SCALE = 128.0 ** -0.5
GELU_C = math.sqrt(2.0 / math.pi)
NSLOT = 3
SLOTF = 4096
DOUBLINGS = 10


class Queue:

    def __init__(self, sem):
        self.sem, self.n, self.items, self.seen = sem, 0, [], {}

    def wait(self, *tokens):
        for tok in tokens:
            if tok is None:
                continue
            if not isinstance(tok[-1], int):
                self.wait(*tok)
                continue
            sem, val = tok
            if self.seen.get(id(sem), 0) < val:
                self.seen[id(sem)] = val
                self.items.append(lambda e, s=sem, v=val: e.wait_ge(s, v))

    def do(self, fn, *tokens, inc=True):
        self.wait(*tokens)
        if inc:
            self.n += 1
            self.items.append(lambda e, f=fn: f(e).then_inc(self.sem, 1))
        else:
            self.items.append(fn)
        return (self.sem, self.n)

    @property
    def t(self):
        return (self.sem, self.n)

    def run(self, e):
        for f in self.items:
            f(e)


def pipeline(n, stages):
    for t in range(n + len(stages) - 1):
        for s in range(len(stages) - 1, -1, -1):
            if 0 <= t - s < n:
                stages[s](t - s)


def build(nc, A, out):
    with ExitStack() as ctx:
        sem = lambda name: ctx.enter_context(nc.semaphore(name))
        P, V, S, G = (Queue(sem(n)) for n in ("s_pe", "s_dve", "s_act", "s_pool"))
        SP = Queue(sem("s_sp"))

        dma_count = {}

        def dma(q, dst, src, s, *tokens):
            q.wait(*tokens)
            dma_count[s] = dma_count.get(s, 0) + 16
            q.items.append(lambda e: e.dma_start(dst, src).then_inc(sems[s], 16))
            return (sems[s], dma_count[s])

        sems = {n: sem("d_" + n) for n in (
            ["rows", "x", "ctx", "lam", "sub", "b", "c", "ar", "ai", "dt", "hc", "ms", "cl0", "cl1", "kk", "out", "bc0", "bc1", "zf", "qkv", "sd"]
            + ["ringx"] + [f"st{i}" for i in range(4)] + ["at0", "at1", "at3", "p0", "p1", "p2", "p3", "x1"]
            + [f"ring{i}" for i in range(NSLOT)])}

        sb = lambda name, n: ctx.enter_context(nc.sbuf_tensor(name, [128, n], F32))
        ring = sb("ring", NSLOT * SLOTF)
        sm = sb("sm", 16 * 128)
        ident = sb("ident", 128)
        cols = sb("cols", 512)
        MODC = sb("MODC", 416)
        st = sb("st", 256)
        ACC = sb("ACC", 512)
        first = ctx.enter_context(ExitStack())
        sb1 = lambda name, n: first.enter_context(nc.sbuf_tensor(name, [128, n], F32))
        AR = sb1("arena", 28672)
        LT = sb1("LT", 2 * 128 * 17)
        L1, L2 = LT[:, 0:2304], LT[:, 2304:4352]
        MSB = sb1("MSB", 2048)
        BBD = sb1("BBD", 512)
        SUBG = sb1("SUBG", 256)
        SF = sb1("SF", 256 * 2)
        LR8 = sb1("LR8", 256)
        LS8 = sb1("LS8", 256)
        banks = [ctx.enter_context(nc.psum_tensor(f"bank{i}", [128, 512], F32)) for i in range(8)]

        m_state_d = nc.dram_tensor("m_state", [128, 128 * 256], F32).ap()
        cl_d = nc.dram_tensor("cl_out", [128, 128 * 256], F32).ap()
        proj_d = [nc.dram_tensor(f"proj{i}", [128, 4096], F32).ap() for i in range(4)]
        toep_d = nc.dram_tensor("toep", [8, 16, 128, 128], F32).ap()

        def reg(off, n):
            return AR[:, off:off + n]

        slots = [{"ap": ring[:, i * SLOTF:(i + 1) * SLOTF], "sem": f"ring{i}", "free": None} for i in range(NSLOT)]
        turn_of = {"n": 0}

        def next_slot():
            sl = slots[turn_of["n"] % len(slots)]
            turn_of["n"] += 1
            return sl

        def add_slot(ap, *tokens):
            k = turn_of["n"] % len(slots)
            slots[:] = slots[k:] + slots[:k]
            slots.insert(0, {"ap": ap, "sem": "ringx", "free": tokens})
            turn_of["n"] = 0

        def drop_slot():
            k = turn_of["n"] % len(slots)
            slots[:] = slots[k:] + slots[:k]
            turn_of["n"] = 0
            x_ = next(sl for sl in slots if sl["sem"] == "ringx")
            slots.remove(x_)
            return x_["free"]

        def load(src):
            sl = next_slot()
            n = 1
            for d_ in src.shape[1:]:
                n *= d_
            tv = sl["ap"][:, 0:n]
            if len(src.shape) == 3:
                tv = tv.rearrange("p (a b) -> p a b", a=src.shape[1])
            return sl, tv, dma(SP, tv, src, sl["sem"], sl["free"])

        def load_w(W, k0, n0, n=256):
            return load(W[k0:k0 + 2048, n0:n0 + n].rearrange("(k p) n -> p k n", p=128))

        def take(fn):
            return fn()

        def release(i, tok):
            i["free"] = tok

        bank_free = [None] * 8
        turn = {}

        def bank(group):
            k = turn.get(group, 0)
            turn[group] = k + 1
            i = group[k % len(group)]
            return i, banks[i], bank_free[i]

        GA = (0, 1, 2)
        GB = (3, 4)
        GC = (5, 6)

        def mm(o, l, r, start, stop, *w, inc=False):
            return P.do(lambda e: e.matmul(o, l, r, start=start, stop=stop, skip_group_check=True), *w, inc=inc)

        def tr(o, i, *w, inc=False, k=128):
            idn = ident[0:k, 0:k]
            return P.do(lambda e: e.transpose(o, i, idn), *w, inc=inc)

        def tt(q, o, a, b, op, *w):
            return q.do(lambda e: e.tensor_tensor(o, a, b, op), *w)

        def ts(q, o, a, s1, s2, o1, o2, *w):
            if s2 is None:
                return q.do(lambda e: e.tensor_scalar(o, a, s1, None, o1), *w)
            return q.do(lambda e: e.tensor_scalar(o, a, s1, s2, o1, o2), *w)

        def stt(o, a, s, b, o1, o2, *w):
            return V.do(lambda e: e.scalar_tensor_tensor(out=o, in0=a, scalar=s, in1=b, op0=o1, op1=o2), *w)

        def act(o, i, f, *w, **kw):
            return S.do(lambda e: e.activation(o, i, f, **kw), *w)

        def recip(o, a, *w):
            return V.do(lambda e: e.reciprocal(o, a), *w)

        def copy(q, o, a, *w):
            if q is S:
                return S.do(lambda e: e.copy(o, a), *w)
            return q.do(lambda e: e.tensor_copy(o, a), *w)

        def rsqrt(o, v, tmp, *w):
            a = act(tmp, v, ACT.Ln, *w)
            b = act(o, tmp, ACT.Exp, a, scale=-0.5)
            tt(V, tmp, o, o, MUL, b)
            tt(V, tmp, tmp, v, MUL, V.t)
            ts(V, tmp, tmp, -0.5, 1.5, MUL, ADD, V.t)
            return tt(V, o, o, tmp, MUL, V.t)

        G.do(lambda e: e.memset(ident[:, :], 0.0))
        id_tok = G.do(lambda e: e.affine_select(out=ident[:, :], in_=ident[:, :], compare_op=ALU.not_equal, fill=1.0,
                                                base=0, pattern=[[-1, 128]], channel_multiplier=1), G.t)

        vecs = [("c", A["c"].rearrange("a (r n) -> (a r) n", n=128), 16),
                ("c2", A["c_2"].rearrange("a (r n) -> (a r) n", n=128), 16),
                ("cc", A["c_ctx_2"].rearrange("(r n) -> r n", n=128), 16),
                ("bm", A["b_mod"].rearrange("l (r n) -> (l r) n", n=128), 96),
                ("bkv", A["kv_b_mod"].rearrange("(r n) -> r n", n=128), 32),
                ("bm2", A["b_mod_2"].rearrange("l (r n) -> (l r) n", n=128), 96),
                ("npre", A["norm_mix_pre_2"].rearrange("l (r n) -> (l r) n", n=128), 16),
                ("npost", A["norm_mix_post_2"].rearrange("l (r n) -> (l r) n", n=128), 16),
                ("mpre", A["norm_mlp_pre_2"].rearrange("l (r n) -> (l r) n", n=128), 16),
                ("mpost", A["norm_mlp_post_2"].rearrange("l (r n) -> (l r) n", n=128), 16)]
        col = {}
        pos = 0
        rows_base = 0
        for name, src, n in vecs:
            col[name] = pos
            r = 0
            while r < n:
                tile, p0 = (pos + r) // 128, (pos + r) % 128
                m = min(n - r, 128 - p0)
                rows_tok = dma(SP, reg(rows_base + tile * 128, 128)[p0:p0 + m, :], src[r:r + m, :], "rows")
                r += m
            pos += n
        col["sd"] = pos
        sd_src = A["s5_d_2"][0].rearrange("(g a m h) -> g a m h", g=2, a=16, m=4)
        tile, p0 = pos // 128, pos % 128
        assert p0 + 16 <= 128
        for g2 in range(2):
            sd_dst = reg(rows_base + tile * 128, 128)[p0:p0 + 16, :].rearrange("p (m g h) -> p m g h", m=4, g=2)
            rows_tok = dma(SP, sd_dst[:, :, g2, :], sd_src[g2], "rows")
        pos += 16
        ncol = pos
        for tile in range((ncol + 127) // 128):
            m = min(128, ncol - tile * 128)
            i, b, fr = bank(GA)
            t = tr(b[:, 0:m], reg(rows_base + tile * 128, 128)[0:m, :], rows_tok, id_tok, fr, inc=True, k=m)
            bank_free[i] = copy(V, cols[:, tile * 128:tile * 128 + m], b[:, 0:m], t)
        rows_read = P.t

        def C(name, a=0, n=16):
            return cols[:, col[name] + a:col[name] + a + n]

        cact = sm[:, 15 * 128:15 * 128 + 48]
        tmp = sm[:, 15 * 128 + 48:15 * 128 + 96]
        ts(V, tmp, C("c", 0, 48), -80.0, None, MAX, None, V.t)
        t = act(tmp, tmp, ACT.Exp, V.t, scale=-1.0)
        ts(V, tmp, tmp, 1.0, None, ADD, None, t)
        recip(tmp, tmp, V.t)
        cact_tok = tt(V, cact, tmp, C("c", 0, 48), MUL, V.t)
        cpair = cact[:, 16:48].rearrange("p (v k) -> p k v", v=2)

        MB0 = banks[7]
        m_off = {"m2": 0, "m2x": 96, "m0": 128, "kv": 176, "m1": 208}
        mod_tok = {}
        ones = sm[:, 14 * 128:14 * 128 + 1]
        ones_tok = V.do(lambda e: e.memset(ones, 1.0))
        acc_free = [None, None]
        wm, wm2 = A["w_mod"], A["w_mod_2"][0]
        groups = [("m0s", wm[0], "m0", 0, 32, "bm", 0), ("m2a", wm2, "m2", 0, 32, "bm2", 0),
                  ("m0g", wm[0], "m0", 32, 48, "bm", 0), ("m1s", wm[1], "m1", 0, 32, "bm", 48),
                  ("kv", A["kv_w_mod"], "kv", 0, 32, "bkv", 0), ("m1g", wm[1], "m1", 32, 48, "bm", 48), ("m2b", wm2, "m2", 32, 80, "bm2", 0),
                  ("m2c", wm2, "m2", 80, 96, "bm2", 0)]
        jobs = [(g, nt) for g in groups for nt in range(g[3], g[4], 2)]

        def mod(n=1, dve=False):
            for _ in range(n):
                mod_sums()
                if not jobs:
                    return
                (name, W, dst, nt0, nt1, bias, boff), nt = jobs.pop(0)
                base = m_off[dst]
                c0 = 0 if dst in ("m0", "m1") or dst == "kv" else 16
                i, w, tok = take(lambda: load_w(W, 0, 128 * nt))
                if name == "m2a" and dve:
                    for k in range(KT):
                        for v in range(2):
                            o_, c_ = ACC[:, 256 * v:256 * v + 256], cpair[:, k, v:v + 1]
                            if k == 0:
                                ts(V, o_, w[:, k, :], c_, None, MUL, None, tok, acc_free, cact_tok, V.t)
                            else:
                                stt(o_, w[:, k, :], c_, o_, MUL, ADD, V.t)
                    release(i, V.t)
                    mod.pending.append(("pair", None, nt, V.t))
                elif name != "m2a" and dve:
                    h = mod.turn % 2
                    mod.turn += 1
                    a = mod.room[h]
                    ends = [None] * len(a)
                    for k in range(KT):
                        c_ = k % len(a)
                        if k < len(a):
                            ends[c_] = ts(V, a[c_], w[:, k, :], cact[:, c0 + k:c0 + k + 1], None, MUL, None, tok,
                                          acc_free[h], cact_tok)
                        else:
                            ends[c_] = stt(a[c_], w[:, k, :], cact[:, c0 + k:c0 + k + 1], a[c_], MUL, ADD, ends[c_])
                    release(i, V.t)
                    mod.pending.append((h, a, base + nt, V.t))
                else:
                    for j in range(2):
                        for k in range(KT):
                            if name == "m2a":
                                o, r = MB0[:, 256 + 2 * (nt + j):258 + 2 * (nt + j)], cpair[:, k, :]
                            else:
                                o, r = MB0[:, base + nt + j:base + nt + j + 1], cact[:, c0 + k:c0 + k + 1]
                            t = mm(o, w[:, k, j * 128:(j + 1) * 128], r, k == 0, k == KT - 1, tok, cact_tok,
                                   inc=(j == 1 and k == KT - 1))
                    release(i, t)
                if nt + 2 == nt1:
                    mod_sums()
                    if name == "m2a":
                        pr = MB0[:, 256:320].rearrange("p (n v) -> p v n", v=2)
                        tt(V, MODC[:, 0:32], pr[:, 0, :], C(bias, 0, 32), ADD, P.t)
                        tt(V, MODC[:, 96:128], pr[:, 1, :], C(bias, 0, 32), ADD)
                    else:
                        tt(V, MODC[:, base + nt0:base + nt1], MB0[:, base + nt0:base + nt1],
                           C(bias, boff + nt0, nt1 - nt0), ADD, P.t)
                    mod_tok[name] = V.t
                    P.wait(V.t)

        mod.turn = 0
        mod.pending = []
        mod.room = [[reg(4096 + 512 * h, 256), reg(4096 + 512 * h + 256, 256)] for h in range(2)]

        def mod_sums():
            for h, a, o, at in mod.pending:
                if h == "pair":
                    for j in range(2):
                        for v in range(2):
                            c_ = 256 + 2 * (o + j) + v
                            t = mm(MB0[:, c_:c_ + 1], ACC[:, 256 * v + 128 * j:256 * v + 128 * j + 128], ones, True,
                                   True, at, ones_tok, inc=(j == 1 and v == 1))
                    acc_free[:] = [t, t]
                    continue
                for j in range(2):
                    for n, x_ in enumerate(a):
                        acc_free[h] = mm(MB0[:, o + j:o + j + 1], x_[:, 128 * j:128 * j + 128], ones, n == 0,
                                         n == len(a) - 1, at, ones_tok, inc=(n == len(a) - 1))
            mod.pending = []


        def mod_until(name, **kw):
            while name not in mod_tok:
                mod(1, **kw)

        def M(name, a, n=16):
            return MODC[:, m_off[name] + a:m_off[name] + a + n]

        def bcast(dst, colap, *w, group=(5, 6)):
            for q in range(4):
                i, b, fr = bank(group)
                for j in range(4):
                    k = 4 * q + j
                    t = mm(b[:, 128 * j:128 * j + 128], colap[:, k:k + 1].to_broadcast([128, 128]), ident[:, :],
                           True, True, fr, *w, inc=(j == 3))
                bank_free[i] = copy(S, dst[:, 512 * q:512 * q + 512], b[:, :], t, *w)
            return bank_free[i]

        def x_transposed(src, dst, acol_, bcol_, *w, each=None):
            for k2 in range(8):
                i, b, fr = bank(GA)
                for j in range(2):
                    for t2 in range(2):
                        k = 2 * k2 + j
                        t = tr(b[:, 256 * j + 128 * t2:256 * j + 128 * t2 + 128], src[:, t2, 128 * k:128 * k + 128],
                               fr, *w, inc=(j == 1 and t2 == 1))
                for j in range(2):
                    k = 2 * k2 + j
                    if k2 % 2 == 0:
                        tok = ts(V, dst[:, k, :], b[:, 256 * j:256 * j + 256], acol_[:, k:k + 1], bcol_[:, k:k + 1],
                                 MUL, ADD, t, *w)
                    else:
                        tok2 = act(dst[:, k, :], b[:, 256 * j:256 * j + 256], ACT.Identity, t, *w,
                                   scale=acol_[:, k:k + 1], bias=bcol_[:, k:k + 1])
                bank_free[i] = V.t if k2 % 2 == 0 else S.t
                if each:
                    each(k2, V.t, S.t)
            return tok, tok2

        R1, R2, R3, R4, R5 = 0, 4096, 8192, 12288, 16384

        def rms_stat(xv, junk, slot, eps, *w):
            for t2 in range(2):
                a = act(junk, xv[:, t2, :], ACT.Square, *w, S.t, accum_out=st[:, slot + 2 + t2:slot + 3 + t2])
            ts(V, st[:, slot + 2:slot + 4], st[:, slot + 2:slot + 4], 1.0 / D, eps, MUL, ADD, S.t)
            return rsqrt(st[:, slot:slot + 2], st[:, slot + 2:slot + 4], st[:, slot + 4:slot + 6], V.t)

        def make_u(xv, hv, rslot, abc, bbc, hc, hc2, U, step, *w):
            pe, pm, arrived, late = [None, None], [None, None], {}, []

            def rows(pc):
                cs = slice(256 * pc, 256 * pc + 256)
                hb = hc[:, 2048 * (pc % 2):2048 * (pc % 2) + 2048].rearrange("p (q n) -> p q n", q=8)
                for t2 in range(2):
                    stt(hv[:, t2, cs], xv[:, t2, cs], st[:, rslot + t2:rslot + t2 + 1], abc[:, cs], MUL, MUL, *w)
                for t2 in range(2):
                    tt(V, hv[:, t2, cs], hv[:, t2, cs], bbc[:, cs], ADD, V.t)
                for t2 in range(2):
                    arrived[pc] = dma(S, hb[16 * t2:16 * t2 + 16, :, :], hv[:, t2, cs], f"at{pc % 2}", V.t, pm[pc % 2])

            def turn_rows(pc):
                tok = arrived[pc]
                hb = hc[:, 2048 * (pc % 2):2048 * (pc % 2) + 2048].rearrange("p (q n) -> p q n", q=8)
                h2 = hc2[:, 2048 * (pc % 2):2048 * (pc % 2) + 2048].rearrange("p (g q h) -> p g q h", g=16, q=8)
                sv = hb[0:32, :, :].rearrange("p q (g h) -> p g q h", h=16)
                c1 = copy(V, h2[0:32, 0:8, :, :], sv[:, 0:8], tok, pe[pc % 2], *w)
                c2 = copy(S, h2[0:32, 8:16, :, :], sv[:, 8:16], tok, pe[pc % 2], *w)
                pm[pc % 2] = (c1, c2)
                if late:
                    put_u()
                if pc % 2:
                    step(pc // 2)
                i, b, fr = bank(GB)
                for j in range(16):
                    t = tr(b[:, 32 * j:32 * j + 32], h2[0:32, j, :, :].rearrange("p q h -> p (q h)"), c1, c2, fr,
                           inc=(j == 15), k=32)
                pe[pc % 2] = t
                late.append((i, b, pc, t))

            def put_u():
                i, b, pc, t = late.pop(0)
                bank_free[i] = copy(S, U[:, 16 * pc:16 * pc + 16, :], b[:, :].rearrange("p (g c) -> p g c", g=16), t, *w)

            rows(0)
            for pc in range(8):
                if pc < 7:
                    rows(pc + 1)
                turn_rows(pc)
            put_u()
            return S.t

        def by_pair(dst, src, s_, q_, *w):
            n = dst.shape[1] // 2
            for d_ in range(2):
                for g2 in range(2):
                    tok = dma(q_, dst[64 * d_:64 * d_ + 64, n * g2:n * g2 + n], src[d_, 64 * g2:64 * g2 + 64], s_, *w)
            return tok

        hT = reg(24576, 4096).rearrange("p (k n) -> p k n", k=16)
        x0 = reg(R4, 4096).rearrange("p (t n) -> p t n", t=2)
        x_tok = dma(S, x0, A["x"][0].rearrange("(t p) n -> p t n", p=128), "x")
        braw = reg(R5, 4096).rearrange("p (r g q h) -> p r g q h", r=2, g=2, h=16)
        craw = reg(R5 + 4096, 4096).rearrange("p (r g h q) -> p r g h q", r=2, g=2, h=16)
        smt = [sm[:, i * 128:(i + 1) * 128] for i in range(15)]
        are, aim, dtb, zr, zi, wr, wi, ta, tb, tc = smt[:10]
        a_re_tok = by_pair(are, A["s5_a_re_2"][0], "ar", G)
        a_im_tok = by_pair(aim, A["s5_a_im_2"][0], "ai", G)
        dt_tok = by_pair(tc[:, 0:2], A["s5_log_dt_2"][0].unsqueeze(2), "dt", G)
        tcr, tci, t1r, t1i = smt[0], smt[1], smt[2], smt[3]
        L1v = L1[:, :].rearrange("p (r d t) -> p r d t", r=2, t=9)
        L2v = L2[:, :].rearrange("p (r d t) -> p r d t", r=2, t=8)

        def discretise():
            t = act(tc[:, 2:4], tc[:, 0:2], ACT.Exp, dt_tok)
            sc0 = 2.0 ** -DOUBLINGS
            for g in range(2):
                h = slice(g * 64, g * 64 + 64)
                ts(V, zr[:, h], are[:, h], tc[:, 2 + g:3 + g], sc0, MUL, MUL, t, a_re_tok, a_im_tok)
                ts(V, zi[:, h], aim[:, h], tc[:, 2 + g:3 + g], sc0, MUL, MUL)
            ts(V, wr, zr, 1.0 / 6, 1.0, MUL, ADD, V.t)
            ts(V, wi, zi, 1.0 / 6, None, MUL, None)
            for n in (5, 4, 3, 2):
                tt(V, ta, zr, wr, MUL, V.t)
                tt(V, tb, zi, wi, MUL)
                tt(V, ta, ta, tb, SUB, V.t)
                tt(V, tb, zr, wi, MUL, V.t)
                tt(V, wi, zi, wr, MUL, V.t)
                tt(V, tb, tb, wi, ADD, V.t)
                ts(V, wr, ta, 1.0 / n, 1.0, MUL, ADD, V.t)
                ts(V, wi, tb, 1.0 / n, None, MUL, None)
                yield
            tt(V, ta, zr, wr, MUL, V.t)
            tt(V, tb, zi, wi, MUL)
            tt(V, ta, ta, tb, SUB, V.t)
            tt(V, tb, zr, wi, MUL, V.t)
            tt(V, wi, zi, wr, MUL, V.t)
            tt(V, wi, tb, wi, ADD, V.t)
            copy(V, wr, ta, V.t)
            for _ in range(DOUBLINGS):
                stt(ta, wr, 2.0, wr, ADD, MUL, V.t)
                tt(V, tb, wi, wi, MUL)
                stt(wi, wr, 1.0, wi, ADD, MUL, V.t)
                tt(V, wr, ta, tb, SUB, V.t)
                ts(V, wi, wi, 2.0, None, MUL, None, V.t)
                yield
            cr, ci, den, lbr, lbi, pr_, pi_ = smt[8], smt[9], smt[10], smt[11], smt[12], smt[13], smt[14]
            tt(V, den, are, are, MUL, V.t)
            tt(V, zr, aim, aim, MUL)
            tt(V, den, den, zr, ADD, V.t)
            recip(den, den, V.t)
            tt(V, ta, wr, are, MUL, V.t)
            tt(V, zr, wi, aim, MUL)
            tt(V, ta, ta, zr, ADD, V.t)
            tt(V, cr, ta, den, MUL, V.t)
            tt(V, ta, wi, are, MUL, V.t)
            tt(V, zr, wr, aim, MUL)
            tt(V, ta, ta, zr, SUB, V.t)
            tt(V, ci, ta, den, MUL, V.t)
            ts(V, lbr, wr, 1.0, None, ADD, None, V.t)
            copy(V, lbi, wi)
            yield
            i, b, fr = bank(GA)
            for j, s_ in enumerate((cr, ci, lbr, lbi)):
                t = tr(b[:, 128 * j:128 * j + 128], s_, V.t, fr, id_tok, inc=(j == 3))
            bank_free[i] = copy(V, sm[:, 0:512], b[:, :], t)

            curr, curi, nxr, nxi = smt[4], smt[5], smt[6], smt[7]
            pa, pb_ = smt[10], smt[11]
            V.do(lambda e: e.memset(curr, 1.0), V.t)
            V.do(lambda e: e.memset(curi, 0.0), V.t)
            for tau in range(9):
                for r_, cur in enumerate((curr, curi)):
                    copy(V, L1v[:, r_, 0:64, tau], cur[:, 0:64], V.t)
                    copy(V, L1v[:, r_, 64:128, 8 - tau], cur[:, 64:128])
                    if tau < 8:
                        copy(V, L2v[:, r_, 0:64, 7 - tau], cur[:, 0:64])
                        copy(V, L2v[:, r_, 64:128, tau], cur[:, 64:128])
                if tau == 8:
                    copy(V, LR8[:, 0:128], curr)
                    copy(V, LR8[:, 128:256], curr)
                    ts(V, LS8[:, 0:128], curi, -1.0, None, MUL, None)
                    copy(V, LS8[:, 128:256], curi)
                    break
                tt(V, pa, curr, t1r, MUL, V.t)
                tt(V, pb_, curi, t1i, MUL)
                tt(V, nxr, pa, pb_, SUB, V.t)
                tt(V, pa, curr, t1i, MUL, V.t)
                tt(V, pb_, curi, t1r, MUL)
                tt(V, nxi, pa, pb_, ADD, V.t)
                curr, nxr = nxr, curr
                curi, nxi = nxi, curi
                yield

        for r_, nm in enumerate(("re", "im")):
            b_tok = by_pair(reg(R5 + 2048 * r_, 2048), A[f"s5_b_{nm}_2"][0].rearrange("d g p h -> d g (p h)"), "b", G)
            c_tok = by_pair(reg(R5 + 4096 + 2048 * r_, 2048), A[f"s5_c_{nm}_2"][0].rearrange("d g h p -> d g (h p)"),
                            "c", G)
        pieces = discretise()
        for i in range(16):
            mod(1, dve=(i % 4 != 2))
            if i > 1:
                next(pieces, None)
                next(pieces, None)
        for _ in pieces:
            pass
        L_tok = V.t
        mod.room = [[ACC[:, 0:256]], [ACC[:, 256:512]]]
        acc_free[:] = [None, None]
        sc1 = st[:, 110:126]
        ts(V, sc1, M("m0", 16), 1.0, None, ADD, None, mod_tok["m0s"])
        hT_toks = x_transposed(x0, hT, sc1, M("m0", 0), x_tok, V.t)

        def to_state(raw_fn, dst, tok, *w):
            for r_ in range(2):
                for h4 in range(4):
                    i, b, fr = bank(GA)
                    for j in range(4):
                        for g2 in range(2):
                            t = mm(b[64 * g2:64 * g2 + 64, 128 * j:128 * j + 128], raw_fn(r_, g2, 4 * h4 + j),
                                   ident[:, :], True, True, tok, fr, inc=(j == 3 and g2 == 1))
                    bank_free[i] = copy(S, dst[:, r_, :, 4 * h4:4 * h4 + 4].rearrange("p d h -> p h d"),
                                        b[:, :].rearrange("p (h d) -> p h d", h=4), t, *w)
            return bank_free[i]


        bT = reg(R3, 4096).rearrange("p (r d h) -> p r d h", r=2, h=16)
        Bb = reg(R2, 4096).rearrange("p (r d h) -> p r d h", r=2, h=16)
        cT = reg(R4, 4096).rearrange("p (r d h) -> p r d h", r=2, h=16)
        bT_tok = to_state(lambda r_, g2, h: braw[:, r_, g2, :, h], bT, b_tok)
        cT_tok = to_state(lambda r_, g2, h: craw[:, r_, g2, h, :], cT, c_tok, hT_toks)
        tmpb = reg(R5, 2048).rearrange("p (d h) -> p d h", h=16)

        def bcw(x):
            return x.unsqueeze(2).to_broadcast([128, 128, 16])

        tt(V, tmpb, bT[:, 1], bcw(tci), MUL, bT_tok, P.t)
        tt(V, Bb[:, 0], bT[:, 0], bcw(tcr), MUL)
        tt(V, Bb[:, 0], Bb[:, 0], tmpb, SUB, V.t)
        tt(V, tmpb, bT[:, 0], bcw(tci), MUL, V.t)
        tt(V, Bb[:, 1], bT[:, 1], bcw(tcr), MUL)
        tt(V, Bb[:, 1], Bb[:, 1], tmpb, ADD, V.t)
        Bb_tok = V.t
        stage = {"bufs": [MSB[:, 512 * i:512 * i + 512] for i in range(3)], "n": 0, "free": [None] * 4,
                 "after": None}
        proj_tok = [None] * 4
        win = A["a_w_in"][0]
        sub_tok = dma(G, SUBG[:, :], A["a_subln_g"].to_broadcast([128, 256]), "sub")
        ts(V, SUBG[:, :], SUBG[:, :], 1.0 - LAM_INIT, None, MUL, None, sub_tok)
        subg_tok = V.t
        gx = ACC

        def project(pnl):
            which, loc = pnl // 8, pnl % 8
            sbi = stage["n"] % len(stage["bufs"])
            stage["n"] += 1
            buf = stage["bufs"][sbi]
            i, wt, tok = take(lambda: load_w(win, 0, 256 * pnl))
            if which < 2:
                bi, b, fr = bank(GA)
                for j in range(2):
                    for k in range(KT):
                        t = mm(b[:, 256 * j:256 * j + 256], wt[:, k, 128 * j:128 * j + 128], hT[:, k, :],
                               k == 0, k == KT - 1, tok, fr, hT_toks, inc=(j == 1 and k == KT - 1))
                release(i, t)
                if which == 0:
                    tok = S.do(lambda e: e.mul(buf, b[:, :], QK_SCALE), t, stage["free"][sbi], stage["after"])
                else:
                    tok = copy(S, buf, b[:, :], t, stage["free"][sbi], stage["after"])
                bank_free[bi] = tok
                dst = proj_d[which][:, 512 * loc:512 * loc + 512]
                stage["free"][sbi] = proj_tok[which] = dma(G, dst, buf, f"st{sbi}", tok)
            else:
                bi, b, fr = bank(GA)
                for t2 in range(2):
                    for k in range(KT):
                        t = mm(b[:, 256 * t2:256 * t2 + 256], hT[:, k, 128 * t2:128 * t2 + 128], wt[:, k, :],
                               k == 0, k == KT - 1, tok, fr, hT_toks, inc=(t2 == 1 and k == KT - 1))
                release(i, t)
                if which == 2:
                    tok = copy(S, buf, b[:, :], t, stage["free"][sbi], stage["after"])
                else:
                    gb_ = GXB
                    t = act(gb_, b[:, :], ACT.Sigmoid, t, V.t)
                    g2v = gb_.rearrange("p (t n) -> p t n", t=2)
                    tt(V, g2v, g2v, SUBG[:, :].unsqueeze(1).to_broadcast([128, 2, 256]), MUL, t, subg_tok)
                    tok = tt(V, buf, b[:, :], gb_, MUL, V.t, stage["free"][sbi], stage["after"])
                bank_free[bi] = tok
                dst = proj_d[which].rearrange("p (t n) -> p t n", t=2)[:, :, 256 * loc:256 * loc + 256]
                stage["free"][sbi] = proj_tok[which] = dma(G, dst, buf.rearrange("p (t n) -> p t n", t=2),
                                                           f"st{sbi}", tok)

        GXB = MSB[:, 1536:2048]
        project(0)
        project(1)


        def cmul(xr, xi, Lv, T, d0, outr, outi, t1, t2, neg, w_r, w_i):
            o4 = lambda y: y.rearrange("p (d t h) -> p d t h", d=8, t=T)
            for k in range(0, 8, 8):
                X = lambda x: x[:, d0:d0 + 8, :].unsqueeze(2).to_broadcast([128, 8, T, 16])
                Lb = lambda r_: Lv[:, r_, d0:d0 + 8, :].unsqueeze(3).to_broadcast([128, 8, T, 16])
                tt(V, o4(outr), X(xr), Lb(0), MUL, *w_r)
                tt(V, o4(t1), X(xi), Lb(1), MUL, V.t)
                tt(V, outr, outr, t1, SUB, V.t)
                r_tok = V.t
                tt(V, o4(outi), X(xr), Lb(1), MUL, *w_i)
                tt(V, o4(t2), X(xi), Lb(0), MUL, V.t)
                if neg:
                    stt(outi, outi, -1.0, t2, MUL, SUB, V.t)
                else:
                    tt(V, outi, outi, t2, ADD, V.t)
                return r_tok, V.t

        def v_matmuls(mv, Uv, d0, dst, base_tok, *w):
            i, b, fr = bank(GA + GB + GC)
            bv = b[:, :].rearrange("p (d r c) -> p d r c", r=2, c=32)
            for dd in range(8):
                gp = (d0 + dd) % 64
                for r_ in range(2):
                    for g2 in range(2):
                        t = mm(bv[64 * g2:64 * g2 + 64, dd, r_, :], mv[:, dd, r_, 64 * g2:64 * g2 + 64],
                               Uv[:, gp + 64 * g2, :], True, True, fr, base_tok, *w,
                               inc=(dd == 7 and r_ == 1 and g2 == 1))
            dv = dst if d0 < 64 else dst[:, ::-1]
            for r_ in range(2):
                bank_free[i] = copy(S, dv[:, :, r_, :].rearrange("p k d -> p d k"), bv[:, :, r_, :], t)
            return t, bank_free[i]

        KK = reg(R1, 3840).rearrange("p (a j h) -> p a j h", a=16, j=15)
        mask16 = smt[0]
        V.do(lambda e: e.tensor_reduce(mask16[:, 0:16], ident[:, :].rearrange("p (b h) -> p h b", b=8), AX, ADD),
             V.t, id_tok)
        tt(V, KK[:, :, 7, :], C("sd").unsqueeze(2).to_broadcast([128, 16, 16]),
           mask16[:, 0:16].unsqueeze(1).to_broadcast([128, 16, 16]), MUL, V.t, rows_read)
        cl_bufs = [(reg(R3, 1152), reg(R3 + 1152, 1152)), (reg(R5, 1152), reg(R5 + 1152, 1152))]
        ct1, ct2 = reg(R3 + 2304, 1152), reg(R5 + 2304, 1152)
        bd = BBD[:, :].rearrange("p (d r m) -> p d r m", d=8, r=2)
        bd_zero = G.do(lambda e: e.memset(BBD[:, :], 0.0))

        cl_dma = None
        kk_pe = None
        pend = {}

        def cl_make(ch):
            d0 = 8 * ch
            for g2 in range(2):
                for r_ in range(2):
                    tok = copy(G, bd[64 * g2:64 * g2 + 64, :, r_, 16 * g2:16 * g2 + 16],
                               Bb[64 * g2:64 * g2 + 64, r_, d0:d0 + 8, :], bd_zero, Bb_tok, pend.get("kk_pe"))
            clr, cli = cl_bufs[ch % 2]
            freed = (cT_tok, Bb_tok, pend.get("kk_pe"), pend.get(("cl", ch - 2)))
            r_tok, i_tok = cmul(cT[:, 0], cT[:, 1], L1v, 9, d0, clr, cli, ct1, ct2, True, freed, ())
            oo = 16 if ch < 8 else 0
            clrv = clr.rearrange("p (d x) -> p d x", d=8)
            cliv = cli.rearrange("p (d x) -> p d x", d=8)
            dst = cl_d[:, d0 * 256:d0 * 256 + 2048].rearrange("p (d r x) -> p d r x", d=8, r=2)
            dma(G, dst[:, :, 0, :], clrv[:, :, oo:oo + 128], f"cl{ch % 2}", i_tok)
            pend["cl", ch] = dma(G, dst[:, :, 1, :], cliv[:, :, oo:oo + 128], f"cl{ch % 2}", i_tok)
            return tok, i_tok

        def cl_kernels(ch, bd_tok, i_tok):
            d0 = 8 * ch
            clrv, cliv = (y.rearrange("p (d x) -> p d x", d=8) for y in cl_bufs[ch % 2])
            fwd = ch < 8
            ko = 0 if fwd else 16
            i, b, fr = bank(GB)
            bv = b[:, 0:256].rearrange("p (a x) -> p a x", a=2)
            for a in range(2):
                for m in range(4):
                    dd = 4 * a + m
                    o = bv[32 * m:32 * m + 32, a, :]
                    mm(o, bd[:, dd, 0, :], clrv[:, dd, ko:ko + 128], True, False, bd_tok, i_tok, fr)
                    kk_pe = mm(o, bd[:, dd, 1, :], cliv[:, dd, ko:ko + 128], False, True, inc=(dd == 7))
            pend["kk_pe"] = kk_pe
            a0 = (d0 % 64) // 4
            kb = bv.rearrange("p a (t h) -> p a t h", t=8)
            if fwd:
                copy(V, KK[:, a0:a0 + 2, 8:15, :], kb[:, :, 1:8, :], kk_pe)
                kz = kb[:, :, 0, :]
            else:
                copy(V, KK[:, a0:a0 + 2, 0:7, :], kb[:, :, 0:7, :], kk_pe)
                kz = kb[:, :, 7, :]
            bank_free[i] = tt(V, KK[:, a0:a0 + 2, 7, :], KK[:, a0:a0 + 2, 7, :], kz, ADD, V.t)

        add_slot(reg(R5 + 4096, 4096), cT_tok, P.t)
        for ch in range(16):
            args_ = cl_make(ch)
            if ch == 15:
                ctxv = reg(R4, 4096).rearrange("p (t n) -> p t n", t=2)
                ctx_tok = dma(G, ctxv, A["ctx_2"][0].rearrange("(t p) n -> p t n", p=128), "ctx", V.t)
            project(ch + 2)
            mod(1, dve=ch % 4 != 3)
            cl_kernels(ch, *args_)
            if ch > 8 and ch % 2:
                a_ = 2 * (ch - 9)
                for q in range(8):
                    kk_dma = dma(G, toep_d[q, a_:a_ + 4].rearrange("a p x -> p a x"),
                                 KK[:, a_:a_ + 4, 7 - q:15 - q, :].rearrange("p a j h -> p a (j h)"), "kk", V.t)
        cl_all, kk_all = (pend["cl", 14], pend["cl", 15]), kk_dma
        mod_until("m2a")
        slot_read = drop_slot()
        distm = L1[:, 0:512].rearrange("p (t s) -> p t s", t=2)
        negm = L1[:, 512:1024].rearrange("p (t s) -> p t s", t=2)
        tri = L1[:, 1024:1536].rearrange("p (t s) -> p t s", t=2)
        tables_read = V.t

        for t2 in range(2):
            G.do(lambda e, t2=t2: e.iota(distm[:, t2, :], pattern=[[-1, 256]], base=128 * t2, channel_multiplier=1,
                                         allow_small_or_imprecise_dtypes=True), tables_read)
            G.do(lambda e, t2=t2: e.affine_select(out=distm[:, t2, :], in_=distm[:, t2, :], compare_op=ALU.is_ge,
                                                  fill=1e33, base=128 * t2, pattern=[[-1, 256]],
                                                  channel_multiplier=1), G.t)
            G.do(lambda e, t2=t2: e.memset(negm[:, t2, :], 0.0))
            G.do(lambda e, t2=t2: e.affine_select(out=negm[:, t2, :], in_=negm[:, t2, :], compare_op=ALU.is_ge,
                                                  fill=-1e30, base=128 * t2, pattern=[[-1, 256]],
                                                  channel_multiplier=1), G.t)
            G.do(lambda e, t2=t2: e.memset(tri[:, t2, :], 1.0))
            G.do(lambda e, t2=t2: e.affine_select(out=tri[:, t2, :], in_=tri[:, t2, :], compare_op=ALU.is_ge,
                                                  fill=0.0, base=-128 * t2, pattern=[[1, 256]],
                                                  channel_multiplier=-1), G.t)
        mask_tok = G.t

        lam_t = sm[:, 0:512]
        for i_, n in enumerate(("a_lam_q1", "a_lam_k1", "a_lam_q2", "a_lam_k2")):
            lam_tok = dma(G, sm[:, 128 * i_:128 * i_ + 128], A[n].to_broadcast([128, 128]), "lam", tables_read)
        tt(V, sm[:, 0:128], sm[:, 0:128], sm[:, 128:256], MUL, lam_tok)
        tt(V, sm[:, 256:384], sm[:, 256:384], sm[:, 384:512], MUL, lam_tok)
        ls = st[:, 100:104]
        V.do(lambda e: e.reduce_sum(ls[:, 0:1], sm[:, 0:128], AX), V.t)
        V.do(lambda e: e.reduce_sum(ls[:, 1:2], sm[:, 256:384], AX), V.t)
        t = act(ls[:, 2:4], ls[:, 0:2], ACT.Exp, V.t)
        nlam = st[:, 104:105]
        tt(V, nlam, ls[:, 3:4], ls[:, 2:3], SUB, t)
        ts(V, nlam, nlam, -LAM_INIT, None, ADD, None, V.t)
        lam_ready = V.t


        abc, bbc = reg(R5, 2048), reg(R5 + 2048, 2048)
        hc, hc2 = reg(R5 + 4096, 4096), reg(R3, 4096)
        U = reg(R1, 4096).rearrange("p (g c) -> p g c", c=32)
        project(18)
        acol = st[:, 64:80]
        stt(acol, M("m2x", 16), 1.0, C("npre"), ADD, MUL, mod_tok["m2a"])
        acol2 = st[:, 80:96]
        stt(acol2, M("m2", 16), 1.0, C("npre"), ADD, MUL)
        ctok = V.t
        a1 = bcast(abc, acol, ctok)
        a2 = bcast(bbc, M("m2x", 0), ctok)
        rt = rms_stat(ctxv, hc[:, 0:2048], 0, 1e-6, ctx_tok, slot_read)
        project(19)
        mod(1, dve=True)
        u_steps = iter(range(20, 22))
        u_tok = make_u(ctxv, ctxv, 0, abc, bbc, hc, hc2, U, lambda i: project(next(u_steps)) if i % 2 else mod(1, dve=True),
                       ctx_tok, a1, a2, rt, cl_all, kk_all, P.t, slot_read)

        Vc = reg(R5, 8192).rearrange("p (k r d) -> p k r d", k=32, r=2)
        vmat = MSB[:, :].rearrange("p (d r m) -> p d r m", d=8, r=2)
        blr, bli = reg(R3, 1024), reg(R3 + 1024, 1024)
        bt1, bt2 = reg(R3 + 2048, 1024), reg(R3 + 3072, 1024)
        old_stage = tuple(stage["free"])
        stage.update(bufs=[reg(R4 + 512 * i, 512) for i in range(4)], n=0, free=[None] * 4,
                     after=(old_stage, V.t, u_tok, (sems["at0"], dma_count["at0"]), (sems["at1"], dma_count["at1"])))
        GXB = reg(R4 + 2048, 512)
        S.wait(stage["after"])
        pend["bl_free"] = (P.t, V.t, S.t, G.t)
        pend["ms"] = old_stage

        def bl_make(ch):
            return cmul(Bb[:, 0], Bb[:, 1], L2v, 8, 8 * ch, blr, bli, bt1, bt2, False,
                        (pend["bl_free"],), (pend["bl_free"],))[1]

        def bl_turn(ch, i_tok):
            d0 = 8 * ch
            for r_, src in enumerate((blr, bli)):
                for half in range(2):
                    i, b, fr = bank(GC)
                    for j in range(4):
                        dd = 4 * half + j
                        t = tr(b[:, 128 * j:128 * j + 128], src[:, 128 * dd:128 * dd + 128],
                               i_tok, fr, inc=(j == 3))
                    bank_free[i] = copy(S, vmat[:, 4 * half:4 * half + 4, r_, :],
                                        b[:, :].rearrange("p (d m) -> p d m", d=4), t, pend["ms"], pend.get("v_pe"))
            pend["bl_free"] = P.t
            pend["ms_ready"] = S.t
            pend["ms"] = dma(G, m_state_d[:, d0 * 256:d0 * 256 + 2048], MSB[:, :], "ms", S.t)

        def bl_v(ch):
            pend["v_pe"], pend["v_tok"] = v_matmuls(vmat, U, 8 * ch, Vc[:, :, :, 8 * ch:8 * ch + 8],
                                                    pend["ms_ready"], u_tok)

        npnl = 22
        it = bl_make(0)
        for ch in range(16):
            if ch < 10:
                project(npnl)
                npnl += 1
            if ch:
                bl_v(ch - 1)
            bl_turn(ch, it)
            if ch < 15:
                it = bl_make(ch + 1)
            if ch < 10:
                mod(1, dve=True)
        b_read = (V.t, G.t)
        k_tok = dma(SP, reg(12288, 4096), proj_d[1], "p1", b_read, tuple(stage["free"]), proj_tok[1])
        v_tok = dma(SP, reg(4096, 4096), proj_d[2], "p2", b_read, proj_tok[2])
        q_tok = dma(SP, reg(8192, 4096), proj_d[0], "p0", b_read, P.t, proj_tok[0])
        bl_v(15)
        ms_all = pend["ms"]
        v_ctx = (pend["v_tok"], V.t)

        stA, stB = SF[:, 0:256], SF[:, 256:512]
        t_1, t_2 = sm[:, 512:768], sm[:, 768:1024]
        l_swap = lambda x: x.rearrange("p (r d) -> p r d", r=2)

        def chunk_step(cur, nxt, vk, *w, q=V):
            tt(q, t_1, cur, LR8[:, :], MUL, q.t, *w)
            tt(q, l_swap(t_2), l_swap(cur)[:, ::-1, :], l_swap(LS8[:, :]), MUL)
            tt(q, t_1, t_1, vk, ADD, q.t)
            return tt(q, nxt, t_1, t_2, ADD, q.t)

        scan = {"cur": stA, "nxt": stB, "k": 0}

        def scan_ctx(n):
            for k in range(scan["k"], min(scan["k"] + n, 32)):
                chunk_step(scan["cur"], scan["nxt"], Vc[:, k].rearrange("p r d -> p (r d)"), v_ctx)
                scan["cur"], scan["nxt"], scan["k"] = scan["nxt"], scan["cur"], k + 1

        V.do(lambda e: e.memset(stA, 0.0))

        xv = reg(0, 4096).rearrange("p (t n) -> p t n", t=2)
        exb = MSB[:, 0:256]
        vN = reg(4096, 4096).rearrange("p (t n) -> p t n", t=2)
        qT = reg(8192, 4096).rearrange("p (k n) -> p k n", k=16)
        kT = reg(12288, 4096).rearrange("p (k n) -> p k n", k=16)
        gN = reg(0, 4096).rearrange("p (t n) -> p t n", t=2)
        oN = reg(24576, 4096).rearrange("p (t n) -> p t n", t=2)
        bcA, bcB = reg(12288, 2048), reg(14336, 2048)
        phase0 = (V.t, P.t, S.t, cl_all, ms_all)
        g_tok = dma(SP, reg(0, 4096), proj_d[3], "p3", P.t, proj_tok[3])
        V.wait(phase0)
        S.wait(phase0)

        def plus1(dst, a, *w):
            return ts(V, dst, a, 1.0, None, ADD, None, *w)

        def dense_T(hin, W, n0, npan, dst_fn, *w, side=None):
            for pnl in range(npan):
                i, wt, tok = take(lambda: load_w(W, 0, n0 + 256 * pnl))
                bi, b, fr = bank(GA)
                P.wait(fr, *w)
                for j in range(2):
                    for k in range(KT):
                        t = mm(b[:, 256 * j:256 * j + 256], wt[:, k, 128 * j:128 * j + 128], hin[:, k, :],
                               k == 0, k == KT - 1, tok, inc=(j == 1 and k == KT - 1))
                release(i, t)
                bank_free[bi] = dst_fn(pnl, b[:, :].rearrange("p (j n) -> p j n", j=2), t)
                if side:
                    side()

        def dense_N(hin, W, n0, npan, dst_fn, *w, kslots=1, side=None):
            for pnl in range(npan):
                bb = [bank(GB), bank(GC)] if kslots > 1 else [bank(GB), bank(GB)]
                for ks in range(kslots):
                    i, wt, tok = take(lambda: load_w(W, 2048 * ks, n0 + 256 * pnl))
                    for t2 in range(2):
                        bi, b, fr = bb[t2]
                        for k in range(KT):
                            t = mm(b[:, 0:256], hin[:, ks * KT + k, 128 * t2:128 * t2 + 128], wt[:, k, :],
                                   ks == 0 and k == 0, ks == kslots - 1 and k == KT - 1, tok, fr, *w,
                                   inc=(k == KT - 1))
                        if ks == kslots - 1:
                            bank_free[bi] = dst_fn(pnl, t2, b[:, 0:256], t)
                    release(i, t)
                if side:
                    side()

        def silu_panel(dst, ps, tk, ex, extra=None):
            t = act(ex, ps, ACT.Sigmoid, tk, V.t)
            if extra is not None:
                tt(V, ex, ex, extra, MUL, t)
                t = V.t
            return tt(V, dst, ps, ex, MUL, t)

        def put_q(pnl, b, t):
            return S.do(lambda e: e.mul(qT[:, 2 * pnl:2 * pnl + 2, :], b, QK_SCALE), t)

        def put_k(pnl, b, t):
            return copy(V, kT[:, 2 * pnl:2 * pnl + 2, :], b, t)

        def put_v(pnl, t2, b, t):
            return copy(S, vN[:, t2, 256 * pnl:256 * pnl + 256], b, t)

        exb = MSB[:, 0:256]

        h_dead = P.t

        NBUF = 3
        wk = L2[:, 0:1536].rearrange("p (i x) -> p i x", i=NBUF)
        aT_ = MSB[:, 256:1792].rearrange("p (i x) -> p i x", i=6)
        stat = st[:, 128:176]
        ssq = st[:, 176:192]
        info = {}

        def items_a(i):
            return i // 2, i % 2

        def a_scores(i):
            h, t2 = items_a(i)
            w_ = 128 * (t2 + 1)
            bi, b, fr = bank(GA)
            for c in range(2):
                t = mm(b[:, 256 * c:256 * c + w_], qT[:, 2 * h + c, 128 * t2:128 * t2 + 128],
                       kT[:, 2 * h + c, 0:w_], True, True, fr, q_tok, k_tok, inc=(c == 1))
            info[i] = {"b": bi, "s": t}

        def a_soft(i):
            h, t2 = items_a(i)
            w_ = 128 * (t2 + 1)
            slope = 2.0 ** (-8.0 * (h + 1) / 8)
            n = info[i]
            b = banks[n["b"]]
            p = wk[:, i % NBUF, :].rearrange("p (c s) -> p c s", c=2)[:, :, 0:w_]
            sb_ = stat[:, 6 * (i % NBUF):6 * (i % NBUF) + 6]
            prev = info.get(i - NBUF, {})
            bv = b[:, :].rearrange("p (c s) -> p c s", c=2)[:, :, 0:w_]
            t = stt(p, distm[:, t2, 0:w_].unsqueeze(1).to_broadcast([128, 2, w_]), -slope, bv, MUL, ADD,
                    n["s"], mask_tok, prev.get("tr"), V.t)
            bank_free[n["b"]] = t
            V.do(lambda e: e.tensor_reduce(sb_[:, 0:2], p, AX, MAX, negate=True), V.t)
            mx = V.t
            for c in range(2):
                t = act(p[:, c, :], p[:, c, :], ACT.Exp, mx, bias=sb_[:, c:c + 1], accum_out=sb_[:, 2 + c:3 + c])
            n["e"] = S.t

        def a_mix(i):
            h, t2 = items_a(i)
            w_ = 128 * (t2 + 1)
            n = info[i]
            p = wk[:, i % NBUF, :].rearrange("p (c s) -> p c s", c=2)[:, :, 0:w_]
            sb_ = stat[:, 6 * (i % NBUF):6 * (i % NBUF) + 6]
            recip(sb_[:, 4:6], sb_[:, 2:4], n["e"])
            tt(V, sb_[:, 5:6], sb_[:, 5:6], nlam, MUL, V.t)
            ts(V, p[:, 0, :], p[:, 0, :], sb_[:, 4:5], None, MUL, None, V.t)
            n["a"] = stt(p[:, 0, :], p[:, 1, :], sb_[:, 5:6], p[:, 0, :], MUL, ADD, V.t)

        def a_turn(i):
            h, t2 = items_a(i)
            n = info[i]
            p = wk[:, i % NBUF, 0:256]
            bi, b, fr = bank(GB)
            for s in range(t2 + 1):
                t = tr(b[:, 128 * s:128 * s + 128], p[:, 128 * s:128 * s + 128], n["a"], fr, inc=(s == t2))
            n["tr"] = t
            w_ = 128 * (t2 + 1)
            bank_free[bi] = copy(V, aT_[:, i % NBUF * 2:i % NBUF * 2 + 2, :].rearrange("p a b -> p (a b)")[:, 0:w_],
                                 b[:, 0:w_], t, info.get(i - NBUF, {}).get("pv"))
            n["aT"] = bank_free[bi]

        def a_out(i):
            h, t2 = items_a(i)
            n = info[i]
            bi, b, fr = bank(GC)
            av = aT_[:, i % NBUF * 2:i % NBUF * 2 + 2, :].rearrange("p a b -> p (a b)")
            for s in range(t2 + 1):
                t = mm(b[:, 0:256], av[:, 128 * s:128 * s + 128], vN[:, s, 256 * h:256 * h + 256],
                       s == 0, s == t2, n["aT"], fr, v_tok, inc=(s == t2))
            n["pv"] = t
            o = oN[:, t2, 256 * h:256 * h + 256]
            c1 = copy(S, o, b[:, 0:256], t, h_dead)
            act(MSB[:, 1792:2048], b[:, 0:256], ACT.Square, S.t, accum_out=ssq[:, 2 * h + t2:2 * h + t2 + 1])
            bank_free[bi] = S.t

        pipeline(16, [lambda i: (a_scores(i), mod(1, dve=True) if i % 4 == 3 else None), a_soft, a_mix, a_turn, a_out])
        ts(V, ssq, ssq, 1.0 / 256, 1e-5, MUL, ADD, S.t)
        rs = st[:, 192:208]
        rsqrt(rs, ssq, st[:, 208:224], V.t)
        for h in range(8):
            for t2 in range(2):
                o = oN[:, t2, 256 * h:256 * h + 256]
                stt(o, o, rs[:, 2 * h + t2:2 * h + t2 + 1], gN[:, t2, 256 * h:256 * h + 256], MUL, MUL, V.t, g_tok)

        x_tok = dma(G, xv, A["x"][0].rearrange("(t p) n -> p t n", p=128), "x1", V.t)

        def to_T(src, dst, *w):
            for k2 in range(8):
                i, b, fr = bank(GA)
                for j in range(2):
                    for t2 in range(2):
                        k = 2 * k2 + j
                        t = tr(b[:, 256 * j + 128 * t2:256 * j + 128 * t2 + 128], src[:, t2, 128 * k:128 * k + 128],
                               fr, *w, inc=(j == 1 and t2 == 1))
                q_ = V if k2 % 2 else S
                bank_free[i] = copy(q_, dst[:, 2 * k2:2 * k2 + 2, :], b[:, :].rearrange("p (j n) -> p j n", j=2),
                                    t, *w)
            return V.t, S.t

        oT = qT
        toks = to_T(oN, oT, V.t, P.t)

        dmod = lambda: mod(1, dve=True)

        bs = MSB[:, 512:560].rearrange("p (t c s) -> p t c s", t=2, c=4)

        def residual(toks, W, gdone, side=None):
            def put(pnl, t2, b, t):
                cs = slice(256 * pnl, 256 * pnl + 256)
                tmp_ = MSB[:, 256 * t2:256 * t2 + 256]
                r = tt(V, tmp_, b, bcA[:, cs], MUL, t, gdone, V.t)
                stt(xv[:, t2, cs], xv[:, t2, cs], ALPHA, tmp_, MUL, ADD, V.t)
                if pnl % 2:
                    c = pnl // 2
                    V.do(lambda e: e.bn_stats(bs[:, t2, c, :], xv[:, t2, 512 * c:512 * c + 512]), V.t)
                return r
            dense_N(oT, W, 0, 8, put, *toks, side=side)
            return V.t

        def layer_norm(l, *w):
            lg = dma(G, bcA, A["ln_g"][l:l + 1, :].to_broadcast([128, 2048]), "bc0", *w)
            lb = dma(G, bcB, A["ln_b"][l:l + 1, :].to_broadcast([128, 2048]), "bc1", *w)
            mv = st[:, 0:4].rearrange("p (t s) -> p t s", t=2)
            for t2 in range(2):
                V.do(lambda e, t2=t2: e.bn_aggr(mv[:, t2, :], bs[:, t2, :, :].rearrange("p c s -> p (c s)")), V.t)
            ts(V, st[:, 4:6], mv[:, :, 1], 1e-5, None, ADD, None, V.t)
            rsqrt(st[:, 6:8], st[:, 4:6], st[:, 8:10], V.t)
            for t2 in range(2):
                for hf in range(2):
                    cs = slice(1024 * hf, 1024 * hf + 1024)
                    stt(xv[:, t2, cs], xv[:, t2, cs], mv[:, t2, 0:1], bcA[:, cs], SUB, MUL, V.t, lg)
                for hf in range(2):
                    cs = slice(1024 * hf, 1024 * hf + 1024)
                    stt(xv[:, t2, cs], xv[:, t2, cs], st[:, 6 + t2:7 + t2], bcB[:, cs], MUL, ADD, V.t, lb)
            return V.t

        mod_until("m0g", dve=True)
        gb = bcast(bcA, M("m0", 32), mod_tok["m0g"], P.t)
        residual((toks, x_tok), A["a_w_out"][0], gb, side=lambda: (dmod(), scan_ctx(4)))
        xt = layer_norm(0, V.t)

        gN = reg(20480, 4096).rearrange("p (t n) -> p t n", t=2)
        add_slot(reg(16384, 4096), V.t)
        h1 = hT
        mod_until("m1s", dve=True)
        sc2 = st[:, 110:126]
        plus1(sc2, M("m1", 16), xt, P.t, S.t)
        toks = x_transposed(xv, h1, sc2, M("m1", 0), V.t, P.t)
        dense_T(h1, A["b_w_in"][0], 0, 8, put_q, *toks, side=dmod)
        q_tok = S.t

        def put_g2(pnl, t2, b, t):
            return silu_panel(gN[:, t2, 256 * pnl:256 * pnl + 256], b, t, exb)

        dense_N(h1, A["b_w_in"][0], 2048, 8, put_g2, *toks, side=dmod)
        g_tok = V.t
        mod_until("kv", dve=True)
        plus1(sc2, M("kv", 16), V.t, P.t, S.t)
        toks = x_transposed(xv, h1, sc2, M("kv", 0), V.t, P.t)
        dense_T(h1, A["kv_w"], 0, 8, put_k, *toks, side=dmod)
        k_tok = V.t
        dense_N(h1, A["kv_w"], 2048, 8, put_v, *toks, side=dmod)
        v_tok = S.t
        zw = sm[:, 768:1024].rearrange("p (k n) -> p k n", k=16)
        bf = sm[:, 1024:1040]
        zf_tok = dma(G, zw, A["kv_w"][:, 4096:4112].rearrange("(k p) n -> p k n", p=128), "zf", G.t)
        zf_tok = dma(G, bf, A["kv_b_f"].rearrange("(a n) -> a n", a=1).to_broadcast([128, 16]), "zf")
        lf = sm[:, 1056:1088].rearrange("p (t h) -> p t h", t=2)
        tz = sm[:, 1088:1120].rearrange("p (t h) -> p t h", t=2)
        bi, b, fr = bank(GA)
        for t2 in range(2):
            for k in range(KT):
                t = mm(b[:, 16 * t2:16 * t2 + 16], h1[:, k, 128 * t2:128 * t2 + 128], zw[:, k, :], k == 0, k == KT - 1,
                       fr, zf_tok, *toks, inc=(t2 == 1 and k == KT - 1))
        bz = b[:, 0:32].rearrange("p (t h) -> p t h", t=2)
        zz = sm[:, 1120:1152].rearrange("p (t h) -> p t h", t=2)
        bank_free[bi] = tt(V, zz, bz, bf.unsqueeze(1).to_broadcast([128, 2, 16]), ADD, t, zf_tok)
        ts(V, tz, zz, -1.0, None, MUL, None, V.t)
        tt(V, tz, tz, zz, MIN, V.t)
        t = act(tz, tz, ACT.Exp, V.t)
        t = act(tz, tz, ACT.Ln, t, bias=1.0)
        ts(V, lf, zz, 0.0, None, MIN, None, V.t)
        tt(V, lf, lf, tz, SUB, V.t, t)
        nFT = sm[:, 1408:1664]
        bi, b, fr = bank(GA)
        for s in range(2):
            t = mm(b[0:16, 0:256], lf[:, s, :], tri[:, s, :], s == 0, s == 1, V.t, fr, mask_tok, inc=(s == 1))
        bank_free[bi] = ts(V, nFT[0:16, :], b[0:16, 0:256], -1.0, None, MUL, None, t)
        FN = sm[:, 1664:1696].rearrange("p (t h) -> p t h", t=2)
        bi, b, fr = bank(GA)
        for t2 in range(2):
            for s_ in range(t2 + 1):
                t = mm(b[:, 16 * t2:16 * t2 + 16], tri[:, s_, 128 * t2:128 * t2 + 128], lf[:, s_, :], s_ == 0, s_ == t2,
                       fr, inc=(s_ == t2))
        bank_free[bi] = copy(V, FN, b[:, 0:32].rearrange("p (t h) -> p t h", t=2), t)
        f_tok = V.t
        h_dead = P.t
        info.clear()
        wk2 = L2[:, 0:1024].rearrange("p (i x) -> p i x", i=4)
        stat2 = st[:, 128:144]

        def f_scores(i):
            h, t2 = i // 2, i % 2
            w_ = 128 * (t2 + 1)
            bi, b, fr = bank(GA)
            sel = ident[0:16, h:h + 1]
            mm(b[:, 0:w_], qT[:, h, 128 * t2:128 * t2 + 128], kT[:, h, 0:w_], True, False, fr, q_tok, k_tok, f_tok)
            t = mm(b[:, 0:w_], sel.to_broadcast([16, 128]), nFT[0:16, 0:w_], False, True, inc=True)
            info[i] = {"b": bi, "s": t}

        def f_soft(i):
            h, t2 = i // 2, i % 2
            w_ = 128 * (t2 + 1)
            n = info[i]
            p = wk2[:, i % 4, 0:w_]
            s_ = stat2[:, 4 * (i % 4):4 * (i % 4) + 4]
            bank_free[n["b"]] = stt(p, banks[n["b"]][:, 0:w_], FN[:, t2, h:h + 1], negm[:, t2, 0:w_], ADD, ADD,
                                    n["s"], mask_tok, info.get(i - 4, {}).get("tr"), V.t)
            V.do(lambda e: e.tensor_reduce(s_[:, 0:1], p, AX, MAX, negate=True), V.t, info.get(i - 4, {}).get("o"))
            act(p, p, ACT.Exp, V.t, bias=s_[:, 0:1], accum_out=s_[:, 1:2])
            n["e"] = S.t

        def f_turn(i):
            h, t2 = i // 2, i % 2
            w_ = 128 * (t2 + 1)
            n = info[i]
            p = wk2[:, i % 4, 0:w_]
            bi, b, fr = bank(GB)
            for s in range(t2 + 1):
                t = tr(b[:, 128 * s:128 * s + 128], p[:, 128 * s:128 * s + 128], n["e"], fr, inc=(s == t2))
            n["tr"] = t
            bank_free[bi] = copy(S, aT_[:, i % 3 * 2:i % 3 * 2 + 2, :].rearrange("p a b -> p (a b)")[:, 0:w_],
                                 b[:, 0:w_], t, info.get(i - 3, {}).get("pv"))
            n["aT"] = bank_free[bi]

        def f_out(i):
            h, t2 = i // 2, i % 2
            n = info[i]
            bi, b, fr = bank(GC)
            av = aT_[:, i % 3 * 2:i % 3 * 2 + 2, :].rearrange("p a b -> p (a b)")
            for s in range(t2 + 1):
                t = mm(b[:, 0:128], av[:, 128 * s:128 * s + 128], vN[:, s, 128 * h:128 * h + 128],
                       s == 0, s == t2, n["aT"], fr, v_tok, inc=(s == t2))
            n["pv"] = t
            s_ = stat2[:, 4 * (i % 4):4 * (i % 4) + 4]
            recip(s_[:, 2:3], s_[:, 1:2], n["e"])
            cs = slice(128 * h, 128 * h + 128)
            bank_free[bi] = stt(oN[:, t2, cs], b[:, 0:128], s_[:, 2:3], gN[:, t2, cs], MUL, MUL, V.t, t, h_dead, g_tok)
            n["o"] = V.t

        pipeline(32, [f_scores, f_soft, f_turn, f_out])
        toks = to_T(oN, oT, V.t, P.t)
        gb = bcast(bcA, M("m1", 32), mod_tok["m1g"], V.t, P.t)
        abc, bbc = reg(24576, 2048), reg(26624, 2048)
        a1 = bcast(abc, acol2, P.t)
        a2 = bcast(bbc, M("m2", 0))
        residual(toks, A["b_w_out"][0], gb, side=dmod)
        slot_read = drop_slot()
        xt = layer_norm(1, V.t)

        everything = (V.t, P.t, S.t, G.t)

        def load_cl(n):
            i = next_slot()
            t_ = i["ap"]
            dma(SP, t_[:, 0:2048], cl_d[:, n * 2048:(n + 1) * 2048], i["sem"], i["free"])
            tok = dma(SP, t_[:, 2048:4096], cl_d[:, 16384 + n * 2048:16384 + (n + 1) * 2048], i["sem"])
            return i, t_.rearrange("p (b d r x) -> p b d r x", b=2, d=8, r=2), tok

        def load_toep(n):
            i = next_slot()
            t_ = i["ap"][:, 0:2048].rearrange("p (g x) -> p g x", x=128)
            for qq in range(8):
                src = toep_d[qq].rearrange("a (b h) x -> h (a b) x", h=16)[:, 16 * n:16 * n + 16, :]
                tok = dma(SP, t_[16 * qq:16 * qq + 16, :, :], src, i["sem"], i["free"])
            return i, t_, tok

        SP.wait(ms_all, cl_all, kk_all)
        hcL, hc2L = reg(4096, 4096), reg(8192, 4096)
        hL = reg(16384, 4096).rearrange("p (t n) -> p t n", t=2)
        UL = LT[:, 0:4096].rearrange("p (g c) -> p g c", c=32)
        VL = reg(20480, 8192).rearrange("p (f k r d) -> p f k r d", f=2, k=32, r=2)
        rt = rms_stat(xv, reg(12288, 2048), 0, 1e-6, *everything)
        u_tok = make_u(xv, hL, 0, abc, bbc, hcL, hc2L, UL, lambda i: None, a1, a2, rt, *everything, slot_read)
        u_read = (V.t, P.t, u_tok)
        S.wait(u_read)
        v_half = {}

        def v_part(f):
            for d_ in range(2):
                for sl in range(2):
                    d0 = 64 * d_ + 32 * f + 16 * sl
                    i, wt, tok = take(lambda: load(m_state_d[:, d0 * 256:d0 * 256 + 4096]))
                    mv = wt.rearrange("p (d r m) -> p d r m", d=16, r=2)
                    for hf in range(2):
                        c0 = 32 * d_ + 16 * sl + 8 * hf
                        t, v_half[f] = v_matmuls(mv[:, 8 * hf:8 * hf + 8], UL, d0 + 8 * hf,
                                                 VL[:, f, :, :, c0:c0 + 8], tok, u_tok)
                        if hf:
                            release(i, t)
                        yield

        Sb = reg(4096, 16384).rearrange("p (r v d g c) -> p r v d g c", r=2, v=2, d=64, g=2)
        SbD = reg(4096, 16384).rearrange("p (r d g c) -> p r d g c", r=2, d=128, g=2)
        G.do(lambda e: e.memset(SbD[0:64, :, :, 1, :], 0.0), u_read)
        z0 = G.do(lambda e: e.memset(SbD[64:128, :, :, 0, :], 0.0))
        s_tok, scan_done = {}, {}

        def scan_part(f, side, at):
            half = lambda y: y.rearrange("p (r v d) -> p r v d", r=2, v=2)[:, :, :, 32 * f:32 * f + 32]
            cur, nxt = stA, stB
            saved = None
            hs = slice(32 * f, 32 * f + 32)
            for k in range(32):
                for g2 in range(2):
                    pp = slice(64 * g2, 64 * g2 + 64)
                    c3 = half(cur)[pp]
                    copy(S, Sb[pp, :, 0, hs, g2, k], c3[:, :, 0], V.t, u_read)
                    copy(S, Sb[pp, :, 1, hs, g2, 31 - k], c3[:, :, 1])
                if k < 31:
                    vk = VL[:, f, k].rearrange("p r (v d) -> p r v d", v=2)
                    tt(V, half(t_1), half(cur), half(LR8[:, :]), MUL, V.t, saved)
                    tt(V, half(t_2), half(cur)[:, ::-1], half(LS8[:, :]), MUL)
                    tt(V, half(t_1), half(t_1), vk, ADD, V.t, v_half[f])
                    tt(V, half(nxt), half(t_1), half(t_2), ADD, V.t)
                saved = S.t
                cur, nxt = nxt, cur
                if k % at == at - 1:
                    next(side, None)
            s_tok[f], scan_done[f] = S.t, V.t
            for _ in side:
                pass

        Y = reg(20480, 8192).rearrange("p (k q g h) -> p k q g h", k=8, q=8, g=8)

        def y_part(f):
            for q in range(4 * f, 4 * f + 4):
                i1, cl, tok1 = take(lambda: load_cl(q))
                i2, wt, tok2 = take(lambda: load_toep(q))
                for g4 in range(2):
                    bi, b, fr = bank(GA)
                    for j in range(4):
                        gg = 4 * g4 + j
                        gp = 8 * q + gg
                        o = b[0:64, 128 * j:128 * j + 128]
                        for d_ in range(2):
                            for r_ in range(2):
                                mm(o, SbD[:, r_, 64 * d_ + gp, :, :].rearrange("p g c -> p (g c)"),
                                   cl[:, d_, gg, r_, :], d_ == 0 and r_ == 0, False, tok1, fr, s_tok[f], z0)
                        for g2 in range(2):
                            t = mm(b[32 * g2:32 * g2 + 32, 128 * j:128 * j + 128], UL[:, gp + 64 * g2, :],
                                   wt[:, 2 * gg + g2, :], False, True, tok2, inc=(j == 3 and g2 == 1))
                    bank_free[bi] = copy(V if f and g4 else S,
                                         Y[0:64, q, :, 4 * g4:4 * g4 + 4, :].rearrange("p q g h -> p g q h"),
                                         b[0:64, :].rearrange("p (g q h) -> p g q h", g=4, q=8), t, scan_done[f])
                    if g4:
                        release(i1, t)
                        release(i2, t)
                    yield

        v_first = v_part(0)
        for i in range(8):
            next(v_first, None)
            if i % 2:
                mod(1, dve=True)
        for _ in v_first:
            pass
        scan_part(0, v_part(1), 3)
        scan_part(1, y_part(0), 4)
        for i, _ in enumerate(y_part(1)):
            if i in (0, 3):
                mod(1, dve=True)
        y_tok = (V.t, S.t, P.t)
        zT = reg(4096, 4096).rearrange("p (k n) -> p k n", k=16)
        for k8 in range(8):
            bi, b, fr = bank(GA)
            for q in range(8):
                t = tr(b[:, 64 * q:64 * q + 64], Y[0:64, k8, q, :, :].rearrange("p g h -> p (g h)"), fr, y_tok, inc=(q == 7), k=64)
            bv = b[:, :].rearrange("p (q g c) -> p q g c", q=8, g=2)
            ends = []
            for g2 in range(2):
                ends.append(copy(S if k8 % 2 else V, zT[:, 8 * g2 + k8, :].rearrange("p (c q) -> p q c", q=8), bv[:, :, g2, :],
                                 t, y_tok))
            bank_free[bi] = tuple(ends)
        z_tok = (V.t, S.t, P.t)
        dead = (P.t, V.t, S.t, G.t)
        first.close()
        sbr = lambda name, n: ctx.enter_context(nc.sbuf_tensor(name, [128, n], F32R))
        sb("x_stays", 4096)
        Y = sb("y_mlp", 4096)
        N1 = sb("n1", 4096)
        HH, HL, DH, DL = (sbr(n_, 4096) for n_ in ("in_hi", "in_lo", "hid_hi", "hid_lo"))
        WHI, WLO = sbr("w_hi", 4096), sbr("w_lo", 4096)
        by_k = lambda a: a[:, :].rearrange("p (k n) -> p k n", k=16)
        HHk, HLk, DHk, DLk, WHk, WLk, raw = (by_k(a) for a in (HH, HL, DH, DL, WHI, WLO, N1))
        tmpN = yN = Y[:, :].rearrange("p (t n) -> p t n", t=2)
        aN = N1[:, :].rearrange("p (t n) -> p t n", t=2)
        SQ = sm[:, 0:1024]
        exs = [sm[:, 1024 + 256 * j_:1280 + 256 * j_] for j_ in range(2)]

        def split(hi, lo, src, *w):
            h = copy(S, hi, src, *w)
            return h, tt(V, lo, src, hi, SUB, h, *w)

        q_free = [dead] * 4
        q_tok = [None] * 4
        pair_free = [(bank_free[2 * i], bank_free[2 * i + 1]) for i in range(3)]
        hid_tok = [None] * 8
        h_tok = [None] * 4
        y_tok = [None] * 8
        sq_free = [None, None]
        ex_free = [None, None]
        now = {}

        def split_q(src, q, *w):
            ks = slice(4 * q, 4 * q + 4)
            h_tok[q] = split(HHk[:, ks, :], HLk[:, ks, :], src[:, ks, :], *w)

        def split_in(src, *w):
            for q in range(4):
                split_q(src, q, *w)

        def split_w(steps, n, q):
            if n >= len(steps):
                return
            kind, g, p = steps[n]
            if q == 0:
                if kind == "in":
                    now["w"] = take(lambda: load_w(A["w_mlp_in_2"][0], 0, 2048 * g + 256 * p))
                elif kind == "out":
                    now["w"] = take(lambda: load_w(A["w_mlp_out_2"][0], 2048 * g, 256 * p))
                else:
                    now["w"] = take(lambda: load_w(A["s5_w_glu_2"][0], 0, 2048 * g + 256 * p))
            i, wt, tok = now["w"]
            ks = slice(4 * q, 4 * q + 4)
            q_tok[q] = split(WHk[:, ks, :], WLk[:, ks, :], wt[:, ks, :], tok, q_free[q])
            if q == 3:
                release(i, (V.t, S.t))

        def multiply(steps, n, q):
            kind, g, p = steps[n]
            pr = n % 3
            a_hi, a_lo = (DHk, DLk) if kind == "out" else (HHk, HLk)
            w_ = (hid_tok[2 * q], hid_tok[2 * q + 1]) if kind == "out" else (h_tok[q],)
            P.wait(pair_free[pr], q_tok[q], *w_)
            for j in range(2):
                o = banks[2 * pr + j][:, 0:256]
                for k in range(4 * q, 4 * q + 4):
                    for m, (wx, ax) in enumerate(((WHk, a_hi), (WHk, a_lo), (WLk, a_hi))):
                        blk = slice(128 * j, 128 * j + 128)
                        l_, r_ = (wx[:, k, blk], ax[:, k, :]) if kind == "in" else (ax[:, k, blk], wx[:, k, :])
                        t = mm(o, l_, r_, k == 0 and m == 0, k == KT - 1 and m == 2,
                               inc=(j == 1 and k == 4 * q + 3 and m == 2))
            q_free[q] = t
            return t

        def finish(steps, n, t):
            kind, g, p = steps[n]
            pr = n % 3
            squares()
            for j in range(2):
                b = banks[2 * pr + j][:, 0:256]
                cs = slice(256 * p, 256 * p + 256)
                if kind == "in":
                    act(SQ[:, 512 * (p % 2) + 256 * j:512 * (p % 2) + 256 * j + 256], b, ACT.Relu, t, dead,
                        sq_free[p % 2])
                elif kind == "glu" and g == 0:
                    y_tok[p] = copy(S, aN[:, j, cs], b, t, dead)
                elif kind == "glu":
                    e_ = act(exs[j], b, ACT.Sigmoid, t, dead, ex_free[j])
                    ex_free[j] = tt(V, aN[:, j, cs], aN[:, j, cs], exs[j], MUL, e_, y_tok[p])
                    sq_todo.append((j, p, ex_free[j]))
                elif g == 0:
                    y_tok[p] = copy(V, yN[:, j, cs], b, t, h_tok)
                else:
                    y_tok[p] = tt(V, yN[:, j, cs], b, yN[:, j, cs], ADD, t, y_tok[p])
            pair_free[pr] = V.t if kind == "out" else S.t
            if kind == "in":
                sq = SQ[:, 512 * (p % 2):512 * (p % 2) + 512]
                t = tt(V, sq, sq, sq, MUL, S.t)
                sq3 = sq.rearrange("p (k n) -> p k n", k=2)
                hid_tok[p] = split(DHk[:, 2 * p:2 * p + 2, :], DLk[:, 2 * p:2 * p + 2, :], sq3, t)
                sq_free[p % 2] = V.t

        sq_todo = []
        ssq = st[:, 128:144]

        def squares():
            while sq_todo:
                j, p, t = sq_todo.pop(0)
                act(SQ[:, 0:256], aN[:, j, 256 * p:256 * p + 256], ACT.Square, t, S.t,
                    accum_out=ssq[:, 8 * j + p:8 * j + p + 1])

        def run_steps(steps, side):
            last = None
            for n in range(len(steps)):
                for q in range(4):
                    t = multiply(steps, n, q)
                    if q == 0 and n:
                        finish(steps, n - 1, last)
                    split_w(steps, n + 1, q)
                last = t
                side(n)
            finish(steps, len(steps) - 1, last)

        glu = [("glu", g, p) for g in range(2) for p in range(8)]
        for q in range(4):
            split_w(glu, 0, q)

        def gelu_a(q):
            z, e_ = reg(4096 + 1024 * q, 1024), reg(8192 + 1024 * q, 1024)
            t = act(e_, z, ACT.Square, dead)
            ts(V, e_, e_, 0.044715, 1.0, MUL, ADD, t)
            gelu_t[q] = tt(V, e_, e_, z, MUL, V.t)

        def gelu_b(q):
            z, e_ = reg(4096 + 1024 * q, 1024), reg(8192 + 1024 * q, 1024)
            t = act(e_, e_, ACT.Sigmoid, gelu_t[q], scale=2.0 * GELU_C)
            split_q(zT, q, tt(V, z, z, e_, MUL, t))

        gelu_t = {}
        pipeline(4, [gelu_a, lambda q: None, gelu_b])
        dead = (dead, V.t, S.t)

        pcol = st[:, 64:80]
        bcA, junk = reg(20480, 2048), reg(22528, 2048)
        gate = {}

        def glu_side(n):
            if "m2b" not in mod_tok:
                if n % 4 == 1:
                    mod(1, dve=True)
            elif "t" not in gate:
                tt(V, pcol, M("m2", 32), C("npost"), MUL, V.t, dead)
                gate["t"] = bcast(bcA, pcol, V.t, dead, group=(6,))

        run_steps(glu, glu_side)
        while "t" not in gate:
            glu_side(1)
        gb = gate["t"]

        def rms_tile(v, t2, junk_, *w):
            m_ = st[:, 2 + t2:3 + t2]
            a = act(junk_, v[:, t2, :], ACT.Square, S.t, *w, accum_out=m_)
            ts(V, m_, m_, 1.0 / D, 1e-6, MUL, ADD, a)
            return rsqrt(st[:, t2:t2 + 1], m_, st[:, 4 + t2:5 + t2], V.t)

        def add_gated(v, tmp_, t2):
            for hf in range(2):
                cs = slice(1024 * hf, 1024 * hf + 1024)
                stt(tmp_[:, t2, cs], v[:, t2, cs], st[:, t2:t2 + 1], bcA[:, cs], MUL, MUL, V.t, gb)
            for hf in range(2):
                cs = slice(1024 * hf, 1024 * hf + 1024)
                tt(V, xv[:, t2, cs], xv[:, t2, cs], tmp_[:, t2, cs], ADD, V.t)
            return V.t

        squares()
        V.do(lambda e: e.reduce_sum(st[:, 2:4], ssq.rearrange("p (t n) -> p t n", t=2), AX), S.t)
        ts(V, st[:, 2:4], st[:, 2:4], 1.0 / D, 1e-6, MUL, ADD, V.t)
        rsqrt(st[:, 0:2], st[:, 2:4], st[:, 4:6], V.t)
        x0_tok = add_gated(aN, tmpN, 0)
        sq0 = act(junk, xv[:, 0, :], ACT.Square, S.t, x0_tok, accum_out=st[:, 2:3])
        x1_tok = add_gated(aN, tmpN, 1)
        sq1 = act(junk, xv[:, 1, :], ACT.Square, S.t, x1_tok, accum_out=st[:, 3:4])
        ts(V, st[:, 2:3], st[:, 2:3], 1.0 / D, 1e-6, MUL, ADD, sq0)
        rsqrt(st[:, 0:1], st[:, 2:3], st[:, 4:5], V.t)
        ts(V, tmpN[:, 0, :], xv[:, 0, :], st[:, 0:1], None, MUL, None, V.t)
        ts(V, st[:, 3:4], st[:, 3:4], 1.0 / D, 1e-6, MUL, ADD, sq1)
        rsqrt(st[:, 1:2], st[:, 3:4], st[:, 5:6], V.t)
        ts(V, tmpN[:, 1, :], xv[:, 1, :], st[:, 1:2], None, MUL, None, V.t)
        stt(pcol, M("m2", 64), 1.0, C("mpre"), ADD, MUL, P.t, V.t)
        mlp = [(kind, g, p) for g in range(4) for kind in ("in", "out") for p in range(8)]
        for q in range(4):
            bank_free[q] = (bank_free[q], tuple(pair_free))
            split_w(mlp, 0, q)
        x_transposed(tmpN, raw, pcol, M("m2", 48), V.t,
                     each=lambda k2, *t_: split_q(raw, k2 // 2, *t_, P.t) if k2 % 2 else None)
        pair_free[0] = (pair_free[0], bank_free[0], bank_free[1])
        pair_free[1] = (pair_free[1], bank_free[2], bank_free[3])
        raw_read = (V.t, S.t)
        bcA, junk = N1[:, 0:2048], N1[:, 2048:4096]
        gate.clear()

        def mlp_side(n):
            if "m2c" not in mod_tok:
                if n % 6 == 1:
                    mod(1, dve=True)
            elif "t" not in gate:
                pcol2 = st[:, 80:96]
                tt(V, pcol2, M("m2", 80), C("mpost"), MUL)
                gate["t"] = bcast(bcA, pcol2, V.t, raw_read, group=(6,))

        run_steps(mlp, mlp_side)
        gb = gate["t"]
        y_all = V.t
        out_v = out[0].rearrange("(t p) n -> p t n", p=128)
        rms_tile(yN, 0, junk, y_all)
        rms_tile(yN, 1, junk, y_all)
        for t2 in range(2):
            o_tok = dma(SP, out_v[:, t2, :], xv[:, t2, :], "out", add_gated(yN, yN, t2))
        SP.wait(o_tok, V.t, S.t, P.t, G.t)

        assert not jobs and not mod.pending
        block = ctx.enter_context(nc.Block())

        @block.sync
        def _(e):
            SP.run(e)

        @block.gpsimd
        def _(e):
            G.run(e)

        @block.scalar
        def _(e):
            S.run(e)

        @block.vector
        def _(e):
            V.run(e)

        @block.tensor
        def _(e):
            P.run(e)


_INS = ["x", "c", "w_mod", "b_mod", "ln_g", "ln_b", "a_w_in", "a_w_out", "a_lam_q1", "a_lam_k1", "a_lam_q2",
        "a_lam_k2", "a_subln_g", "kv_w_mod", "kv_b_mod", "kv_w", "kv_b_f", "b_w_in", "b_w_out", "c_2", "ctx_2",
        "c_ctx_2", "w_mod_2", "b_mod_2", "norm_mix_pre_2", "norm_mix_post_2", "norm_mlp_pre_2", "norm_mlp_post_2",
        "w_mlp_in_2", "w_mlp_out_2", "s5_a_re_2", "s5_a_im_2", "s5_log_dt_2", "s5_b_re_2", "s5_b_im_2",
        "s5_c_re_2", "s5_c_im_2", "s5_d_2", "s5_w_glu_2"]


def kernel(**inputs):
    import numpy as _np
    import concourse.bacc as _bacc
    from concourse.bass_utils import run_bass_kernel_spmd as _run

    nc = _bacc.Bacc("TRN2", target_bir_lowering=False, num_devices=1)
    arrays, args = {}, {}
    for name in _INS:
        a = _np.ascontiguousarray(inputs[name])
        arrays[f"in_{name}"] = a
        args[name] = nc.dram_tensor(f"in_{name}", a.shape, mybir.dt.from_np(a.dtype), kind="ExternalInput").ap()
    out = nc.dram_tensor("out_0", (1, 256, 2048), F32, kind="ExternalOutput").ap()
    build(nc, args, out)
    r = _run(nc, [arrays], core_ids=[0])
    return r.results[0]["out_0"]
```
